# Optimizing a Trainium2 kernel written in Bass

```python
import jax, jax.numpy as jnp
from jax import lax
import numpy as np

D_MODEL = 1024
BATCH = 1
SEQ = 512
DEPTH = 1
DEC_BATCH = 8
DEC_SEQ = 8
PAST_LEN = 4096
PAGE_SIZE = 128

RET_H = 4
RET_DK = 64
RET_DV = 128
DN_H = 4
DN_DK = 128
DN_DV = 128
CONV_W = 4
CHUNK = 64
ROPE_BASE = 10000.0
N_GROUPS = 4
EXPERTS_PER_GROUP = 4
N_EXPERTS = N_GROUPS * EXPERTS_PER_GROUP
TOP_K = 2
D_EXPERT = 256
PLE_DIM = 256
EPS = 1e-6

RET_QK = RET_H * RET_DK
RET_VW = RET_H * RET_DV
DN_QK = DN_H * DN_DK
DN_VW = DN_H * DN_DV
DN_CONV_CH = 2 * DN_QK + DN_VW
IN_WIDTHS = (RET_QK, RET_QK, RET_VW, RET_VW, DN_CONV_CH, DN_VW, DN_H, DN_H, D_MODEL, D_MODEL)
IN_COLS = sum(IN_WIDTHS)

kernel_name = "hybrid_retention_gdn_hmoe_step"

def _split_points():
    pts, acc = [], 0
    for w in IN_WIDTHS[:-1]:
        acc += w
        pts.append(acc)
    return pts

def rmsnorm(x, g):
    xf = x.astype(jnp.float32)
    y = xf * lax.rsqrt(jnp.mean(xf * xf, axis=-1, keepdims=True) + EPS)
    return (y * g.astype(jnp.float32)).astype(x.dtype)

def rms_plain(xf):
    return xf * lax.rsqrt(jnp.mean(xf * xf, axis=-1, keepdims=True) + EPS)

def l2norm(xf):
    return xf * lax.rsqrt(jnp.sum(xf * xf, axis=-1, keepdims=True) + EPS)

def rotary(x, pos):
    half = x.shape[-1] // 2
    inv = 1.0 / (ROPE_BASE ** (jnp.arange(half, dtype=jnp.float32) / half))
    ang = pos.astype(jnp.float32)[:, None] * inv[None, :]
    cos, sin = jnp.cos(ang), jnp.sin(ang)
    x1, x2 = x[..., :half], x[..., half:]
    return jnp.concatenate([x1 * cos - x2 * sin, x1 * sin + x2 * cos], axis=-1)

def chunk_len(L):
    return CHUNK if L % CHUNK == 0 else L

def to_chunks(x, c):
    B, H, L = x.shape[:3]
    x = x.reshape((B, H, L // c, c) + x.shape[3:])
    return jnp.moveaxis(x, 2, 0)

def from_chunks(x):
    x = jnp.moveaxis(x, 0, 2)
    return x.reshape((x.shape[0], x.shape[1], -1) + x.shape[4:])

def retention(q, k, v, log_gamma, s0):
    c = chunk_len(q.shape[2])
    idx = jnp.arange(c, dtype=jnp.float32)
    diff = idx[:, None] - idx[None, :]
    causal = diff >= 0
    lg = log_gamma[:, None, None]
    decay = jnp.where(causal, jnp.exp(jnp.where(causal, diff, 0.0) * lg), 0.0)
    q_dec = jnp.exp((idx + 1.0)[None, :] * log_gamma[:, None])
    k_dec = jnp.exp((c - 1.0 - idx)[None, :] * log_gamma[:, None])
    chunk_dec = jnp.exp(c * log_gamma)

    def step(s, inp):
        qc, kc, vc = inp
        scores = jnp.einsum('bhid,bhjd->bhij', qc, kc) * decay
        o = (jnp.einsum('bhij,bhjv->bhiv', scores, vc)
             + jnp.einsum('bhid,bhdv->bhiv', qc * q_dec[..., None], s))
        s = s * chunk_dec[:, None, None] + jnp.einsum('bhjd,bhjv->bhdv', kc * k_dec[..., None], vc)
        return s, o

    s, o = lax.scan(step, s0, (to_chunks(q, c), to_chunks(k, c), to_chunks(v, c)))
    return from_chunks(o), s

def gated_delta(q, k, v, g, beta, s0):
    c = chunk_len(q.shape[2])
    dv = v.shape[-1]
    incl = jnp.tril(jnp.ones((c, c), dtype=bool))
    strict = jnp.tril(jnp.ones((c, c), dtype=bool), k=-1)
    eye = jnp.eye(c, dtype=jnp.float32)

    def step(s, inp):
        qc, kc, vc, gc, bc = inp
        G = jnp.cumsum(gc, axis=-1)
        diff = G[..., :, None] - G[..., None, :]
        dec = jnp.where(incl, jnp.exp(jnp.where(incl, diff, 0.0)), 0.0)
        kk = jnp.einsum('bhid,bhjd->bhij', kc, kc)
        a_mat = jnp.where(strict, kk * dec * bc[..., :, None], 0.0)
        eG = jnp.exp(G)[..., None]
        rhs = jnp.concatenate([bc[..., None] * vc, bc[..., None] * eG * kc], axis=-1)
        sol = lax.linalg.triangular_solve(eye + a_mat, rhs, left_side=True, lower=True,
                                          unit_diagonal=True)
        u_mat, w_mat = sol[..., :dv], sol[..., dv:]
        delta = u_mat - jnp.einsum('bhid,bhdv->bhiv', w_mat, s)
        qk = jnp.einsum('bhid,bhjd->bhij', qc, kc) * dec
        o = (jnp.einsum('bhid,bhdv->bhiv', qc * eG, s)
             + jnp.einsum('bhij,bhjv->bhiv', qk, delta))
        g_last = G[..., -1:]
        s = (s * jnp.exp(g_last)[..., None]
             + jnp.einsum('bhjd,bhjv->bhdv', kc * jnp.exp(g_last - G)[..., None], delta))
        return s, o

    s, o = lax.scan(step, s0, (to_chunks(q, c), to_chunks(k, c), to_chunks(v, c),
                               to_chunks(g, c), to_chunks(beta, c)))
    return from_chunks(o), s

def hybrid_layer(h, p_l, s_ret, s_dn, s_conv, positions,
                 norm_mix, w_in, conv_w, dn_a_log, dn_dt_bias, dn_norm,
                 w_ret_up, w_dn_up, w_out,
                 norm_ffn, w_router_group, b_router_group, w_router_expert, b_router_expert,
                 w_gate_up, w_down, norm_ple, w_ple_gate, w_ple_proj):
    B, L, _ = h.shape
    dt = h.dtype
    f32 = jnp.float32

    def heads(t, n):
        return t.reshape(B, L, n, -1).transpose(0, 2, 1, 3).astype(f32)

    u = rmsnorm(h, norm_mix)
    proj = jnp.einsum('bld,de->ble', u, w_in)
    rq, rk, rv, rg, dqkv, dz, da, db, gate_a, gate_b = jnp.split(proj, _split_points(), axis=-1)

    q = rotary(heads(rq, RET_H), positions) * (RET_DK ** -0.5)
    k = rotary(heads(rk, RET_H), positions)
    v = heads(rv, RET_H)
    log_gamma = jnp.log(1.0 - 2.0 ** (-5.0 - jnp.arange(RET_H, dtype=f32)))
    o_r, s_ret_new = retention(q, k, v, log_gamma, s_ret.astype(f32))
    o_r = rms_plain(o_r).transpose(0, 2, 1, 3).reshape(B, L, RET_VW)
    o_r = o_r * jax.nn.silu(rg.astype(f32))
    branch_a = jnp.einsum('blv,vd->bld', o_r.astype(dt), w_ret_up)

    xpad = jnp.concatenate([s_conv.astype(dt), dqkv], axis=1)
    conv = xpad[:, 0:L] * conv_w[0]
    for j in range(1, CONV_W):
        conv = conv + xpad[:, j:j + L] * conv_w[j]
    conv = jax.nn.silu(conv.astype(f32))
    conv_new = xpad[:, L:]
    cq, ck, cv = jnp.split(conv, [DN_QK, 2 * DN_QK], axis=-1)
    qd = l2norm(heads(cq, DN_H)) * (DN_DK ** -0.5)
    kd = l2norm(heads(ck, DN_H))
    vd = heads(cv, DN_H)
    g = -jnp.exp(dn_a_log.astype(f32)) * jax.nn.softplus(da.astype(f32) + dn_dt_bias.astype(f32))
    beta = jax.nn.sigmoid(db.astype(f32))
    o_d, s_dn_new = gated_delta(qd, kd, vd, g.transpose(0, 2, 1), beta.transpose(0, 2, 1),
                                s_dn.astype(f32))
    o_d = rms_plain(o_d) * dn_norm.astype(f32)
    o_d = o_d.transpose(0, 2, 1, 3).reshape(B, L, DN_VW) * jax.nn.silu(dz.astype(f32))
    branch_b = jnp.einsum('blv,vd->bld', o_d.astype(dt), w_dn_up)

    merged = jax.nn.sigmoid(gate_a) * branch_a + jax.nn.sigmoid(gate_b) * branch_b
    h = h + jnp.einsum('bld,de->ble', merged, w_out)

    u = rmsnorm(h, norm_ffn)
    grp_logits = (jnp.einsum('bld,dg->blg', u, w_router_group) + b_router_group).astype(f32)
    grp_prob = jax.nn.softmax(grp_logits, axis=-1)
    grp = jnp.argmax(grp_logits, axis=-1)
    p_grp = jnp.take_along_axis(grp_prob, grp[..., None], axis=-1)
    exp_logits = (jnp.einsum('bld,de->ble', u, w_router_expert) + b_router_expert).astype(f32)
    exp_logits = exp_logits.reshape(B, L, N_GROUPS, EXPERTS_PER_GROUP)
    in_grp = jnp.take_along_axis(exp_logits, grp[..., None, None], axis=2)[..., 0, :]
    top_v, top_i = lax.top_k(in_grp, TOP_K)
    w_top = jax.nn.softmax(top_v, axis=-1) * p_grp
    expert_id = grp[..., None] * EXPERTS_PER_GROUP + top_i
    combine = jnp.sum(jax.nn.one_hot(expert_id, N_EXPERTS, dtype=f32) * w_top[..., None], axis=-2)
    combine = combine.astype(dt)
    moe = jnp.zeros_like(h)
    for e in range(N_EXPERTS):
        gu = jnp.einsum('bld,df->blf', u, w_gate_up[e])
        hid = jax.nn.silu(gu[..., :D_EXPERT]) * gu[..., D_EXPERT:]
        moe = moe + combine[..., e:e + 1] * jnp.einsum('blf,fd->bld', hid, w_down[e])
    h = h + moe

    u = rmsnorm(h, norm_ple)
    gate = jax.nn.sigmoid(jnp.einsum('bld,de->ble', u, w_ple_gate))
    h = h + gate * jnp.einsum('blp,pd->bld', p_l, w_ple_proj)
    return h, s_ret_new, s_dn_new, conv_new

def setup_inputs(seed: int = 0) -> dict:
    key = jax.random.key(seed)
    ks = jax.random.split(key, 32)
    f32 = jnp.float32

    def nrm(k, shape, scale):
        return jax.random.normal(k, shape, f32) * scale

    def gain(k, shape):
        return 1.0 + 0.05 * jax.random.normal(k, shape, f32)

    dt_init = jax.random.uniform(ks[11], (DEPTH, DN_H), f32, 0.001, 0.1)
    return {
        "x_prompt": nrm(ks[0], (BATCH, SEQ, D_MODEL), 1.0),
        "x_sample": nrm(ks[1], (DEC_BATCH, DEC_SEQ, D_MODEL), 1.0),
        "p_prompt": nrm(ks[2], (DEPTH, BATCH, SEQ, PLE_DIM), 1.0),
        "p_sample": nrm(ks[3], (DEPTH, DEC_BATCH, DEC_SEQ, PLE_DIM), 1.0),
        "state_ret": nrm(ks[4], (DEPTH, DEC_BATCH, RET_H, RET_DK, RET_DV), 0.5),
        "state_dn": nrm(ks[5], (DEPTH, DEC_BATCH, DN_H, DN_DK, DN_DV), 0.1),
        "state_conv": nrm(ks[6], (DEPTH, DEC_BATCH, CONV_W - 1, DN_CONV_CH), 0.5),
        "norm_mix": gain(ks[7], (DEPTH, D_MODEL)),
        "w_in": nrm(ks[8], (DEPTH, D_MODEL, IN_COLS), D_MODEL ** -0.5),
        "conv_w": nrm(ks[9], (DEPTH, CONV_W, DN_CONV_CH), CONV_W ** -0.5),
        "dn_a_log": jnp.log(jax.random.uniform(ks[10], (DEPTH, DN_H), f32, 1.0, 16.0)),
        "dn_dt_bias": jnp.log(jnp.expm1(dt_init)),
        "dn_norm": gain(ks[12], (DEPTH, DN_DV)),
        "w_ret_up": nrm(ks[13], (DEPTH, RET_VW, D_MODEL), RET_VW ** -0.5),
        "w_dn_up": nrm(ks[14], (DEPTH, DN_VW, D_MODEL), DN_VW ** -0.5),
        "w_out": nrm(ks[15], (DEPTH, D_MODEL, D_MODEL), D_MODEL ** -0.5),
        "norm_ffn": gain(ks[16], (DEPTH, D_MODEL)),
        "w_router_group": nrm(ks[17], (DEPTH, D_MODEL, N_GROUPS), D_MODEL ** -0.5),
        "b_router_group": nrm(ks[18], (DEPTH, N_GROUPS), 0.01),
        "w_router_expert": nrm(ks[19], (DEPTH, D_MODEL, N_EXPERTS), D_MODEL ** -0.5),
        "b_router_expert": nrm(ks[20], (DEPTH, N_EXPERTS), 0.01),
        "w_gate_up": nrm(ks[21], (DEPTH, N_EXPERTS, D_MODEL, 2 * D_EXPERT), D_MODEL ** -0.5),
        "w_down": nrm(ks[22], (DEPTH, N_EXPERTS, D_EXPERT, D_MODEL), D_EXPERT ** -0.5),
        "norm_ple": gain(ks[23], (DEPTH, D_MODEL)),
        "w_ple_gate": nrm(ks[24], (DEPTH, D_MODEL, D_MODEL), D_MODEL ** -0.5),
        "w_ple_proj": nrm(ks[25], (DEPTH, PLE_DIM, D_MODEL), PLE_DIM ** -0.5),
        "norm_final": gain(ks[26], (D_MODEL,)),
    }

def reference(x_prompt, x_sample, p_prompt, p_sample, state_ret, state_dn, state_conv,
              norm_mix, w_in, conv_w, dn_a_log, dn_dt_bias, dn_norm,
              w_ret_up, w_dn_up, w_out,
              norm_ffn, w_router_group, b_router_group, w_router_expert, b_router_expert,
              w_gate_up, w_down, norm_ple, w_ple_gate, w_ple_proj, norm_final):
    f32 = jnp.float32
    bp, lp = x_prompt.shape[0], x_prompt.shape[1]
    ls = x_sample.shape[1]
    pos_prompt = jnp.arange(lp, dtype=jnp.int32)
    pos_sample = PAST_LEN + jnp.arange(ls, dtype=jnp.int32)
    zero_ret = jnp.zeros((bp, RET_H, RET_DK, RET_DV), f32)
    zero_dn = jnp.zeros((bp, DN_H, DN_DK, DN_DV), f32)
    zero_conv = jnp.zeros((bp, CONV_W - 1, DN_CONV_CH), x_prompt.dtype)

    hp, hs = x_prompt, x_sample
    ret_p, dn_p, conv_p, ret_s, dn_s, conv_s = [], [], [], [], [], []
    for i in range(DEPTH):
        weights = (norm_mix[i], w_in[i], conv_w[i], dn_a_log[i], dn_dt_bias[i], dn_norm[i],
                   w_ret_up[i], w_dn_up[i], w_out[i],
                   norm_ffn[i], w_router_group[i], b_router_group[i], w_router_expert[i],
                   b_router_expert[i], w_gate_up[i], w_down[i], norm_ple[i], w_ple_gate[i],
                   w_ple_proj[i])
        hp, r_p, d_p, c_p = hybrid_layer(hp, p_prompt[i], zero_ret, zero_dn, zero_conv,
                                         pos_prompt, *weights)
        hs, r_s, d_s, c_s = hybrid_layer(hs, p_sample[i], state_ret[i], state_dn[i],
                                         state_conv[i], pos_sample, *weights)
        ret_p.append(r_p)
        dn_p.append(d_p)
        conv_p.append(c_p)
        ret_s.append(r_s)
        dn_s.append(d_s)
        conv_s.append(c_s)

    y_prompt = rmsnorm(hp, norm_final)
    y_sample = rmsnorm(hs, norm_final)
    ret_prompt = jnp.stack(ret_p, axis=0)
    dn_prompt = jnp.stack(dn_p, axis=0)
    conv_prompt = jnp.stack(conv_p, axis=0)
    ret_sample = jnp.stack(ret_s, axis=0)
    dn_sample = jnp.stack(dn_s, axis=0)
    conv_sample = jnp.stack(conv_s, axis=0)
    return (y_prompt, y_sample, ret_prompt, dn_prompt, conv_prompt, ret_sample, dn_sample, conv_sample)


_drawn_inputs = setup_inputs


def setup_inputs(seed=0):
    import zlib

    import numpy as np

    out = dict(_drawn_inputs(seed))
    spreads = {}
    factors = {'dn_norm': 2.898, 'b_router_expert': 13.169, 'norm_ple': 6.814, 'b_router_group': 5.124}
    for name, (base, spread) in spreads.items():
        noise = np.random.default_rng([zlib.crc32(name.encode()), seed]).standard_normal(out[name].shape)
        drawn = base * np.exp(spread * noise) if base else spread * noise
        out[name] = __import__('jax').numpy.asarray(drawn.astype(out[name].dtype))
    for name, factor in factors.items():
        out[name] = (out[name] * factor).astype(out[name].dtype)
    return out
```

```python
from contextlib import ExitStack

import numpy as np

import concourse.bass as bass
from concourse import mybir

F32 = mybir.dt.float32
U32 = mybir.dt.uint32
ALU = mybir.AluOpType
ACT = mybir.ActivationFunctionType
AX = mybir.AxisListType

P = 128
D = 1024
KD = D // P
LP, NB, LS = 512, 8, 8
TOK = LP + NB * LS
NT = 5
HALF = TOK // 2
H = 4
RDK, DK, DV = 64, 128, 128
CW = 4
NCONV = 12
NG, NE_G, NEXP, DE = 4, 4, 16, 256
NOV = 8
SLOTS = (NEXP + NOV) * P
PAST = 4096
EPS = 1e-6
CHUNK_W = 4096
RING = 3
GAMMA = [1.0 - 2.0 ** (-5.0 - h) for h in range(H)]
LEVELS = [2, 4, 8, 16, 32, 64]
BIG = 3.0e38


def ntok(t):
    return P if t < 4 else NB * LS


def levels(t):
    return LEVELS if t < 4 else [2, 4]


def constant_tables():
    f = np.float32
    p = np.arange(P)
    c = {}
    c["ident"] = np.eye(P, dtype=f)
    c["ones"] = np.ones((P, P), f)
    c["tri"] = (p[:, None] <= p[None, :]).astype(f)
    same = (p[:64, None] // LS) == (p[None, :64] // LS)
    pad = lambda a: np.concatenate([a, np.zeros((P - a.shape[0],) + a.shape[1:], a.dtype)]).astype(f)
    c["tri_s"] = pad(same & (p[:64, None] <= p[None, :64]))
    c["blk_s"] = pad(same)
    c["low"] = (p[:, None] > p[None, :]).astype(f)
    c["low_s"] = pad(same & (p[:64, None] > p[None, :64]))
    c["before"] = (p[:, None] < p[None, :]).astype(f)
    for s in [1] + LEVELS:
        m = (p[:, None] // (2 * s) == p[None, :] // (2 * s)) & ((p[:, None] // s) % 2 == 0) & ((p[None, :] // s) % 2 == 1)
        c[f"lev{s}"] = m.astype(f)
    c["lev1t"] = c["lev1"].T.copy()
    g = np.array(GAMMA, np.float64)
    i = p[None, None, :] - p[:, None, None]
    c["rdec"] = np.where(i >= 0, g[None, :, None] ** np.maximum(i, 0), 0.0).astype(f).reshape(P, -1)
    c["rdec_s"] = pad(np.where(same[:, None, :], c["rdec"].reshape(P, H, P)[:64, :, :64], 0.0).reshape(64, -1))
    c["rq"] = np.broadcast_to(0.125 * g[None, :, None] ** (p[None, None, :] + 1), (P, H, P)).astype(f).reshape(P, -1)
    c["rq_s"] = np.broadcast_to(0.125 * g[None, :, None] ** (p[None, None, :64] % LS + 1), (P, H, 64)).astype(f).reshape(P, -1)
    c["rk"] = (g[None, :] ** (P - 1 - p[:, None])).astype(f)
    c["rk_s"] = pad(g[None, :] ** (LS - 1 - p[:64, None] % LS))
    c["rstep"] = np.broadcast_to((g ** P)[None, :], (P, H)).astype(f)
    half = RDK // 2
    inv = (f(1.0) / (f(10000.0) ** (np.arange(half, dtype=f) / f(half)))).astype(f)
    pos = np.zeros((NT, P), f)
    for t in range(4):
        pos[t] = t * P + p
    pos[4, :64] = PAST + p[:64] % LS
    ang = (pos[:, :, None] * inv).astype(f).astype(np.float64)
    cos, sin = np.cos(ang), np.sin(ang)
    c["cos"] = cos.transpose(1, 0, 2).astype(f).reshape(P, -1)
    c["sin"] = np.stack([-sin, sin], 2).transpose(1, 0, 2, 3).astype(f).reshape(P, -1)
    c["row"] = pad((p[:64, None] // LS) == np.arange(NB)[None, :])
    c["first"] = np.broadcast_to(np.array([4, 3, 2, 1], f), (P, 4)).copy()
    valid = np.ones((P, NT), f)
    valid[64:, 4] = 0
    c["valid"] = valid
    c["slot0"] = np.broadcast_to(P * np.arange(NEXP, dtype=f), (P, NEXP)).copy()
    c["ovbase"] = np.broadcast_to(P * (NEXP - 1 - np.arange(NEXP, dtype=f)), (P, NEXP)).copy()
    c["iota"] = np.broadcast_to(np.arange(NOV, dtype=f), (P, NOV)).copy()
    c["eps"] = np.full((P, 1), EPS, f)
    return c


def const_layout():
    at, off = {}, 0
    for k, v in constant_tables().items():
        at[k] = (off, v.shape[1])
        off += v.shape[1]
    return at, off


CHUNKS = ["qk", "v", "dq", "dk", "dv", "rg", "dz", "ga0", "ga1", "upr", "gb0", "gb1", "upd", "wo0", "wo1", "proj"]


def schedule():
    s = [("ss",), ("ab",)]
    for t in range(NT):
        s += [("tmq", t)]
        if t: s += [("rS", t - 1)]
        s += [("tmv", t)]
        if t: s += [("rO", t - 1)]
        s += [("rTq", t), ("rTk", t)]
        if t: s += [("rU", t - 1)]
    s += [("cv", 0), ("rS", 4), ("cv", 1), ("cvs", 0), ("rO", 4)]
    s += [("rUs", h) for h in range(H)]
    s += [("cv", 2), ("cvs", 1)]
    s += [("rN", 0), ("rN", 1), ("nf", "rN", 0), ("rN", 2), ("nf", "rN", 1), ("rN", 3), ("nf", "rN", 2), ("nf", "rN", 3)]
    for m in range(3, NCONV):
        s += [("cv", m), ("cvs", m - 1)]
        if m == 7:
            s += [x for t in range(NT) for x in (("gG", t), ("gC", t))] + [("gE",)]
    for m in range(H):
        s += [("rg", m)] + ([("cvs", NCONV - 1)] if m == 0 else [])
        s += [("rgs", m), ("qn", 2 * m), ("qn", 2 * m + 1)]
        s += [("nf", "qn", 2 * m), ("nf", "qn", 2 * m + 1)]
    for t in range(NT):
        s += [("gK", t), ("gQ", t)]
    for t in range(NT):
        s += [("gA", t)]
    s += [("l1", t) for t in range(NT)]
    for v in LEVELS:
        on = [t for t in range(NT) if v in levels(t)]
        s += [("lA", v, t) for t in on[:2]]
        for n, t in enumerate(on):
            s += [("lY", v, t)]
            if n + 2 < len(on): s += [("lA", v, on[n + 2])]
        for t in on:
            if v != levels(t)[-1]: s += [("lX", v, t)]
            s += [("lT", v, t)]
    for t in range(NT):
        s += [("gV", t), ("gk", t), ("gW", t), ("gU", t), ("gq", t)]
    s += [("sO", 0), ("sU", 0), ("dz", 0), ("sD", 1), ("sDs",), ("sO", 1), ("sU", 1), ("sT",), ("dz", 1), ("dzs", 0),
          ("sD", 2), ("dz", 2), ("dzs", 1), ("sO", 2), ("sU", 2), ("sO", 4), ("dz", 3), ("dzs", 2), ("sD", 3), ("dzs", 3),
          ("sO", 3), ("sU", 3)]
    s += [("sUs", h) for h in range(H)]
    s += [("oN", 0), ("oN", 1), ("nf", "oN", 0), ("oN", 2), ("nf", "oN", 1), ("oN", 3), ("nf", "oN", 2), ("nf", "oN", 3)]
    s += [("gt", m) for m in range(8)] + [("up", m) for m in range(8)]
    s += [("gt", m) for m in range(8, 16)] + [("up", m) for m in range(8, 16)]
    for n in range(2):
        s += [("wo", n, t) for t in range(NT)]
    s += [("u2", t) for t in range(NT)]
    for t in range(NT):
        s += [("x2", t, n) for n in range(2)]
    s += [("rt",), ("rank",)]
    s += [("pp", t, n) for t in range(NT) for n in range(2)]
    return s


PAIR = {"ss", "tmq", "tmv", "rUs", "rN", "qn", "oN", "cv", "rg", "dz", "sUs", "gt", "up", "wo", "pp"}
SINGLE = {"ab", "rTq", "rTk", "rS", "rO", "rU", "gG", "gC", "gK", "gQ", "gA", "lY", "lX", "lT", "gV", "gk", "gW", "gU",
          "sD", "sDs", "sO", "sU", "sT", "x2", "rt", "rank"}
CHUNK_OF = {"tmq": lambda s: 0, "tmv": lambda s: 1, "cv": lambda s: 2 + s[1] // 4, "rg": lambda s: 5, "dz": lambda s: 6,
            "gt": lambda s: (7, 8, 10, 11)[s[1] // 4], "up": lambda s: (9, 12)[s[1] // 8],
            "wo": lambda s: 13 + s[1], "pp": lambda s: 15}


class Plan:

    def __init__(self):
        self.steps = schedule()
        self.order, self.mm, self.buf, self.before, self.chunk_last, self.norm = {}, {}, {}, {}, {}, {}
        count, nmm, npair, nsingle, last = {}, 0, 0, 0, {}
        for s in self.steps:
            k = s[0]
            count[k] = count.get(k, 0) + 1
            self.order[s] = count[k]
            if k in PAIR or k in SINGLE:
                nmm += 1
                self.mm[s] = nmm
                key = ("pair", npair % 2) if k in PAIR else ("single", nsingle % 4)
                if k in PAIR: npair += 1
                else: nsingle += 1
                self.buf[s] = key[1]
                self.before[s] = last.get(key)
                last[key] = s
            if k in CHUNK_OF:
                self.chunk_last[CHUNK_OF[k](s)] = s
            if k in ("rN", "qn", "oN"):
                self.norm[s] = len(self.norm)
        self.last_use = last
        self.norm_step = {n: s for s, n in self.norm.items()}


def build(nc, a, o):
    plan = Plan()
    CAT, NCONST = const_layout()
    STEPS = plan.steps

    u_rows = nc.dram_tensor("u_rows", (TOK, D), F32, kind="Internal").ap()
    slot_token = nc.dram_tensor("slot_token", (SLOTS, 1), U32, kind="Internal").ap()
    y_slots = nc.dram_tensor("y_slots", (SLOTS, D), F32, kind="Internal").ap()

    with ExitStack() as ctx:
        def sb(name, shape, dt=F32):
            return ctx.enter_context(nc.sbuf_tensor(name, shape, dt))

        sems = {}

        def sem(name):
            if name not in sems:
                sems[name] = ctx.enter_context(nc.semaphore(name))
            return sems[name]

        const = sb("const", [P, NCONST])

        def C(name, n=P):
            off, w = CAT[name]
            return const[0:n, off:off + w]

        vec = sb("vec", [P, 8 * 3 + 48 + 4 + 4 + 1 + 20])
        g_mix, g_ffn, g_ple = (vec[:, 8 * i:8 * i + 8] for i in range(3))
        conv_w = vec[:, 24:72].rearrange("p (m j) -> p m j", m=NCONV)
        a_log, dt_b, dn_gain, rt_bias = vec[:, 72:76], vec[:, 76:80], vec[:, 80:81], vec[:, 81:101]
        w_ab = sb("w_ab", [P, KD, 8])
        w_rt = sb("w_rt", [P, KD, 20])
        ab = sb("ab", [P, NT, 8])
        gl = sb("gl", [P, NT, H])
        beta = sb("beta", [P, NT, H])
        gcum = sb("gcum", [P, NT, 8])
        gx = sb("gx", [P, NT, 8])
        sm = sb("sm", [P, 3, NT, H])
        glast = sb("glast", [P, 4, H])
        glast_s = sb("glast_s", [P, H, NB])

        RINGO, UT, OR, CS, SQ, RR, MISC = 0, 12288, 16896, 19200, 26112, 27264, 28416
        BLK = MISC + 612
        MEM = BLK + 36 * 512
        mem = sb("mem", [P, MEM])

        def view(off, *dims, n=P):
            size = int(np.prod(dims))
            v = mem[0:n, off:off + size]
            if len(dims) == 2:
                v = v.rearrange("p (a b) -> p a b", a=dims[0])
            if len(dims) == 3:
                v = v.rearrange("p (a b c) -> p a b c", a=dims[0], b=dims[1])
            return v

        def slot(i):
            return BLK + 512 * i

        ring = [view(RINGO + CHUNK_W * i, CHUNK_W) for i in range(RING)]
        uT = view(UT, KD, TOK)
        o_ret = view(OR, H, TOK)
        cs = view(CS, NCONV, TOK)
        sq = [view(SQ + TOK * i, TOK) for i in range(2)]
        rr = [view(RR + TOK * i, TOK) for i in range(2)]
        cst = view(MISC, NCONV, NB, CW - 1)
        cnew = view(MISC + 288, NCONV, 27)
        qk = [view(slot(0) + 512 * i, 512) for i in range(2)]
        rot = [view(slot(2) + 512 * i, 512) for i in range(2)]
        rtmp = view(slot(4), 512)
        vt = [view(slot(5) + 512 * i, 512) for i in range(2)]
        qT = [view(slot(7) + 512 * i, H, P) for i in range(2)]
        kT = [view(slot(9) + 512 * i, H, P) for i in range(2)]
        qdT = [view(slot(11) + 512 * i, H, P) for i in range(2)]
        kdec_r = [view(slot(13) + 256 * i, H, RDK) for i in range(2)]
        sT = [view(slot(14) + 512 * i, H, P) for i in range(2)]
        S_ret = view(slot(16), H, DV)
        vexp = view(slot(17), NB, DV)
        sr = view(slot(20), NB, H, DV)
        cbuf = [view(slot(28) + 603 * i, 603) for i in range(2)]
        acc = [view(slot(28) + 1206 + 576 * i, TOK) for i in range(2)]
        def hb(base, t, n=None):
            w = ntok(t)
            return view(base, H, w, n=w if n is None else n)
        Am_ = [(slot(0 + t) if t < 4 else slot(20)) for t in range(NT)]
        D2_ = [(slot(4 + t) if t < 4 else slot(20) + 256) for t in range(NT)]
        E_ = [(slot(8 + t) if t < 4 else slot(21)) for t in range(NT)]
        AT_ = [(slot(12 + t) if t < 4 else slot(21) + 256) for t in range(NT)]
        X_ = [(slot(16 + t) if t < 4 else slot(22)) for t in range(NT)]
        XT_ = [(slot(23 + t) if t < 4 else slot(31)) for t in range(NT)]
        Y_ = [(slot(27 + t) if t < 4 else slot(31) + 256) for t in range(NT)]
        MSK = [slot(32), slot(33)]
        A = [hb(Am_[t], t) for t in range(NT)]
        D2 = [hb(D2_[t], t) for t in range(NT)]
        E = [hb(E_[t], t, P) for t in range(NT)]
        AT = [hb(AT_[t], t) for t in range(NT)]
        X = [hb(X_[t], t) for t in range(NT)]
        Gr = [hb(X_[t], t, P) for t in range(NT)]
        XT = [hb(XT_[t], t) for t in range(NT)]
        Y = [hb(Y_[t], t) for t in range(NT)]
        U_ = [(slot(0 + t) if t < 4 else slot(34)) for t in range(NT)]
        U = [view(U_[t], H, DV, n=ntok(t)) for t in range(NT)]
        nwT = [hb(AT_[t], t, P) for t in range(NT)]
        KD_ = [(slot(16 + t) if t < 4 else slot(35)) for t in range(NT)]
        kdec = [view(KD_[t], H, DK, n=ntok(t)) for t in range(NT)]
        bek = [view(slot(27 + t) if t < 4 else slot(28), H, DK, n=ntok(t)) for t in range(NT)]
        bV = [view(MSK[t % 2], H, DV, n=ntok(t)) for t in range(NT)]
        S_dn = view(SQ, H, DV)
        dlt = [view(MSK[t % 2], H, DV, n=ntok(t)) for t in range(4)] + [view(SQ + 512, H, DV, n=64)]
        sdn = view(slot(23), NB, H, DV)
        dexp = view(MSK[0], NB, DV, n=64)
        dTs = view(slot(22), H, 64)
        o_dn = view(CS + 8 * TOK, H, TOK)
        dzs = view(CS, H, TOK)
        sg = view(slot(18), KD, TOK)
        mT = view(slot(27), KD, TOK)
        h2 = view(CS, NT, D)
        pp = view(RINGO + 7168, NT, D)
        u2n = [view(OR + D * i, D) for i in range(2)]
        u2T = view(UT, KD, TOK)
        pT = view(SQ, 2, TOK)
        lg = sb("lg", [P, NT, 20])
        oneh = sb("oneh", [P, 3, NT, 4])
        rt = sb("rt", [P, 8, NT, 4])
        rs = sb("rs", [P, 8, NT])
        e12 = sb("e12", [P, 3, NT, NEXP])
        rk = sb("rk", [P, 6, NEXP])
        rx = sb("rx", [P, NT, NEXP])
        ov = sb("ov", [P, 4, NEXP])
        ovm = sb("ovm", [P, NOV, NEXP])
        ovf = sb("ovf", [P, NOV + 1])
        ovi = sb("ovi", [P, NOV + 1], U32)
        posu = sb("posu", [P, 2, NT], U32)
        placeu = sb("placeu", [P, 4, NT], U32)
        placef = sb("placef", [P, 4, NT])
        tokid = sb("tokid", [P, NT], U32)
        ids = sb("ids", [P, NEXP + NOV], U32)
        idx1 = sb("idx1", [P, 1], U32)
        wcomb = sb("wcomb", [P, 2, NT])
        ms = sb("ms", [P, 3, NT])
        zero = sb("zero", [P, SLOTS // P], U32)
        WB = [BLK, BLK + 6144, BLK + 12288, RINGO]
        w_gu_flat = [view(b, CHUNK_W) for b in WB]
        w_dn_flat = [view(b + 4096, 2 * D) for b in WB]
        w_gu = [view(b, KD, 2 * DE) for b in WB]
        w_dn = [view(b + 4096, 2, D) for b in WB]
        xg = [view(OR + D * i, D) for i in range(2)]
        xT = [view(SQ + D * i, KD, P) for i in range(2)]
        hid = [view(CS + 5120 + DE * i, DE) for i in range(2)]
        hT = [view(CS + 5632 + DE * i, 2, P) for i in range(2)]
        sgt = [view(CS + 6144 + DE * i, DE) for i in range(2)]
        yb = [view(UT + D * i, D) for i in range(2)]
        w_pg = [view(BLK + CHUNK_W * i, KD, 512) for i in range(2)]
        ga = [[view(BLK + 8192 + 2048 * i + D * j, D) for j in range(2)] for i in range(2)]
        yout = [view(BLK + 12288 + D * i, D) for i in range(2)]
        nfin = view(BLK + 14336, D)
        sgp = [view(SQ + D * i, D) for i in range(2)]
        u3n = [view(OR + D * i, D) for i in range(2)]
        u3T = view(UT, KD, TOK)

        pair = [ctx.enter_context(nc.psum_tensor(f"pair{i}", [P, 2, 512], F32)) for i in range(2)]
        single = [ctx.enter_context(nc.psum_tensor(f"single{i}", [P, 512], F32)) for i in range(4)]

        def split(ap):
            return ap.rearrange("p (a b) -> p a b", a=2)

        def pair576(s):
            return pair[plan.buf[s]][:, :, 0:HALF]

        def heads(s, n, w):
            return single[plan.buf[s]][0:n, 0:H * w].rearrange("p (h w) -> p h w", h=H)

        def tri(t):
            return C("tri") if t < 4 else C("tri_s", 64)

        def bc(ap, n, a_, w):
            return ap.unsqueeze(2).broadcast_to([n, a_, w])

        def bh(ap, n, w):
            return ap.unsqueeze(1).broadcast_to([n, H, w])

        s_mm = sem("mm_done")

        def ev(kind):
            return sem("ev_" + kind)

        def mm_wait(eng, s):
            eng.wait_ge(s_mm, plan.mm[s])

        def ev_wait(eng, s):
            eng.wait_ge(ev(s[0]), plan.order[s])

        block = ctx.enter_context(nc.Block())

        @block.sync
        def _(sp):
            for n, name in enumerate(CHUNKS):
                if n >= RING:
                    mm_wait(sp, plan.chunk_last[n - RING])
                dst = ring[n % RING][:, 0:2 * D] if name == "proj" else ring[n % RING]
                sp.dma_start(dst, a["w_" + name]).then_inc(sem(f"ring{n % RING}"), 16)
            free = {0: ("up", 0), 1: ("up", 15), 2: ("wo", 1, 4), 3: ("pp", 4, 1)}
            for e in range(4):
                mm_wait(sp, free[e])
                if e == 1:
                    sp.wait_ge(sem("mT"), KD)
                sp.dma_start(w_gu_flat[e], a["w_gu"][e * P:(e + 1) * P, :]).then_inc(sem(f"wgu{e}"), 16)
                sp.dma_start(w_dn_flat[e], a["w_down"][e * P:(e + 1) * P, :]).then_inc(sem(f"wgu{e}"), 16)

            def after_expert(e, u, more):
                sp.wait_ge(sem("y_ready"), 2 * e + 2)
                sp.dma_start(y_slots[bass.ds(e * P, P), :], yb[u % 2]).then_inc(sem(f"y_stored{u % 2}"), 16)
                if more:
                    sp.dma_start(w_gu_flat[u], a["w_gu"][bass.ds((e + 4) * P, P), :]).then_inc(sem(f"wgu{u}"), 16)
                    sp.dma_start(w_dn_flat[u], a["w_down"][bass.ds((e + 4) * P, P), :]).then_inc(sem(f"wgu{u}"), 16)

            for e in range(4):
                after_expert(e, e, True)
            with sp.Fori(1, 3) as i:
                for u in range(4):
                    after_expert(4 * i + u, u, True)
            for e in range(12, 16):
                after_expert(e, e % 4, False)
            sp.wait_ge(sem("ov_ready"), 1)
            n_ov = sp.value_load(ovi[0:1, NOV:NOV + 1], min_val=0, max_val=NOV)
            with sp.If(n_ov > 0):
                with sp.Fori(0, n_ov) as i:
                    sp.wait_ge(sem("ov_free"), i + 1)
                    e = sp.value_load(ovi[0:1, bass.ds(i, 1)], min_val=0, max_val=NEXP - 1)
                    sp.dma_start(w_gu_flat[0], a["w_gu"][bass.ds(e * P, P), :]).then_inc(sem("ov_w"), 16)
                    sp.dma_start(w_dn_flat[0], a["w_down"][bass.ds(e * P, P), :]).then_inc(sem("ov_w"), 16)
                    sp.wait_ge(sem("ov_y"), 2 * i + 2)
                    sp.dma_start(y_slots[bass.ds((i + NEXP) * P, P), :], yb[0]).then_inc(sem("ov_stored"), 16)
                    sp.wait_ge(sem("ov_stored"), 16 * i + 16)
                    sp.sem_inc(sem("ov_free"), 1)
            for b in range(2):
                sp.wait_ge(sem(f"y_stored{b}"), 16 * 8)
            sp.sem_inc(sem("y_all"), 1)
            for n in range(2):
                sp.dma_start(view(BLK + CHUNK_W * n, CHUNK_W), a[f"w_pg{n}"]).then_inc(sem("w_pg"), 16)
            sp.dma_start(nfin, a["norm_final"]).then_inc(sem("w_pg"), 16)
            for t in range(NT):
                sp.wait_ge(sem("y_out"), t + 1)
                sp.dma_start(o["y"][t * P:t * P + ntok(t), :], yout[t % 2][0:ntok(t), :]).then_inc(sem(f"out{t % 2}"), 16)
            sp.wait_ge(sem("out0"), 48)
            sp.wait_ge(sem("out1"), 32)

        @block.tensor
        def _(pe):
            def bank_free(s):
                prev = plan.before[s]
                if prev is not None:
                    ev_wait(pe, prev)

            def chunk(s):
                n = CHUNK_OF[s[0]](s)
                pe.wait_ge(sem(f"ring{n % RING}"), 16 * (n // RING + 1))
                return ring[n % RING]

            def gemm_channels(s, w, rhs, kk, fresh=True):
                pb = pair[plan.buf[s]]
                for k in range(kk):
                    for hf in range(2):
                        last = nc.tensor.matmul(pb[:, hf, 0:HALF], w(k), rhs[:, k, hf * HALF:(hf + 1) * HALF],
                                                start=(k == 0), stop=(k == kk - 1))
                last.then_inc(s_mm, 1)

            pe.wait_ge(sem("ld_const"), 16)
            for s in STEPS:
                k0 = s[0]
                if s not in plan.mm:
                    continue
                bank_free(s)
                if k0 == "ss":
                    pb = pair[plan.buf[s]]
                    for k in range(KD):
                        pe.wait_ge(sem("xsq"), k + 1)
                        for hf in range(2):
                            last = nc.tensor.matmul(pb[:, hf, 0:HALF], C("ones"), sq[k % 2][:, hf * HALF:(hf + 1) * HALF],
                                                    start=(k == 0), stop=(k == KD - 1))
                        if k < KD - 1:
                            last.then_inc(sem("xsq_used"), 1)
                    last.then_inc(s_mm, 1)
                elif k0 == "ab":
                    pe.wait_ge(sem("uT"), KD)
                    pe.wait_ge(sem("ld_small"), 16 * 5)
                    out = single[plan.buf[s]]
                    for t in range(NT):
                        for k in range(KD):
                            last = nc.tensor.matmul(out[0:ntok(t), 8 * t:8 * t + 8], uT[:, k, t * P:t * P + ntok(t)],
                                                    w_ab[:, k, :], start=(k == 0), stop=(k == KD - 1))
                    last.then_inc(s_mm, 1)
                elif k0 in ("tmq", "tmv"):
                    t = s[1]
                    w = chunk(s).rearrange("p (k c) -> p k c", k=KD)
                    for k in range(KD):
                        last = nc.tensor.matmul(pair[plan.buf[s]][0:ntok(t), 0, :], uT[:, k, t * P:t * P + ntok(t)],
                                                w[:, k, :], start=(k == 0), stop=(k == KD - 1))
                    last.then_inc(s_mm, 1)
                elif k0 in ("rTq", "rTk"):
                    t, n = s[1], ntok(s[1])
                    pe.wait_ge(sem("rot"), t + 1)
                    base = 0 if k0 == "rTq" else H * RDK
                    out = heads(s, RDK, n)
                    for h in range(H):
                        last = nc.tensor.transpose(out[:, h, :], rot[t % 2][0:n, base + h * RDK:base + (h + 1) * RDK],
                                                   C("ident")[0:n, 0:n])
                    last.then_inc(s_mm, 1)
                elif k0 == "rS":
                    t, n = s[1], ntok(s[1])
                    ev_wait(pe, ("rTq", t))
                    ev_wait(pe, ("rTk", t))
                    out = heads(s, n, n)
                    for h in range(H):
                        last = nc.tensor.matmul(out[:, h, :], kT[t % 2][0:RDK, h, 0:n], qT[t % 2][0:RDK, h, 0:n],
                                                start=True, stop=True)
                    last.then_inc(s_mm, 1)
                elif k0 == "rO":
                    t, n = s[1], ntok(s[1])
                    ev_wait(pe, ("rS", t))
                    ev_wait(pe, ("tmv", t))
                    if 0 < t < 4:
                        ev_wait(pe, ("rU", t - 1))
                    if t == 4:
                        pe.wait_ge(sem("ld_sr"), 16)
                    out = heads(s, P, n)
                    for h in range(H):
                        last = nc.tensor.matmul(out[:, h, :], vt[t % 2][0:n, h * DV:(h + 1) * DV], sT[t % 2][0:n, h, 0:n],
                                                start=True, stop=(t == 0), skip_group_check=(t == 4))
                        if 0 < t < 4:
                            last = nc.tensor.matmul(out[:, h, :], S_ret[0:RDK, h, :], qdT[t % 2][0:RDK, h, 0:n],
                                                    start=False, stop=True)
                        if t == 4:
                            for b in range(NB):
                                last = nc.tensor.matmul(out[:, h, LS * b:LS * b + LS], sr[0:RDK, b, h, :],
                                                        qdT[t % 2][0:RDK, h, LS * b:LS * b + LS],
                                                        start=False, stop=(b == NB - 1), skip_group_check=True)
                    last.then_inc(s_mm, 1)
                elif k0 == "rU":
                    t = s[1]
                    pe.wait_ge(sem("rkdec"), t + 1)
                    ev_wait(pe, ("tmv", t))
                    out = heads(s, RDK, DV)
                    for h in range(H):
                        last = nc.tensor.matmul(out[:, h, :], kdec_r[t % 2][:, h, :], vt[t % 2][:, h * DV:(h + 1) * DV],
                                                start=True, stop=True)
                    last.then_inc(s_mm, 1)
                elif k0 == "rUs":
                    h = s[1]
                    pe.wait_ge(sem("rkdec"), 5)
                    pe.wait_ge(sem("vexp"), h + 1)
                    pb = pair[plan.buf[s]]
                    for hf in range(2):
                        last = nc.tensor.matmul(pb[0:RDK, hf, :], kdec_r[0][0:64, h, :], vexp[0:64, 4 * hf:4 * hf + 4, :],
                                                start=True, stop=True)
                    last.then_inc(s_mm, 1)
                elif k0 in ("rN", "qn", "oN"):
                    q = plan.norm[s]
                    pe.wait_ge(sem("nsq"), q + 1)
                    pb = pair[plan.buf[s]]
                    for hf in range(2):
                        last = nc.tensor.matmul(pb[:, hf, 0:HALF], C("ones"), sq[q % 2][:, hf * HALF:(hf + 1) * HALF],
                                                start=True, stop=True)
                    last.then_inc(s_mm, 1)
                elif k0 in ("cv", "rg", "dz", "gt"):
                    w = chunk(s).rearrange("p (k c) -> p k c", k=KD)
                    m = s[1] % 4
                    if k0 == "cv":
                        pb = pair[plan.buf[s]]
                        for k in range(KD):
                            lhsT = w[:, k, m * P:(m + 1) * P]
                            nc.tensor.matmul(pb[:, 0, :], lhsT, uT[:, k, 0:LP], start=(k == 0), stop=(k == KD - 1))
                            last = nc.tensor.matmul(pb[:, 1, 0:NB * LS], lhsT, uT[:, k, LP:TOK],
                                                    start=(k == 0), stop=(k == KD - 1))
                        last.then_inc(s_mm, 1)
                    else:
                        gemm_channels(s, lambda k: w[:, k, m * P:(m + 1) * P], uT, KD)
                elif k0 == "up":
                    w = chunk(s).rearrange("p (k c) -> p k c", k=H)
                    m = s[1] % 8
                    if s[1] < 8:
                        pe.wait_ge(sem("o_ret"), H)
                        src = o_ret
                    else:
                        pe.wait_ge(sem("o_dn"), H)
                        src = o_dn
                    gemm_channels(s, lambda k: w[:, k, m * P:(m + 1) * P], src, H)
                elif k0 == "gG":
                    t, n = s[1], ntok(s[1])
                    pe.wait_ge(sem("g_beta"), 1)
                    out = heads(s, P, n)
                    for h in range(H):
                        last = nc.tensor.matmul(out[:, h, :], gl[0:n, t, h:h + 1].broadcast_to([n, P]), tri(t),
                                                start=True, stop=True)
                    last.then_inc(s_mm, 1)
                elif k0 == "gC":
                    t, n = s[1], ntok(s[1])
                    out = single[plan.buf[s]]
                    nc.tensor.matmul(out[0:n, 0:4], tri(t), gl[0:n, t, :], start=True, stop=True)
                    nc.tensor.matmul(out[0:n, 4:8], C("ones") if t < 4 else C("blk_s", 64), gl[0:n, t, :],
                                     start=True, stop=True).then_inc(s_mm, 1)
                elif k0 in ("gK", "gQ"):
                    t, n = s[1], ntok(s[1])
                    pe.wait_ge(sem("nfin"), 4 + 8)
                    out = heads(s, n, n)
                    for h in range(H):
                        kh = cs[:, 4 + h, t * P:t * P + n]
                        last = nc.tensor.matmul(out[:, h, :], kh, kh if k0 == "gK" else cs[:, h, t * P:t * P + n],
                                                start=True, stop=True)
                    last.then_inc(s_mm, 1)
                elif k0 == "gA":
                    t, n = s[1], ntok(s[1])
                    ev_wait(pe, ("gK", t))
                    out = heads(s, n, n)
                    for h in range(H):
                        last = nc.tensor.transpose(out[:, h, :], A[t][:, h, :], C("ident")[0:n, 0:n])
                    last.then_inc(s_mm, 1)
                elif k0 == "lY":
                    _, v, t = s
                    n = ntok(t)
                    pe.wait_ge(sem("lA"), plan.order[("lA", v, t)])
                    if v == 2:
                        pe.wait_ge(sem("l1X"), t + 1)
                    else:
                        ev_wait(pe, ("lX", v // 2, t))
                    out = heads(s, n, n)
                    am = hb(MSK[plan.order[("lA", v, t)] % 2], t)
                    for h in range(H):
                        last = nc.tensor.matmul(out[:, h, :], am[:, h, :], X[t][:, h, :], start=True, stop=True)
                    last.then_inc(s_mm, 1)
                elif k0 in ("lX", "lT"):
                    _, v, t = s
                    n = ntok(t)
                    ev_wait(pe, ("lY", v, t))
                    if v == 2:
                        pe.wait_ge(sem("l1T"), t + 1)
                    else:
                        ev_wait(pe, ("lT", v // 2, t))
                    out = heads(s, n, n)
                    for h in range(H):
                        if k0 == "lX":
                            last = nc.tensor.matmul(out[:, h, :], XT[t][:, h, :], Y[t][:, h, :], start=True, stop=True)
                        else:
                            last = nc.tensor.matmul(out[:, h, :], Y[t][:, h, :], XT[t][:, h, :], start=True, stop=True)
                    last.then_inc(s_mm, 1)
                elif k0 in ("gV", "gk"):
                    t, n = s[1], ntok(s[1])
                    if k0 == "gV":
                        pe.wait_ge(sem("conv"), NCONV)
                    out = single[plan.buf[s]][0:n, :].rearrange("p (h w) -> p h w", h=H)
                    for h in range(H):
                        last = nc.tensor.transpose(out[:, h, :], cs[:, (8 if k0 == "gV" else 4) + h, t * P:t * P + n],
                                                   C("ident"))
                    last.then_inc(s_mm, 1)
                elif k0 == "gW":
                    t, n = s[1], ntok(s[1])
                    ev_wait(pe, ("lT", levels(t)[-1], t))
                    pe.wait_ge(sem("bek"), t + 1)
                    out = heads(s, P, n)
                    for h in range(H):
                        last = nc.tensor.matmul(out[:, h, :], bek[t][:, h, :], XT[t][:, h, :], start=True, stop=True)
                    last.then_inc(s_mm, 1)
                elif k0 == "gU":
                    t, n = s[1], ntok(s[1])
                    ev_wait(pe, ("gV", t))
                    out = single[plan.buf[s]][0:n, :].rearrange("p (h w) -> p h w", h=H)
                    for h in range(H):
                        last = nc.tensor.matmul(out[:, h, :], XT[t][:, h, :], bV[t][:, h, :], start=True, stop=True)
                    last.then_inc(s_mm, 1)
                elif k0 in ("sD", "sDs"):
                    t = s[1] if k0 == "sD" else 4
                    n = ntok(t)
                    ev_wait(pe, ("gW", t))
                    if t < 4:
                        ev_wait(pe, ("sU", t - 1))
                        out = single[plan.buf[s]][0:n, :].rearrange("p (h w) -> p h w", h=H)
                        for h in range(H):
                            last = nc.tensor.matmul(out[:, h, :], nwT[t][:, h, :], S_dn[:, h, :], start=True, stop=True)
                    else:
                        pe.wait_ge(sem("ld_sd"), 16)
                        out = heads(s, P, n)
                        for h in range(H):
                            for b in range(NB):
                                last = nc.tensor.matmul(out[:, h, LS * b:LS * b + LS], sdn[:, b, h, :],
                                                        nwT[t][:, h, LS * b:LS * b + LS], start=True, stop=True)
                    last.then_inc(s_mm, 1)
                elif k0 == "sT":
                    ev_wait(pe, ("sDs",))
                    out = single[plan.buf[s]][0:64, :].rearrange("p (h w) -> p h w", h=H)
                    for h in range(H):
                        last = nc.tensor.transpose(out[:, h, :], dTs[:, h, :], C("ident"))
                    last.then_inc(s_mm, 1)
                elif k0 == "sO":
                    t, n = s[1], ntok(s[1])
                    ev_wait(pe, ("gQ", t))
                    pe.wait_ge(sem("qe"), t + 1)
                    if t == 0:
                        ev_wait(pe, ("gU", 0))
                    elif t < 4:
                        ev_wait(pe, ("sD", t))
                    else:
                        ev_wait(pe, ("sT",))
                    dl = U[0] if t == 0 else dlt[t]
                    out = heads(s, P, n)
                    for h in range(H):
                        last = nc.tensor.matmul(out[:, h, :], dl[:, h, :], D2[t][:, h, :], start=True, stop=(t == 0),
                                                skip_group_check=(t == 4))
                        if 0 < t < 4:
                            last = nc.tensor.matmul(out[:, h, :], S_dn[:, h, :], E[t][:, h, :], start=False, stop=True)
                        if t == 4:
                            for b in range(NB):
                                last = nc.tensor.matmul(out[:, h, LS * b:LS * b + LS], sdn[:, b, h, :],
                                                        E[t][:, h, LS * b:LS * b + LS],
                                                        start=False, stop=(b == NB - 1), skip_group_check=True)
                    last.then_inc(s_mm, 1)
                elif k0 == "sU":
                    t = s[1]
                    ev_wait(pe, ("gk", t))
                    dl = U[0] if t == 0 else dlt[t]
                    out = heads(s, P, P)
                    for h in range(H):
                        last = nc.tensor.matmul(out[:, h, :], kdec[t][:, h, :], dl[:, h, :], start=True, stop=True)
                    last.then_inc(s_mm, 1)
                elif k0 == "sUs":
                    h = s[1]
                    ev_wait(pe, ("gk", 4))
                    pe.wait_ge(sem("dexp"), h + 1)
                    pb = pair[plan.buf[s]]
                    for hf in range(2):
                        last = nc.tensor.matmul(pb[:, hf, :], kdec[4][:, h, :], dexp[:, 4 * hf:4 * hf + 4, :],
                                                start=True, stop=True)
                    last.then_inc(s_mm, 1)
                elif k0 == "wo":
                    _, n, t = s
                    w = chunk(s).rearrange("p (k c) -> p k c", k=KD)
                    ev_wait(pe, ("up", 15))
                    pe.wait_ge(sem("mT"), KD)
                    for k in range(KD):
                        last = nc.tensor.matmul(pair[plan.buf[s]][0:ntok(t), 0, :], mT[:, k, t * P:t * P + ntok(t)],
                                                w[:, k, :], start=(k == 0), stop=(k == KD - 1))
                    last.then_inc(s_mm, 1)
                elif k0 == "x2":
                    _, t, n = s
                    pe.wait_ge(sem("u2n"), t + 1)
                    out = single[plan.buf[s]][:, 0:4 * ntok(t)].rearrange("p (k w) -> p k w", k=4)
                    for k in range(4):
                        last = nc.tensor.transpose(out[:, k, :], u2n[t % 2][0:ntok(t), (4 * n + k) * P:(4 * n + k + 1) * P],
                                                   C("ident")[0:ntok(t), 0:ntok(t)])
                    last.then_inc(s_mm, 1)
                elif k0 == "rt":
                    ev_wait(pe, ("x2", 4, 1))
                    out = single[plan.buf[s]]
                    for t in range(NT):
                        for k in range(KD):
                            last = nc.tensor.matmul(out[0:ntok(t), 20 * t:20 * t + 20], u2T[:, k, t * P:t * P + ntok(t)],
                                                    w_rt[:, k, :], start=(k == 0), stop=(k == KD - 1))
                    last.then_inc(s_mm, 1)
                elif k0 == "rank":
                    pe.wait_ge(sem("picked"), 1)
                    out = single[plan.buf[s]]
                    for t in range(NT):
                        for t2 in range(t + 1):
                            nc.tensor.matmul(out[:, 16 * t:16 * t + 16], C("ones") if t2 < t else C("before"),
                                             e12[:, 2, t2, :], start=(t2 == 0), stop=(t2 == t))
                    for t in range(NT):
                        last = nc.tensor.matmul(out[:, 80:96], C("ones"), e12[:, 2, t, :], start=(t == 0), stop=(t == NT - 1))
                    last.then_inc(s_mm, 1)
                elif k0 == "pp":
                    _, t, n = s
                    w = chunk(s)[:, 0:2 * D].rearrange("p (k c) -> p k c", k=2)
                    pe.wait_ge(sem("ld_p"), 16)
                    for k in range(2):
                        last = nc.tensor.matmul(pair[plan.buf[s]][0:ntok(t), 0, :], pT[:, k, t * P:t * P + ntok(t)],
                                                w[:, k, n * 512:(n + 1) * 512], start=(k == 0), stop=(k == 1))
                    last.then_inc(s_mm, 1)
                else:
                    raise AssertionError(s)

            for key, s in plan.last_use.items():
                ev_wait(pe, s)

            def xpose(n_gather, n_prev, u):
                pe.wait_ge(sem(f"xg{u % 2}"), n_gather)
                if n_prev is not None:
                    pe.wait_ge(sem("xT"), n_prev)
                for k in range(KD):
                    out = single[k // 4][:, (k % 4) * P:(k % 4 + 1) * P]
                    last = nc.tensor.transpose(out, xg[u % 2][:, k * P:(k + 1) * P], C("ident"))
                last.then_inc(sem("xT_mm"), 1)

            def expert(e, u, nxt, first, xg_next):
                pe.wait_ge(sem("xT"), e + 1)
                pe.wait_ge(sem(f"wgu{u}"), xg_next[1])
                if not first:
                    pe.wait_ge(sem("hid"), e)
                for k in range(KD):
                    last = nc.tensor.matmul(single[3][:, :], xT[u % 2][:, k, :], w_gu[u][:, k, :],
                                            start=(k == 0), stop=(k == KD - 1))
                last.then_inc(sem("gu_mm"), 1)
                if nxt:
                    xpose(xg_next[0], e + 1, u + 1)
                pe.wait_ge(sem("hid"), e + 1)
                if not first:
                    pe.wait_ge(sem("hT"), e)
                for k in range(2):
                    last = nc.tensor.transpose(single[2][:, k * P:(k + 1) * P], hid[u % 2][:, k * P:(k + 1) * P], C("ident"))
                last.then_inc(sem("hT_mm"), 1)
                pe.wait_ge(sem("hT"), e + 1)
                if not (first and u < 2):
                    pe.wait_ge(sem("y_ready"), 2 * e - 2)
                for n in range(2):
                    for k in range(2):
                        last = nc.tensor.matmul(pair[u % 2][:, n, :], hT[u % 2][:, k, :], w_dn[u][:, k, n * 512:(n + 1) * 512],
                                                start=(k == 0), stop=(k == 1))
                last.then_inc(sem("dn_mm"), 1)

            xpose(16, None, 0)
            for e in range(4):
                expert(e, e, True, e == 0, (16 * ((e + 1) // 2 + 1), 32))
            with pe.Fori(1, 3) as i:
                for u in range(4):
                    expert(4 * i + u, u, True, False, ((i * 2 + (u + 1) // 2 + 1) * 16, i * 32 + 32))
            for e in range(12, 16):
                expert(e, e % 4, e < 15, False, (16 * ((e + 1) // 2 + 1), 128))
            pe.wait_ge(sem("ov_ready"), 1)
            pe.wait_ge(sem("y_ready"), 32)
            n_ov = pe.value_load(ovi[0:1, NOV:NOV + 1], min_val=0, max_val=NOV)
            pe.wait_ge(sem("dn_mm"), 16)
            pe.sem_inc(sem("ov_free"), 1)
            with pe.If(n_ov > 0):
                with pe.Fori(0, n_ov) as i:
                    pe.wait_ge(sem("ov_xg"), 16 * i + 16)
                    for k in range(KD):
                        out = single[k // 4][:, (k % 4) * P:(k % 4 + 1) * P]
                        last = nc.tensor.transpose(out, xg[0][:, k * P:(k + 1) * P], C("ident"))
                    last.then_inc(sem("ov_mm"), 1)
                    pe.wait_ge(sem("ov_xT"), i + 1)
                    pe.wait_ge(sem("ov_w"), 32 * i + 32)
                    for k in range(KD):
                        last = nc.tensor.matmul(single[3][:, :], xT[0][:, k, :], w_gu[0][:, k, :],
                                                start=(k == 0), stop=(k == KD - 1))
                    last.then_inc(sem("ov_gu"), 1)
                    pe.wait_ge(sem("ov_hid"), i + 1)
                    for k in range(2):
                        last = nc.tensor.transpose(single[2][:, k * P:(k + 1) * P], hid[0][:, k * P:(k + 1) * P], C("ident"))
                    last.then_inc(sem("ov_hTm"), 1)
                    pe.wait_ge(sem("ov_hT"), i + 1)
                    for n in range(2):
                        for k in range(2):
                            last = nc.tensor.matmul(pair[0][:, n, :], hT[0][:, k, :], w_dn[0][:, k, n * 512:(n + 1) * 512],
                                                    start=(k == 0), stop=(k == 1))
                    last.then_inc(sem("ov_dn"), 1)

            for t in range(NT):
                n = ntok(t)
                pe.wait_ge(sem("u3n"), t + 1)
                if t:
                    pe.wait_ge(sem("u3T"), 2 * t)
                for k in range(KD):
                    out = single[k // 4][:, (k % 4) * n:(k % 4 + 1) * n]
                    last = nc.tensor.transpose(out, u3n[t % 2][0:n, k * P:(k + 1) * P], C("ident")[0:n, 0:n])
                last.then_inc(sem("u3_mm"), 1)
                pe.wait_ge(sem("u3T"), 2 * t + 2)
                pe.wait_ge(sem("w_pg"), 48)
                if t >= 2:
                    pe.wait_ge(sem("sgp"), t - 1)
                for hf in range(2):
                    for k in range(KD):
                        last = nc.tensor.matmul(pair[t % 2][0:n, hf, :], u3T[:, k, t * P:t * P + n], w_pg[hf][:, k, :],
                                                start=(k == 0), stop=(k == KD - 1))
                last.then_inc(sem("pg_mm"), 1)

        @block.scalar
        def _(act):
            act.dma_start(const[:, :], a["const"]).then_inc(sem("ld_const"), 16)
            for k in range(0, KD, 4):
                act.dma_start(uT[:, k:k + 4, :], a["xT"][:, k:k + 4, :]).then_inc(sem(f"ld_x{k // 4}"), 16)
            act.dma_start(vec[:, :], a["vec"]).then_inc(sem("ld_small"), 16)
            act.dma_start(w_ab[:, :, :], a["w_ab"]).then_inc(sem("ld_small"), 16)
            act.dma_start(w_rt[:, :, :], a["w_rt"]).then_inc(sem("ld_small"), 16)
            act.dma_start(cst, a["state_conv"]).then_inc(sem("ld_small"), 16)
            act.dma_start(tokid[:, :], a["tokid"]).then_inc(sem("ld_small"), 16)
            act.dma_start(sr[0:RDK, :, :, :], a["state_ret"]).then_inc(sem("ld_sr"), 16)
            link_n = [0]

            def link(ins):
                link_n[0] += 1
                ins.then_inc(sem("act_link"), 1)
                act.wait_ge(sem("act_link"), link_n[0])

            copy = lambda out, in_, scale=1.0: nc.scalar.activation(out, in_, ACT.Copy, scale=scale)
            act.wait_ge(sem("ld_const"), 16)
            for s in STEPS:
                k0 = s[0]
                if k0 == "ss":
                    mm_wait(act, s)
                    nc.scalar.activation(split(rr[0]), pair576(s), ACT.Sqrt, bias=C("eps"), scale=1.0 / D).then_inc(ev(k0), 1)
                elif k0 == "tmq":
                    t, n = s[1], ntok(s[1])
                    mm_wait(act, s)
                    if t >= 2:
                        act.wait_ge(sem("rot"), t - 1)
                    copy(qk[t % 2][0:n, :], pair[plan.buf[s]][0:n, 0, :]).then_inc(ev(k0), 1)
                elif k0 == "tmv":
                    t, n = s[1], ntok(s[1])
                    mm_wait(act, s)
                    if t >= 2:
                        mm_wait(act, ("rU", t - 2))
                    copy(vt[t % 2][0:n, :], pair[plan.buf[s]][0:n, 0, :]).then_inc(ev(k0), 1)
                elif k0 == "rTk":
                    t, n = s[1], ntok(s[1])
                    mm_wait(act, s)
                    copy(kT[t % 2][0:RDK, :, 0:n], heads(s, RDK, n)).then_inc(ev(k0), 1)
                elif k0 in ("rO", "sO"):
                    t, n = s[1], ntok(s[1])
                    mm_wait(act, s)
                    dst = o_ret if k0 == "rO" else o_dn
                    copy(dst[:, :, t * P:t * P + n], heads(s, P, n)).then_inc(ev(k0), 1)
                elif k0 == "cv":
                    m = s[1]
                    mm_wait(act, s)
                    act.wait_ge(sem("cpad"), 1)
                    if m >= 2:
                        act.wait_ge(sem("cacc"), m - 1)
                        act.wait_ge(sem("cnew"), m - 1)
                    pb = pair[plan.buf[s]]
                    copy(cbuf[m % 2][:, 3:3 + LP], pb[:, 0, :])
                    copy(cbuf[m % 2][:, 515:603].rearrange("p (b l) -> p b l", b=NB)[:, :, 3:11],
                         pb[:, 1, 0:64].rearrange("p (b l) -> p b l", b=NB)).then_inc(ev(k0), 1)
                elif k0 == "cvs":
                    m = s[1]
                    act.wait_ge(sem("cacc"), m + 1)
                    nc.scalar.activation(cs[:, m, :], acc[m % 2], ACT.Silu).then_inc(sem("conv"), 1)
                elif k0 in ("rN", "qn", "oN"):
                    q = plan.norm[s]
                    mm_wait(act, s)
                    if q >= 2:
                        act.wait_ge(sem("nfin"), q - 1)
                    nc.scalar.activation(split(rr[q % 2]), pair576(s), ACT.Sqrt, bias=C("eps"),
                                         scale=1.0 if k0 == "qn" else 1.0 / DV).then_inc(ev(k0), 1)
                elif k0 == "rg":
                    m = s[1]
                    mm_wait(act, s)
                    if m:
                        act.wait_ge(sem("o_ret"), m)
                    else:
                        act.wait_ge(sem("conv"), NCONV - 1)
                    nc.scalar.activation(split(acc[0]), pair576(s), ACT.Silu).then_inc(ev(k0), 1)
                elif k0 == "gG":
                    t, n = s[1], ntok(s[1])
                    mm_wait(act, s)
                    act.wait_ge(sem("ret_free"), 1)
                    copy(Gr[t], heads(s, P, n)).then_inc(ev(k0), 1)
                elif k0 == "gE":
                    for t in range(NT):
                        n = ntok(t)
                        act.wait_ge(sem("gdiff"), t + 1)
                        nc.scalar.activation(A[t], A[t], ACT.Exp, scale=-1.0).then_inc(sem("gexp"), 1)
                        nc.scalar.activation(D2[t], D2[t], ACT.Exp).then_inc(sem("gexp"), 1)
                        nc.scalar.activation(E[t], Gr[t], ACT.Exp).then_inc(sem("gexp"), 1)
                        nc.scalar.activation(gx[0:n, t, 0:4], gcum[0:n, t, 0:4], ACT.Exp).then_inc(sem("gexp"), 1)
                        nc.scalar.activation(gx[0:n, t, 4:8], sm[0:n, 2, t, :], ACT.Exp).then_inc(sem("gexp"), 1)
                elif k0 == "ab":
                    act.wait_ge(sem("ab_abs"), 1)
                    link(nc.scalar.activation(sm[:, 1, :, :], sm[:, 1, :, :], ACT.Exp, scale=-1.0))
                    nc.scalar.activation(sm[:, 1, :, :], sm[:, 1, :, :], ACT.Ln, bias=C("ones")[:, 0:1])
                    nc.scalar.activation(glast[:, 0, :], a_log, ACT.Exp)
                    nc.scalar.activation(beta[:, :, :], ab[:, :, 4:8], ACT.Sigmoid).then_inc(sem("ab_act"), 1)
                elif k0 == "gA":
                    t, n = s[1], ntok(s[1])
                    mm_wait(act, s)
                    copy(AT[t], heads(s, n, n)).then_inc(ev(k0), 1)
                elif k0 == "lY":
                    _, v, t = s
                    n = ntok(t)
                    mm_wait(act, s)
                    copy(Y[t], heads(s, n, n)).then_inc(ev(k0), 1)
                elif k0 == "gW":
                    t, n = s[1], ntok(s[1])
                    mm_wait(act, s)
                    copy(nwT[t], heads(s, P, n), -1.0).then_inc(ev(k0), 1)
                elif k0 == "gU":
                    t, n = s[1], ntok(s[1])
                    mm_wait(act, s)
                    copy(U[t], single[plan.buf[s]][0:n, :].rearrange("p (h w) -> p h w", h=H)).then_inc(ev(k0), 1)
                    if t == 4:
                        mm_wait(act, ("gU", 4))
                        act.dma_start(sdn, a["state_dn"]).then_inc(sem("ld_sd"), 16)
                elif k0 == "sDs":
                    mm_wait(act, s)
                    copy(dTs, heads(s, P, 64)).then_inc(ev(k0), 1)
                elif k0 == "dz":
                    m = s[1]
                    mm_wait(act, s)
                    if m == 0:
                        act.wait_ge(sem("qe"), NT)
                    nc.scalar.activation(split(dzs[:, m, :]), pair576(s), ACT.Silu).then_inc(ev(k0), 1)
                elif k0 == "gt":
                    m = s[1]
                    mm_wait(act, s)
                    if m == 0:
                        act.wait_ge(sem("sd_stored"), 16)
                    if m >= 8:
                        ev_wait(act, ("up", m - 8))
                    nc.scalar.activation(split(sg[:, m % 8, :]), pair576(s), ACT.Sigmoid).then_inc(ev(k0), 1)
                elif k0 == "u2":
                    t, n = s[1], ntok(s[1])
                    if t == 0:
                        ev_wait(act, ("wo", 1, NT - 1))
                        for tt in range(NT):
                            nn = ntok(tt)
                            nc.scalar.activation(yb[0][0:nn, :], h2[0:nn, tt, :], ACT.Square,
                                                 accum_out=ms[0:nn, 0, tt:tt + 1]).then_inc(sem("ms"), 1)
                            act.wait_ge(sem("ms"), tt + 1)
                        nc.scalar.activation(ms[:, 1, :], ms[:, 0, :], ACT.Sqrt, bias=C("eps"), scale=1.0 / D)\
                            .then_inc(sem("ms_root"), 1)
                elif k0 == "rt":
                    act.wait_ge(sem("rt_exp"), 1)
                    nc.scalar.activation(rt[:, 1, :, :], rt[:, 0, :, :], ACT.Exp)
                    nc.scalar.activation(rs[:, 1, :], rs[:, 0, :], ACT.Exp).then_inc(sem("rt_act"), 1)
                elif k0 == "pp":
                    _, t, n = s
                    mm_wait(act, s)
                    copy(pp[0:ntok(t), t, n * 512:(n + 1) * 512], pair[plan.buf[s]][0:ntok(t), 0, :]).then_inc(ev(k0), 1)

            def expert_act(e, u, first):
                act.wait_ge(sem("gu_mm"), e + 1)
                nc.scalar.activation(sgt[u % 2], single[3][:, 0:DE], ACT.Silu).then_inc(sem("silu"), 1)
                act.wait_ge(sem("hT_mm"), e + 1)
                copy(hT[u % 2], single[2][:, 0:2 * P].rearrange("p (k w) -> p k w", k=2)).then_inc(sem("hT"), 1)
                act.wait_ge(sem("dn_mm"), e + 1)
                if not (first and u < 2):
                    act.wait_ge(sem(f"y_stored{u % 2}"), ((e - u) // 2 + u // 2) * 16)
                copy(yb[u % 2][:, 0:512], pair[u % 2][:, 0, :]).then_inc(sem("y_ready"), 1)
                copy(yb[u % 2][:, 512:D], pair[u % 2][:, 1, :]).then_inc(sem("y_ready"), 1)

            for e in range(4):
                expert_act(e, e, e < 4)
            with act.Fori(1, 4) as i:
                for u in range(4):
                    act.wait_ge(sem("gu_mm"), 4 * i + u + 1)
                    nc.scalar.activation(sgt[u % 2], single[3][:, 0:DE], ACT.Silu).then_inc(sem("silu"), 1)
                    act.wait_ge(sem("hT_mm"), 4 * i + u + 1)
                    copy(hT[u % 2], single[2][:, 0:2 * P].rearrange("p (k w) -> p k w", k=2)).then_inc(sem("hT"), 1)
                    act.wait_ge(sem("dn_mm"), 4 * i + u + 1)
                    act.wait_ge(sem(f"y_stored{u % 2}"), 32 * i + 16 * (u // 2))
                    copy(yb[u % 2][:, 0:512], pair[u % 2][:, 0, :]).then_inc(sem("y_ready"), 1)
                    copy(yb[u % 2][:, 512:D], pair[u % 2][:, 1, :]).then_inc(sem("y_ready"), 1)
            act.wait_ge(sem("ov_ready"), 1)
            act.wait_ge(sem("y_stored0"), 128)
            n_ov = act.value_load(ovi[0:1, NOV:NOV + 1], min_val=0, max_val=NOV)
            with act.If(n_ov > 0):
                with act.Fori(0, n_ov) as i:
                    act.wait_ge(sem("ov_gu"), i + 1)
                    nc.scalar.activation(sgt[0], single[3][:, 0:DE], ACT.Silu).then_inc(sem("ov_silu"), 1)
                    act.wait_ge(sem("ov_hTm"), i + 1)
                    copy(hT[0], single[2][:, 0:2 * P].rearrange("p (k w) -> p k w", k=2)).then_inc(sem("ov_hT"), 1)
                    act.wait_ge(sem("ov_dn"), i + 1)
                    copy(yb[0][:, 0:512], pair[0][:, 0, :]).then_inc(sem("ov_y"), 1)
                    copy(yb[0][:, 512:D], pair[0][:, 1, :]).then_inc(sem("ov_y"), 1)
            for t in range(NT):
                n = ntok(t)
                act.wait_ge(sem("h3"), t + 1)
                nc.scalar.activation(sgp[0][0:n, :], h2[0:n, t, :], ACT.Square,
                                     accum_out=ms[0:n, 0, t:t + 1]).then_inc(sem("ms"), 1)
                act.wait_ge(sem("ms"), NT + t + 1)
                nc.scalar.activation(ms[0:n, 1, t:t + 1], ms[0:n, 0, t:t + 1], ACT.Sqrt, bias=C("eps", n),
                                     scale=1.0 / D).then_inc(sem("ms_root"), 1)
            for t in range(NT):
                n = ntok(t)
                act.wait_ge(sem("pg_mm"), t + 1)
                if t >= 2:
                    act.wait_ge(sem("h4"), t - 1)
                nc.scalar.activation(sgp[t % 2][0:n, :].rearrange("p (a b) -> p a b", a=2), pair[t % 2][0:n, :, :],
                                     ACT.Sigmoid).then_inc(sem("sgp"), 1)
            for t in range(NT):
                n = ntok(t)
                act.wait_ge(sem("h4"), t + 1)
                if t == 0:
                    act.wait_ge(sem("h4"), NT)
                nc.scalar.activation(sgp[0][0:n, :], h2[0:n, t, :], ACT.Square,
                                     accum_out=ms[0:n, 0, t:t + 1]).then_inc(sem("ms"), 1)
                act.wait_ge(sem("ms"), 2 * NT + t + 1)
                nc.scalar.activation(ms[0:n, 1, t:t + 1], ms[0:n, 0, t:t + 1], ACT.Sqrt, bias=C("eps", n),
                                     scale=1.0 / D).then_inc(sem("ms_root"), 1)

        @block.vector
        def _(dve):
            V = nc.vector
            link_n = [0]

            def link(ins):
                link_n[0] += 1
                ins.then_inc(sem("dve_link"), 1)
                dve.wait_ge(sem("dve_link"), link_n[0])

            V.memset(cbuf[0][:, 0:3], 0.0)
            V.memset(cbuf[1][:, 0:3], 0.0).then_inc(sem("cpad"), 1)
            V.memset(ab[:, :, :], 0.0)
            V.memset(lg[:, :, :], 0.0)
            V.memset(ms[:, :, :], 1.0)
            link(V.memset(zero[:, :], 0))
            dve.wait_ge(sem("ld_const"), 16)
            for s in STEPS:
                k0 = s[0]
                if k0 == "ss":
                    for k in range(KD):
                        dve.wait_ge(sem(f"ld_x{k // 4}"), 16)
                        if k >= 2:
                            dve.wait_ge(sem("xsq_used"), k - 1)
                        V.tensor_tensor(sq[k % 2], uT[:, k, :], uT[:, k, :], ALU.mult).then_inc(sem("xsq"), 1)
                    ev_wait(dve, s)
                    link(V.reciprocal(rr[0], rr[0]))
                    dve.wait_ge(sem("ld_small"), 16 * 5)
                    for k in range(KD):
                        V.scalar_tensor_tensor(out=uT[:, k, :], in0=uT[:, k, :], scalar=g_mix[:, k:k + 1], in1=rr[0],
                                               op0=ALU.mult, op1=ALU.mult).then_inc(sem("uT"), 1)
                elif k0 == "ab":
                    mm_wait(dve, s)
                    src = single[plan.buf[s]]
                    V.tensor_copy(ab[:, 0:4, :], src[:, 0:32].rearrange("p (t c) -> p t c", t=4))
                    V.tensor_copy(ab[0:64, 4, :], src[0:64, 32:40]).then_inc(ev(k0), 1)
                    ev_wait(dve, s)
                    link(V.tensor_tensor(sm[:, 0, :, :], ab[:, :, 0:4], dt_b.unsqueeze(1).broadcast_to([P, NT, H]), ALU.add))
                    link(V.tensor_scalar(sm[:, 1, :, :], sm[:, 0, :, :], -1.0, None, ALU.mult))
                    V.tensor_tensor(sm[:, 1, :, :], sm[:, 1, :, :], sm[:, 0, :, :], ALU.max).then_inc(sem("ab_abs"), 1)
                    dve.wait_ge(sem("ab_act"), 1)
                    link(V.scalar_tensor_tensor(out=sm[:, 0, :, :].rearrange("p t h -> p (t h)"),
                                                in0=sm[:, 0, :, :].rearrange("p t h -> p (t h)"), scalar=0.0,
                                                in1=sm[:, 1, :, :].rearrange("p t h -> p (t h)"), op0=ALU.max, op1=ALU.add))
                    link(V.tensor_tensor(gl[:, :, :], sm[:, 0, :, :], glast[:, 0, :].unsqueeze(1).broadcast_to([P, NT, H]), ALU.mult))
                    V.tensor_scalar(gl[:, :, :], gl[:, :, :], -1.0, None, ALU.mult).then_inc(sem("g_beta"), 1)
                elif k0 == "rTq":
                    t, n = s[1], ntok(s[1])
                    mm_wait(dve, s)
                    V.tensor_scalar(qT[t % 2][0:RDK, :, 0:n], heads(s, RDK, n), 0.125, None, ALU.mult)
                    dec = (C("rq") if t < 4 else C("rq_s")).rearrange("p (h w) -> p h w", h=H)
                    V.tensor_tensor(qdT[t % 2][0:RDK, :, 0:n], heads(s, RDK, n), dec[0:RDK], ALU.mult).then_inc(ev(k0), 1)
                elif k0 == "rS":
                    t, n = s[1], ntok(s[1])
                    mm_wait(dve, s)
                    dec = (C("rdec") if t < 4 else C("rdec_s", 64)).rearrange("p (h w) -> p h w", h=H)
                    V.tensor_tensor(sT[t % 2][0:n, :, 0:n], heads(s, n, n), dec, ALU.mult).then_inc(ev(k0), 1)
                elif k0 == "rU":
                    t = s[1]
                    mm_wait(dve, s)
                    if t == 0:
                        V.tensor_copy(S_ret[0:RDK], heads(s, RDK, DV)).then_inc(ev(k0), 1)
                    else:
                        ev_wait(dve, ("rU", t - 1))
                        mm_wait(dve, ("rO", t))
                        link(V.tensor_tensor(S_ret[0:RDK], S_ret[0:RDK], bc(C("rstep")[0:RDK], RDK, H, DV), ALU.mult))
                        V.tensor_tensor(S_ret[0:RDK], S_ret[0:RDK], heads(s, RDK, DV), ALU.add).then_inc(ev(k0), 1)
                elif k0 == "rUs":
                    h = s[1]
                    mm_wait(dve, s)
                    pb = pair[plan.buf[s]]
                    for hf in range(2):
                        last = V.scalar_tensor_tensor(out=sr[0:RDK, 4 * hf:4 * hf + 4, h, :], in0=sr[0:RDK, 4 * hf:4 * hf + 4, h, :],
                                                      scalar=float(np.float32(GAMMA[h] ** LS)),
                                                      in1=pb[0:RDK, hf, :].rearrange("p (b v) -> p b v", b=4),
                                                      op0=ALU.mult, op1=ALU.add)
                    last.then_inc(ev(k0), 1)
                elif k0 == "cv":
                    m = s[1]
                    if m >= 2:
                        dve.wait_ge(sem("conv"), m - 1)
                    dve.wait_ge(sem("ld_small"), 16 * 5)
                    smp = cbuf[m % 2][:, 515:603].rearrange("p (b l) -> p b l", b=NB)
                    V.tensor_copy(smp[:, :, 0:3], cst[:, m, :, :]).then_inc(sem("cpads"), 1)
                    ev_wait(dve, s)
                    dve.wait_ge(sem("cpads"), m + 1)
                    V.tensor_copy(cnew[:, m, 0:3], cbuf[m % 2][:, 512:515])
                    V.tensor_copy(cnew[:, m, 3:27].rearrange("p (b l) -> p b l", b=NB), smp[:, :, 8:11]).then_inc(sem("cnew"), 1)
                    accs = acc[m % 2][:, LP:TOK].rearrange("p (b l) -> p b l", b=NB)
                    V.tensor_scalar(acc[m % 2][:, 0:LP], cbuf[m % 2][:, 0:LP], conv_w[:, m, 0:1], None, ALU.mult)
                    link(V.tensor_scalar(accs, smp[:, :, 0:LS], conv_w[:, m, 0:1], None, ALU.mult))
                    for j in range(1, CW):
                        V.scalar_tensor_tensor(out=acc[m % 2][:, 0:LP], in0=cbuf[m % 2][:, j:j + LP], scalar=conv_w[:, m, j:j + 1],
                                               in1=acc[m % 2][:, 0:LP], op0=ALU.mult, op1=ALU.add)
                        last = V.scalar_tensor_tensor(out=accs, in0=smp[:, :, j:j + LS], scalar=conv_w[:, m, j:j + 1],
                                                      in1=accs, op0=ALU.mult, op1=ALU.add)
                        if j < CW - 1:
                            link(last)
                    last.then_inc(sem("cacc"), 1)
                elif k0 in ("rN", "qn", "oN"):
                    q = plan.norm[s]
                    src = {"rN": o_ret, "qn": cs, "oN": o_dn}[k0][:, s[1], :]
                    if k0 == "rN": ev_wait(dve, ("rO", 4))
                    if k0 == "oN":
                        ev_wait(dve, ("sO", 3))
                        dve.wait_ge(sem("dp_stored"), 16)
                    if k0 == "qn": dve.wait_ge(sem("conv"), s[1] + 1)
                    if q >= 2:
                        mm_wait(dve, plan.norm_step[q - 2])
                    V.tensor_tensor(sq[q % 2], src, src, ALU.mult).then_inc(sem("nsq"), 1)
                elif k0 == "nf":
                    _, kind, m = s
                    q = plan.norm[(kind, m)]
                    ev_wait(dve, (kind, m))
                    link(V.reciprocal(rr[q % 2], rr[q % 2]))
                    if kind == "rN":
                        V.tensor_tensor(o_ret[:, m, :], o_ret[:, m, :], rr[q % 2], ALU.mult).then_inc(sem("nfin"), 1)
                    elif kind == "qn":
                        V.scalar_tensor_tensor(out=cs[:, m, :], in0=cs[:, m, :], scalar=DK ** -0.5 if m < H else 1.0,
                                               in1=rr[q % 2], op0=ALU.mult, op1=ALU.mult).then_inc(sem("nfin"), 1)
                    else:
                        V.scalar_tensor_tensor(out=o_dn[:, m, :], in0=o_dn[:, m, :], scalar=dn_gain, in1=rr[q % 2],
                                               op0=ALU.mult, op1=ALU.mult).then_inc(sem("nfin"), 1)
                        dve.wait_ge(sem("nfin"), q + 1)
                        ev_wait(dve, ("dz", m))
                        V.tensor_tensor(o_dn[:, m, :], o_dn[:, m, :], dzs[:, m, :], ALU.mult).then_inc(sem("o_dn"), 1)
                elif k0 == "rgs":
                    m = s[1]
                    ev_wait(dve, ("rg", m))
                    dve.wait_ge(sem("nfin"), m + 1)
                    V.tensor_tensor(o_ret[:, m, :], o_ret[:, m, :], acc[0], ALU.mult).then_inc(sem("o_ret"), 1)
                elif k0 == "gC":
                    t, n = s[1], ntok(s[1])
                    mm_wait(dve, s)
                    V.tensor_copy(gcum[0:n, t, :], single[plan.buf[s]][0:n, 0:8]).then_inc(ev(k0), 1)
                    ev_wait(dve, s)
                    V.tensor_tensor(sm[0:n, 2, t, :], gcum[0:n, t, 4:8], gcum[0:n, t, 0:4], ALU.subtract)
                    ev_wait(dve, ("gG", t))
                    for h in range(H):
                        V.tensor_scalar(A[t][:, h, :], Gr[t][0:n, h, :], gcum[0:n, t, h:h + 1], 0.0, ALU.subtract, ALU.max)
                        last = V.tensor_scalar(D2[t][:, h, :], Gr[t][0:n, h, :], gcum[0:n, t, h:h + 1], 0.0, ALU.subtract, ALU.min)
                    last.then_inc(sem("gdiff"), 1)
                elif k0 == "gE":
                    dve.wait_ge(sem("gexp"), 5 * NT)
                    for t in range(NT):
                        n = ntok(t)
                        if t < 4:
                            V.tensor_copy(glast[:, t, :], E[t][:, :, P - 1])
                        else:
                            V.tensor_copy(glast_s[:, :, :], E[t].rearrange("p h (b l) -> p h b l", b=NB)[:, :, :, LS - 1])
                        last = V.tensor_tensor(gx[0:n, t, 0:4], gx[0:n, t, 0:4], beta[0:n, t, :], ALU.mult)
                    last.then_inc(sem("gx"), 1)
                elif k0 == "gK":
                    t, n = s[1], ntok(s[1])
                    mm_wait(dve, s)
                    dve.wait_ge(sem("gmask"), 2 * t + 1)
                    for h in range(H):
                        last = V.scalar_tensor_tensor(out=A[t][:, h, :], in0=heads(s, n, n)[:, h, :], scalar=beta[0:n, t, h:h + 1],
                                                      in1=A[t][:, h, :], op0=ALU.mult, op1=ALU.mult)
                    last.then_inc(ev(k0), 1)
                elif k0 == "gQ":
                    t, n = s[1], ntok(s[1])
                    mm_wait(dve, s)
                    dve.wait_ge(sem("gmask"), 2 * t + 2)
                    V.tensor_tensor(D2[t], heads(s, n, n), D2[t], ALU.mult).then_inc(ev(k0), 1)
                elif k0 == "l1":
                    t, n = s[1], ntok(s[1])
                    ev_wait(dve, ("gA", t))
                    link(V.tensor_tensor(XT[t], AT[t], bh(C("lev1", n)[:, 0:n], n, n), ALU.mult))
                    V.tensor_tensor(XT[t], bh(C("ident", n)[:, 0:n], n, n), XT[t], ALU.subtract).then_inc(sem("l1T"), 1)
                elif k0 in ("lX", "lT"):
                    _, v, t = s
                    n = ntok(t)
                    mm_wait(dve, s)
                    if k0 == "lX":
                        if v == 2:
                            dve.wait_ge(sem("l1X"), t + 1)
                        dst = X[t]
                    else:
                        dst = XT[t]
                    V.tensor_tensor(dst, dst, heads(s, n, n), ALU.subtract).then_inc(ev(k0), 1)
                elif k0 == "gV":
                    t, n = s[1], ntok(s[1])
                    mm_wait(dve, s)
                    if t >= 2:
                        mm_wait(dve, ("gU", t - 2))
                    V.tensor_tensor(bV[t], single[plan.buf[s]][0:n, :].rearrange("p (h w) -> p h w", h=H),
                                    bc(beta[0:n, t, :], n, H, DV), ALU.mult).then_inc(ev(k0), 1)
                elif k0 == "gk":
                    t, n = s[1], ntok(s[1])
                    mm_wait(dve, s)
                    src = single[plan.buf[s]][0:n, :].rearrange("p (h w) -> p h w", h=H)
                    dve.wait_ge(sem("gx"), 1)
                    V.tensor_tensor(bek[t], src, bc(gx[0:n, t, 0:4], n, H, DK), ALU.mult).then_inc(sem("bek"), 1)
                    V.tensor_tensor(kdec[t], src, bc(gx[0:n, t, 4:8], n, H, DK), ALU.mult).then_inc(ev(k0), 1)
                elif k0 == "sD":
                    t, n = s[1], ntok(s[1])
                    mm_wait(dve, s)
                    ev_wait(dve, ("gU", t))
                    V.tensor_tensor(dlt[t], single[plan.buf[s]][0:n, :].rearrange("p (h w) -> p h w", h=H), U[t],
                                    ALU.add).then_inc(ev(k0), 1)
                elif k0 == "sT":
                    mm_wait(dve, s)
                    ev_wait(dve, ("gU", 4))
                    V.tensor_tensor(dlt[4], single[plan.buf[s]][0:64, :].rearrange("p (h w) -> p h w", h=H), U[4],
                                    ALU.add).then_inc(ev(k0), 1)
                elif k0 == "sU":
                    t = s[1]
                    mm_wait(dve, s)
                    if t == 0:
                        V.tensor_copy(S_dn, heads(s, P, P)).then_inc(ev(k0), 1)
                    else:
                        ev_wait(dve, ("sU", t - 1))
                        for h in range(H):
                            last = V.scalar_tensor_tensor(out=S_dn[:, h, :], in0=S_dn[:, h, :], scalar=glast[:, t, h:h + 1],
                                                          in1=heads(s, P, P)[:, h, :], op0=ALU.mult, op1=ALU.add)
                        last.then_inc(ev(k0), 1)
                elif k0 == "sUs":
                    h = s[1]
                    mm_wait(dve, s)
                    dve.wait_ge(sem("sdec"), h + 1)
                    pb = pair[plan.buf[s]]
                    for hf in range(2):
                        last = V.tensor_tensor(sdn[:, 4 * hf:4 * hf + 4, h, :], sdn[:, 4 * hf:4 * hf + 4, h, :],
                                               pb[:, hf, :].rearrange("p (b v) -> p b v", b=4), ALU.add)
                    last.then_inc(ev(k0), 1)
                elif k0 == "up":
                    m = s[1]
                    mm_wait(dve, s)
                    ev_wait(dve, ("gt", m))
                    if m < 8:
                        V.tensor_tensor(split(mT[:, m, :]), split(sg[:, m, :]), pair576(s), ALU.mult).then_inc(ev(k0), 1)
                    else:
                        V.tensor_tensor(split(sg[:, m - 8, :]), split(sg[:, m - 8, :]), pair576(s), ALU.mult).then_inc(ev(k0), 1)
                        ev_wait(dve, s)
                        V.tensor_tensor(mT[:, m - 8, :], mT[:, m - 8, :], sg[:, m - 8, :], ALU.add).then_inc(sem("mT"), 1)
                elif k0 == "wo":
                    _, n, t = s
                    mm_wait(dve, s)
                    dve.wait_ge(sem("ld_h"), 32)
                    V.tensor_tensor(h2[0:ntok(t), t, n * 512:(n + 1) * 512], h2[0:ntok(t), t, n * 512:(n + 1) * 512],
                                    pair[plan.buf[s]][0:ntok(t), 0, :], ALU.add).then_inc(ev(k0), 1)
                elif k0 == "u2":
                    t, n = s[1], ntok(s[1])
                    if t == 0:
                        dve.wait_ge(sem("ms_root"), 1)
                        link(V.reciprocal(ms[:, 2, :], ms[:, 1, :]))
                    if t >= 2:
                        mm_wait(dve, ("x2", t - 2, 1))
                        dve.wait_ge(sem(f"u_rows{t % 2}"), 16 * (t // 2))
                    V.tensor_scalar(u2n[t % 2][0:n, :], h2[0:n, t, :], ms[0:n, 2, t:t + 1], None, ALU.mult).then_inc(sem("u2n"), 1)
                    for tt in ([t - 1] if t else []) + ([4] if t == 4 else []):
                        for hf in range(2):
                            st = ("x2", tt, hf)
                            mm_wait(dve, st)
                            V.tensor_tensor(u2T[:, 4 * hf:4 * hf + 4, tt * P:tt * P + ntok(tt)],
                                            single[plan.buf[st]][:, 0:4 * ntok(tt)].rearrange("p (k w) -> p k w", k=4),
                                            bc(g_ffn[:, 4 * hf:4 * hf + 4], P, 4, ntok(tt)), ALU.mult).then_inc(ev("x2"), 1)
                elif k0 == "rt":
                    mm_wait(dve, s)
                    src = single[plan.buf[s]]
                    bias = rt_bias.unsqueeze(1)
                    V.tensor_tensor(lg[:, 0:4, :], src[:, 0:80].rearrange("p (t c) -> p t c", t=4), bias.broadcast_to([P, 4, 20]), ALU.add)
                    V.tensor_tensor(lg[0:64, 4, :], src[0:64, 80:100], rt_bias[0:64, :], ALU.add).then_inc(ev(k0), 1)
                    ev_wait(dve, s)
                    b4 = lambda x: x.unsqueeze(2).broadcast_to([P, NT, 4])

                    def first_max(values, best, diff, hot):
                        link(V.reduce_max(best, values, AX.X))
                        link(V.tensor_tensor(diff, values, b4(best), ALU.subtract))
                        link(V.tensor_scalar(hot, diff, 0.0, None, ALU.is_equal))
                        link(V.tensor_tensor(hot, hot, C("first").unsqueeze(1).broadcast_to([P, NT, 4]), ALU.mult))
                        link(V.reduce_max(rs[:, 6, :], hot, AX.X))
                        link(V.tensor_tensor(hot, hot, b4(rs[:, 6, :]), ALU.is_equal))

                    first_max(lg[:, :, 0:4], rs[:, 2, :], rt[:, 0, :, :], oneh[:, 0])
                    for g in range(NG):
                        dst = rt[:, 2, :, :] if g == 0 else rt[:, 3, :, :]
                        link(V.tensor_tensor(dst, lg[:, :, 4 + 4 * g:8 + 4 * g], b4(oneh[:, 0, :, g]), ALU.mult))
                        if g:
                            link(V.tensor_tensor(rt[:, 2, :, :], rt[:, 2, :, :], rt[:, 3, :, :], ALU.add))
                    first_max(rt[:, 2], rs[:, 3, :], rt[:, 3], oneh[:, 1])
                    link(V.tensor_scalar(rt[:, 4], oneh[:, 1], -BIG, None, ALU.mult))
                    link(V.tensor_tensor(rt[:, 4], rt[:, 4], rt[:, 2], ALU.add))
                    first_max(rt[:, 4], rs[:, 4, :], rt[:, 3], oneh[:, 2])
                    V.tensor_tensor(rs[:, 0, :], rs[:, 4, :], rs[:, 3, :], ALU.subtract).then_inc(sem("rt_exp"), 1)
                    link(V.tensor_tensor(oneh[:, 0], oneh[:, 0], b4(C("valid")), ALU.mult))
                    for j in range(2):
                        for g in range(NG):
                            last = V.tensor_tensor(e12[:, j, :, 4 * g:4 * g + 4], oneh[:, 1 + j], b4(oneh[:, 0, :, g]), ALU.mult)
                    link(last)
                    V.tensor_tensor(e12[:, 2], e12[:, 0], e12[:, 1], ALU.add).then_inc(sem("picked"), 1)
                    dve.wait_ge(sem("rt_act"), 1)
                    link(V.reduce_sum(rs[:, 2, :], rt[:, 1], AX.X))
                    link(V.tensor_scalar(rs[:, 3, :], rs[:, 1, :], 1.0, None, ALU.add))
                    link(V.tensor_tensor(rs[:, 2, :], rs[:, 2, :], rs[:, 3, :], ALU.mult))
                    link(V.reciprocal(wcomb[:, 0, :], rs[:, 2, :]))
                    link(V.tensor_tensor(wcomb[:, 1, :], wcomb[:, 0, :], rs[:, 1, :], ALU.mult))
                elif k0 == "rank":
                    mm_wait(dve, s)
                    V.tensor_copy(rk[:, :, :], single[plan.buf[s]][:, 0:96].rearrange("p (t e) -> p t e", t=6)).then_inc(ev(k0), 1)
                    ev_wait(dve, s)
                    cnt = rk[:, 5, :]
                    link(V.tensor_scalar(ov[:, 0, :], cnt, 128.0, None, ALU.is_gt))
                    for k in (256.0, 384.0, 512.0):
                        link(V.tensor_scalar(ov[:, 1, :], cnt, k, None, ALU.is_gt))
                        link(V.tensor_tensor(ov[:, 0, :], ov[:, 0, :], ov[:, 1, :], ALU.add))
                    link(V.tensor_tensor_scan(ov[:, 1, :], C("ones")[:, 0:NEXP], ov[:, 0, :], 0.0, ALU.mult, ALU.add))
                    link(V.tensor_tensor(ov[:, 2, :], ov[:, 1, :], ov[:, 0, :], ALU.subtract))
                    link(V.scalar_tensor_tensor(out=ov[:, 3, :], in0=ov[:, 2, :], scalar=float(P), in1=C("ovbase"), op0=ALU.mult, op1=ALU.add))
                    link(V.tensor_scalar(rx[:, :, :], rk[:, 0:5, :], 128.0, None, ALU.is_ge))
                    link(V.tensor_tensor(rx[:, :, :], rx[:, :, :], ov[:, 3, :].unsqueeze(1).broadcast_to([P, NT, NEXP]), ALU.mult))
                    link(V.tensor_tensor(rx[:, :, :], rx[:, :, :], rk[:, 0:5, :], ALU.add))
                    link(V.tensor_tensor(rx[:, :, :], rx[:, :, :], C("slot0").unsqueeze(1).broadcast_to([P, NT, NEXP]), ALU.add))
                    for j in range(2):
                        link(V.tensor_tensor(e12[:, j], e12[:, j], rx[:, :, :], ALU.mult))
                        link(V.reduce_sum(rs[:, 5, :], e12[:, j], AX.X))
                        link(V.tensor_copy(posu[:, j, :], rs[:, 5, :]))
                    link(V.tensor_scalar(placeu[:, 0:2], posu[:, :, :], P - 1, None, ALU.bitwise_and))
                    link(V.tensor_scalar(placeu[:, 2:4], posu[:, :, :], 7, None, ALU.logical_shift_right))
                    link(V.tensor_copy(placef[:, :, :], placeu[:, :, :]))
                    link(V.tensor_scalar(placef[:, 0:2], placef[:, 0:2], float(NEXP + NOV), None, ALU.mult))
                    link(V.tensor_tensor(placef[:, 0:2], placef[:, 0:2], placef[:, 2:4], ALU.add))
                    link(V.tensor_copy(placeu[:, 0:2], placef[:, 0:2]))
                    link(V.tensor_tensor(ovm[:, :, :], ov[:, 1, :].unsqueeze(1).broadcast_to([P, NOV, NEXP]),
                                         C("iota").unsqueeze(2).broadcast_to([P, NOV, NEXP]), ALU.is_le))
                    link(V.reduce_sum(ovf[:, 0:NOV], ovm[:, :, :], AX.X))
                    link(V.tensor_scalar(ovf[:, 0:NOV], ovf[:, 0:NOV], float(NEXP - 1), None, ALU.min))
                    link(V.tensor_copy(ovf[:, NOV:NOV + 1], ov[:, 1, NEXP - 1:NEXP]))
                    V.tensor_copy(ovi[:, :], ovf[:, :]).then_inc(sem("ov_ready"), 1)

            def expert_dve(e, u, first):
                dve.wait_ge(sem("gu_mm"), e + 1)
                dve.wait_ge(sem("silu"), e + 1)
                if not (first and u < 2):
                    dve.wait_ge(sem("hT_mm"), e - 1)
                V.tensor_tensor(hid[u % 2], sgt[u % 2], single[3][:, DE:2 * DE], ALU.mult).then_inc(sem("hid"), 1)

            def x_evac(u, count, into, done):
                dve.wait_ge(sem("xT_mm"), count)
                for hf in range(2):
                    last = V.tensor_tensor(into[u % 2][:, 4 * hf:4 * hf + 4, :], single[hf][:, :].rearrange("p (k w) -> p k w", k=4),
                                           bc(g_ffn[:, 4 * hf:4 * hf + 4], P, 4, P), ALU.mult)
                last.then_inc(done, 1)

            x_evac(0, 1, xT, sem("xT"))
            for e in range(4):
                expert_dve(e, e, True)
                x_evac(e + 1, e + 2, xT, sem("xT"))
            with dve.Fori(1, 3) as i:
                for u in range(4):
                    expert_dve(4 * i + u, u, False)
                    x_evac(u + 1, 4 * i + u + 2, xT, sem("xT"))
            for e in range(12, 16):
                expert_dve(e, e % 4, False)
                if e < 15:
                    x_evac(e + 1, e + 2, xT, sem("xT"))
            dve.wait_ge(sem("ov_ready"), 1)
            n_ov = dve.value_load(ovi[0:1, NOV:NOV + 1], min_val=0, max_val=NOV)
            dve.wait_ge(sem("dn_mm"), 16)
            with dve.If(n_ov > 0):
                with dve.Fori(0, n_ov) as i:
                    dve.wait_ge(sem("ov_mm"), i + 1)
                    for hf in range(2):
                        last = V.tensor_tensor(xT[0][:, 4 * hf:4 * hf + 4, :], single[hf][:, :].rearrange("p (k w) -> p k w", k=4),
                                               bc(g_ffn[:, 4 * hf:4 * hf + 4], P, 4, P), ALU.mult)
                    last.then_inc(sem("ov_xT"), 1)
                    dve.wait_ge(sem("ov_gu"), i + 1)
                    dve.wait_ge(sem("ov_silu"), i + 1)
                    V.tensor_tensor(hid[0], sgt[0], single[3][:, DE:2 * DE], ALU.mult).then_inc(sem("ov_hid"), 1)
            for t in range(NT):
                n = ntok(t)
                for j in range(2):
                    dve.wait_ge(sem(f"ga{j}{t % 2}"), 16 * (t // 2 + 1))
                    ins = V.scalar_tensor_tensor(out=h2[0:n, t, :], in0=ga[t % 2][j][0:n, :], scalar=wcomb[0:n, j, t:t + 1],
                                                 in1=h2[0:n, t, :], op0=ALU.mult, op1=ALU.add)
                    if j == 0:
                        link(ins)
                ins.then_inc(sem("h3"), 1)
            for t in range(NT):
                n = ntok(t)
                dve.wait_ge(sem("ms_root"), 1 + t + 1)
                link(V.reciprocal(ms[0:n, 2, t:t + 1], ms[0:n, 1, t:t + 1]))
                if t >= 2:
                    dve.wait_ge(sem("u3_mm"), t - 1)
                dve.wait_ge(sem("h3"), t + 1)
                V.tensor_scalar(u3n[t % 2][0:n, :], h2[0:n, t, :], ms[0:n, 2, t:t + 1], None, ALU.mult).then_inc(sem("u3n"), 1)
                dve.wait_ge(sem("u3_mm"), t + 1)
                for hf in range(2):
                    V.tensor_tensor(u3T[:, 4 * hf:4 * hf + 4, t * P:t * P + n], single[hf][:, 0:4 * n].rearrange("p (k w) -> p k w", k=4),
                                    bc(g_ple[:, 4 * hf:4 * hf + 4], P, 4, n), ALU.mult).then_inc(sem("u3T"), 1)
            for t in range(NT):
                n = ntok(t)
                dve.wait_ge(sem("sgp"), t + 1)
                link(V.tensor_tensor(sgp[t % 2][0:n, :], sgp[t % 2][0:n, :], pp[0:n, t, :], ALU.mult))
                V.tensor_tensor(h2[0:n, t, :], h2[0:n, t, :], sgp[t % 2][0:n, :], ALU.add).then_inc(sem("h4"), 1)
            dve.wait_ge(sem("w_pg"), 48)
            for t in range(NT):
                n = ntok(t)
                dve.wait_ge(sem("ms_root"), 1 + NT + t + 1)
                link(V.reciprocal(ms[0:n, 2, t:t + 1], ms[0:n, 1, t:t + 1]))
                if t >= 2:
                    dve.wait_ge(sem(f"out{t % 2}"), 16 * (t // 2))
                V.scalar_tensor_tensor(out=yout[t % 2][0:n, :], in0=h2[0:n, t, :], scalar=ms[0:n, 2, t:t + 1], in1=nfin[0:n, :],
                                       op0=ALU.mult, op1=ALU.mult).then_inc(sem("y_out"), 1)

        @block.gpsimd
        def _(pool):
            G = nc.gpsimd
            for i in range(NOV):
                pool.dma_start(y_slots[(NEXP + i) * P:(NEXP + i + 1) * P, :], a["zeros"]).then_inc(sem("y_zero"), 16)
            pool.wait_ge(sem("dve_link"), 1)
            pool.dma_start(slot_token.rearrange("(p b) o -> p (b o)", p=P), zero[:, :]).then_inc(sem("tok_zero"), 16)
            pool.wait_ge(sem("ld_const"), 16)
            for s in STEPS:
                k0 = s[0]
                if k0 == "tmq":
                    t, n = s[1], ntok(s[1])
                    ev_wait(pool, s)
                    if t >= 2:
                        mm_wait(pool, ("rTk", t - 2))
                        pool.wait_ge(sem("rkdec"), t - 1)
                    x4 = qk[t % 2][0:n, :].rearrange("p (h a w) -> p h a w", h=2 * H, a=2)
                    r4 = rot[t % 2][0:n, :].rearrange("p (h a w) -> p h a w", h=2 * H, a=2)
                    m4 = rtmp[0:n, :].rearrange("p (h a w) -> p h a w", h=2 * H, a=2)
                    cos = C("cos", n).rearrange("p (t w) -> p t w", t=NT)[:, t, :]
                    sin = C("sin", n).rearrange("p (t a w) -> p t a w", t=NT, a=2)
                    cosb = cos.unsqueeze(1).broadcast_to([n, 2 * H, RDK // 2])
                    if t:
                        pool.wait_ge(sem("rot"), t)
                    for a_ in range(2):
                        G.tensor_tensor(r4[:, :, a_, :], x4[:, :, a_, :], cosb, ALU.mult).then_inc(sem("rot_part"), 1)
                        G.tensor_tensor(m4[:, :, a_, :], x4[:, :, 1 - a_, :],
                                        sin[:, t, a_, :].unsqueeze(1).broadcast_to([n, 2 * H, RDK // 2]), ALU.mult)\
                            .then_inc(sem("rot_part"), 1)
                    pool.wait_ge(sem("rot_part"), 4 * (t + 1))
                    G.tensor_tensor(rot[t % 2][0:n, :], rot[t % 2][0:n, :], rtmp[0:n, :], ALU.add).then_inc(sem("rot"), 1)
                    pool.wait_ge(sem("rot"), t + 1)
                    if t >= 2:
                        mm_wait(pool, ("rU", t - 2))
                    G.tensor_tensor(kdec_r[t % 2][0:n], rot[t % 2][0:n, H * RDK:].rearrange("p (h w) -> p h w", h=H),
                                    bc(C("rk", n) if t < 4 else C("rk_s", n), n, H, RDK), ALU.mult).then_inc(sem("rkdec"), 1)
                elif k0 == "rU" and s[1] == 3:
                    ev_wait(pool, s)
                    pool.dma_start(o["ret_prompt"], S_ret[0:RDK]).then_inc(sem("ret_stored"), 16)
                elif k0 == "rUs":
                    h = s[1]
                    ev_wait(pool, ("tmv", 4))
                    if h:
                        mm_wait(pool, ("rUs", h - 1))
                    G.tensor_tensor(vexp[0:64], vt[0][0:64, h * DV:(h + 1) * DV].unsqueeze(1).broadcast_to([64, NB, DV]),
                                    bc(C("row", 64), 64, NB, DV), ALU.mult).then_inc(sem("vexp"), 1)
                    if h == 3:
                        ev_wait(pool, s)
                        pool.dma_start(o["ret_sample"], sr[0:RDK]).then_inc(sem("ret_stored"), 16)
                        pool.wait_ge(sem("ret_stored"), 32)
                        G.memset(idx1[:, :], 0).then_inc(sem("ret_free"), 1)
                elif k0 == "cv" and s[1] == NCONV - 1:
                    pool.wait_ge(sem("cnew"), NCONV)
                    pool.dma_start(o["conv"], cnew).then_inc(sem("cv_stored"), 16)
                elif k0 == "gE":
                    for t in range(NT):
                        n = ntok(t)
                        pool.wait_ge(sem("gexp"), 5 * t + 1)
                        G.tensor_tensor(A[t], A[t], bh(C("low") if t < 4 else C("low_s", 64), n, n), ALU.mult).then_inc(sem("gmask"), 1)
                        pool.wait_ge(sem("gexp"), 5 * t + 2)
                        G.tensor_tensor(D2[t], D2[t], bh(tri(t), n, n), ALU.mult).then_inc(sem("gmask"), 1)
                elif k0 == "l1":
                    t, n = s[1], ntok(s[1])
                    ev_wait(pool, ("gK", t))
                    pool.wait_ge(sem("gx"), 1)
                    G.tensor_tensor(X[t], A[t], bh(C("lev1t", n)[:, 0:n], n, n), ALU.mult).then_inc(sem("l1m"), 1)
                    pool.wait_ge(sem("l1m"), t + 1)
                    G.tensor_tensor(X[t], bh(C("ident", n)[:, 0:n], n, n), X[t], ALU.subtract).then_inc(sem("l1X"), 1)
                elif k0 == "lA":
                    _, v, t = s
                    n = ntok(t)
                    q = plan.order[s]
                    if v == 2:
                        ev_wait(pool, ("gA", t))
                    if q > 2:
                        prev = [x for x in STEPS if x[0] == "lA"][q - 3]
                        mm_wait(pool, ("lY",) + prev[1:])
                    G.tensor_tensor(hb(MSK[q % 2], t), AT[t], bh(C(f"lev{v}", n)[:, 0:n], n, n), ALU.mult).then_inc(sem("lA"), 1)
                elif k0 == "gq":
                    t, n = s[1], ntok(s[1])
                    pool.wait_ge(sem("gx"), 1)
                    G.tensor_tensor(E[t], E[t], cs[:, 0:H, t * P:t * P + n], ALU.mult).then_inc(sem("qe"), 1)
                elif k0 == "sU" and s[1] == 3:
                    ev_wait(pool, s)
                    pool.dma_start(o["dn_prompt"], S_dn).then_inc(sem("dp_stored"), 16)
                elif k0 == "sUs":
                    h = s[1]
                    ev_wait(pool, ("sT",))
                    mm_wait(pool, ("sUs", h - 1) if h else ("sU", 3))
                    G.tensor_tensor(dexp, dlt[4][:, h, :].unsqueeze(1).broadcast_to([64, NB, DV]),
                                    bc(C("row", 64), 64, NB, DV), ALU.mult).then_inc(sem("dexp"), 1)
                    mm_wait(pool, ("sO", 4))
                    G.tensor_tensor(sdn[:, :, h, :], sdn[:, :, h, :], bc(glast_s[:, h, :], P, NB, DV), ALU.mult).then_inc(sem("sdec"), 1)
                    if h == 3:
                        ev_wait(pool, s)
                        pool.dma_start(o["dn_sample"], sdn).then_inc(sem("sd_stored"), 16)
                        pool.wait_ge(sem("dp_stored"), 16)
                elif k0 == "up" and s[1] == 15:
                    mm_wait(pool, s)
                    pool.dma_start(h2[:, 0:4, :], a["x_main"]).then_inc(sem("ld_h"), 16)
                    pool.dma_start(h2[0:64, 4, :], a["x_tail"]).then_inc(sem("ld_h"), 16)
                    pool.dma_start(pT, a["pT"]).then_inc(sem("ld_p"), 16)
                elif k0 == "u2":
                    t, n = s[1], ntok(s[1])
                    pool.wait_ge(sem("u2n"), t + 1)
                    pool.dma_start(u_rows[t * P:t * P + n, :], u2n[t % 2][0:n, :]).then_inc(sem(f"u_rows{t % 2}"), 16)
                elif k0 == "rank":
                    pool.wait_ge(sem("ov_ready"), 1)
                    pool.wait_ge(sem("tok_zero"), 16)
                    pool.wait_ge(sem("ld_small"), 80)
                    for t in range(NT):
                        n = ntok(t)
                        for j in range(2):
                            pool.indirect_dma_start(slot_token, bass.IndirectOffsetOnAxis(ap=placeu[0:n, j, t:t + 1], axis=0),
                                                    tokid[0:n, t:t + 1], None).then_inc(sem("scattered"), 16)
                    pool.wait_ge(sem("scattered"), 16 * 2 * NT)
                    pool.dma_start(ids[:, :], slot_token.rearrange("(p b) o -> p (b o)", p=P)).then_inc(sem("ids"), 16)
                    pool.wait_ge(sem("ids"), 16)
                    pool.wait_ge(sem("u_rows0"), 48)
                    pool.wait_ge(sem("u_rows1"), 32)
                    mm_wait(pool, ("x2", 4, 1))

            def gather(e, col):
                pool.indirect_dma_start(xg[e % 2], None, u_rows, bass.IndirectOffsetOnAxis(ap=col, axis=0)).then_inc(sem(f"xg{e % 2}"), 16)

            for e in range(NEXP):
                if e >= 2:
                    pool.wait_ge(sem("xT_mm"), e - 1)
                gather(e, ids[:, e:e + 1])
            n_ov = pool.value_load(ovi[0:1, NOV:NOV + 1], min_val=0, max_val=NOV)
            pool.wait_ge(sem("xT_mm"), 16)
            with pool.If(n_ov > 0):
                with pool.Fori(0, n_ov) as i:
                    pool.wait_ge(sem("ov_free"), i + 1)
                    pool.sem_inc(sem("ov_pool"), 1)
                    G.tensor_copy(idx1[:, :], ids[:, bass.ds(i + NEXP, 1)]).then_inc(sem("ov_idx"), 1)
                    pool.wait_ge(sem("ov_idx"), i + 1)
                    pool.sem_inc(sem("ov_pool"), 1)
                    pool.indirect_dma_start(xg[0], None, u_rows, bass.IndirectOffsetOnAxis(ap=idx1[:, :], axis=0)).then_inc(sem("ov_xg"), 16)
            pool.wait_ge(sem("y_all"), 1)
            pool.wait_ge(sem("y_zero"), 16 * NOV)
            for t in range(NT):
                n = ntok(t)
                if t >= 2:
                    pool.wait_ge(sem("h3"), t - 1)
                for j in range(2):
                    pool.indirect_dma_start(ga[t % 2][j][0:n, :], None, y_slots,
                                            bass.IndirectOffsetOnAxis(ap=posu[0:n, j, t:t + 1], axis=0)).then_inc(sem(f"ga{j}{t % 2}"), 16)
            pool.wait_ge(sem("cv_stored"), 16)


def tiles(w, cols):
    k, n = w.shape
    return [np.ascontiguousarray(w[:, c:c + cols].reshape(k // P, P, cols).transpose(1, 0, 2)).reshape(P, -1)
            for c in range(0, n, cols)]


def kernel(x_prompt, x_sample, p_prompt, p_sample, state_ret, state_dn, state_conv, norm_mix, w_in, conv_w, dn_a_log,
           dn_dt_bias, dn_norm, w_ret_up, w_dn_up, w_out, norm_ffn, w_router_group, b_router_group, w_router_expert,
           b_router_expert, w_gate_up, w_down, norm_ple, w_ple_gate, w_ple_proj, norm_final):
    import concourse.bacc as bacc
    from concourse.bass_utils import run_bass_kernel_spmd as run

    A_ = np.asarray
    ch = lambda v: A_(v).reshape(-1, P).T
    rep = lambda v: np.broadcast_to(A_(v)[None, :], (P, A_(v).shape[0]))
    x = np.concatenate([A_(x_prompt).reshape(LP, D), A_(x_sample).reshape(NB * LS, D)])
    pe_ = np.concatenate([A_(p_prompt).reshape(LP, 2 * P), A_(p_sample).reshape(NB * LS, 2 * P)])
    a = {"const": np.concatenate(list(constant_tables().values()), 1)}
    a["xT"] = x.T.reshape(KD, P, TOK).transpose(1, 0, 2)
    a["x_main"] = x[:LP].reshape(4, P, D).transpose(1, 0, 2)
    a["x_tail"] = x[LP:]
    a["pT"] = pe_.T.reshape(2, P, TOK).transpose(1, 0, 2)
    a["vec"] = np.concatenate([ch(norm_mix[0]), ch(norm_ffn[0]), ch(norm_ple[0]),
                               A_(conv_w[0]).reshape(CW, NCONV, P).transpose(2, 1, 0).reshape(P, -1),
                               rep(dn_a_log[0]), rep(dn_dt_bias[0]), A_(dn_norm[0])[:, None],
                               rep(b_router_group[0]), rep(b_router_expert[0])], 1)
    w = A_(w_in[0])
    qk, v, rg, dqkv, dz, ab, gates = (w[:, lo:hi] for lo, hi in ((0, 512), (512, 1024), (1024, 1536), (1536, 3072),
                                                                (3072, 3584), (3584, 3592), (3592, 5640)))
    for name, part in (("qk", qk), ("v", v), ("rg", rg), ("dq", dqkv[:, 0:512]), ("dk", dqkv[:, 512:1024]),
                       ("dv", dqkv[:, 1024:]), ("dz", dz), ("ga0", gates[:, 0:512]), ("ga1", gates[:, 512:1024]),
                       ("gb0", gates[:, 1024:1536]), ("gb1", gates[:, 1536:])):
        a["w_" + name] = tiles(part, 512)[0]
    a["w_upr"] = tiles(A_(w_ret_up[0]), D)[0]
    a["w_upd"] = tiles(A_(w_dn_up[0]), D)[0]
    a["w_wo0"], a["w_wo1"] = tiles(A_(w_out[0]), 512)
    a["w_proj"] = tiles(A_(w_ple_proj[0]), D)[0]
    a["w_pg0"], a["w_pg1"] = tiles(A_(w_ple_gate[0]), 512)
    a["w_ab"] = ab.reshape(KD, P, 8).transpose(1, 0, 2)
    a["w_rt"] = np.concatenate([A_(w_router_group[0]), A_(w_router_expert[0])], 1).reshape(KD, P, 20).transpose(1, 0, 2)
    a["w_gu"] = A_(w_gate_up[0]).reshape(NEXP, KD, P, 2 * DE).transpose(0, 2, 1, 3).reshape(NEXP * P, CHUNK_W)
    a["w_down"] = A_(w_down[0]).reshape(NEXP, 2, P, D).transpose(0, 2, 1, 3).reshape(NEXP * P, 2 * D)
    a["state_ret"] = A_(state_ret[0]).transpose(2, 0, 1, 3)
    a["state_dn"] = A_(state_dn[0]).transpose(2, 0, 1, 3)
    a["state_conv"] = A_(state_conv[0]).reshape(NB, CW - 1, NCONV, P).transpose(3, 2, 0, 1)
    a["norm_final"] = rep(norm_final)
    a["tokid"] = (np.arange(P)[:, None] + P * np.arange(NT)[None, :]).astype(np.uint32)
    a["zeros"] = np.zeros((P, D), np.float32)
    a = {k: np.ascontiguousarray(v_) for k, v_ in a.items()}

    nc = bacc.Bacc("TRN2", target_bir_lowering=False, num_devices=1)
    ins = {k: nc.dram_tensor("in_" + k, v_.shape, mybir.dt.from_np(v_.dtype), kind="ExternalInput").ap() for k, v_ in a.items()}
    shapes = {"y": (TOK, D), "ret_prompt": (RDK, H, DV), "ret_sample": (RDK, NB, H, DV), "dn_prompt": (DK, H, DV),
              "dn_sample": (DK, NB, H, DV), "conv": (P, NCONV, 27)}
    outs = {k: nc.dram_tensor("out_" + k, sh, F32, kind="ExternalOutput").ap() for k, sh in shapes.items()}
    build(nc, ins, outs)
    r = run(nc, [{"in_" + k: v_ for k, v_ in a.items()}], core_ids=[0]).results[0]
    y = r["out_y"]
    conv = r["out_conv"].reshape(P, NCONV, 1 + NB, CW - 1).transpose(2, 3, 1, 0).reshape(1 + NB, CW - 1, NCONV * P)
    return (y[:LP].reshape(1, LP, D), y[LP:].reshape(NB, LS, D),
            r["out_ret_prompt"].transpose(1, 0, 2)[None, None], r["out_dn_prompt"].transpose(1, 0, 2)[None, None],
            conv[None, :1], r["out_ret_sample"].transpose(1, 2, 0, 3)[None], r["out_dn_sample"].transpose(1, 2, 0, 3)[None],
            conv[None, 1:])
```

```python
from contextlib import ExitStack

import numpy as np

import concourse.bass as bass
from concourse import mybir

F32 = mybir.dt.float32
U32 = mybir.dt.uint32
ALU = mybir.AluOpType
ACT = mybir.ActivationFunctionType
AX = mybir.AxisListType

P = 128
D = 1024
KD = D // P
LP, NB, LS = 512, 8, 8
TOK = LP + NB * LS
NT = 5
HALF = TOK // 2
H = 4
RDK, DK, DV = 64, 128, 128
CW = 4
NCONV = 12
NG, NE_G, NEXP, DE = 4, 4, 16, 256
NOV = 8
SLOTS = (NEXP + NOV) * P
PAST = 4096
EPS = 1e-6
CHUNK_W = 4096
RING = 3
GAMMA = [1.0 - 2.0 ** (-5.0 - h) for h in range(H)]
LEVELS = [2, 4, 8, 16, 32, 64]
BIG = 3.0e38


def ntok(t):
    return P if t < 4 else NB * LS


def levels(t):
    return LEVELS if t < 4 else [2, 4]


def constant_tables():
    f = np.float32
    p = np.arange(P)
    c = {}
    c["ident"] = np.eye(P, dtype=f)
    c["ones"] = np.ones((P, P), f)
    c["eps"] = np.full((P, 1), EPS, f)
    c["tri"] = (p[:, None] <= p[None, :]).astype(f)
    same = (p[:64, None] // LS) == (p[None, :64] // LS)
    pad = lambda a: np.concatenate([a, np.zeros((P - a.shape[0],) + a.shape[1:], a.dtype)]).astype(f)
    c["tri_s"] = pad(same & (p[:64, None] <= p[None, :64]))
    c["blk_s"] = pad(same)
    c["low"] = (p[:, None] > p[None, :]).astype(f)
    c["low_s"] = pad(same & (p[:64, None] > p[None, :64]))
    c["before"] = (p[:, None] < p[None, :]).astype(f)
    for s in [1] + LEVELS:
        m = (p[:, None] // (2 * s) == p[None, :] // (2 * s)) & ((p[:, None] // s) % 2 == 0) & ((p[None, :] // s) % 2 == 1)
        c[f"lev{s}"] = m.astype(f)
    c["lev1t"] = c["lev1"].T.copy()
    g = np.array(GAMMA, np.float64)
    i = p[None, None, :] - p[:, None, None]
    c["rdec"] = np.where(i >= 0, g[None, :, None] ** np.maximum(i, 0), 0.0).astype(f).reshape(P, -1)
    c["rdec_s"] = pad(np.where(same[:, None, :], c["rdec"].reshape(P, H, P)[:64, :, :64], 0.0).reshape(64, -1))
    c["rq"] = np.broadcast_to(0.125 * g[None, :, None] ** (p[None, None, :] + 1), (P, H, P)).astype(f).reshape(P, -1)
    c["rq_s"] = np.broadcast_to(0.125 * g[None, :, None] ** (p[None, None, :64] % LS + 1), (P, H, 64)).astype(f).reshape(P, -1)
    c["rk"] = (g[None, :] ** (P - 1 - p[:, None])).astype(f)
    c["rk_s"] = pad(g[None, :] ** (LS - 1 - p[:64, None] % LS))
    c["rstep"] = np.broadcast_to((g ** P)[None, :], (P, H)).astype(f)
    half = RDK // 2
    inv = (f(1.0) / (f(10000.0) ** (np.arange(half, dtype=f) / f(half)))).astype(f)
    pos = np.zeros((NT, P), f)
    for t in range(4):
        pos[t] = t * P + p
    pos[4, :64] = PAST + p[:64] % LS
    ang = (pos[:, :, None] * inv).astype(f).astype(np.float64)
    cos, sin = np.cos(ang), np.sin(ang)
    c["cos"] = cos.transpose(1, 0, 2).astype(f).reshape(P, -1)
    c["sin"] = np.stack([-sin, sin], 2).transpose(1, 0, 2, 3).astype(f).reshape(P, -1)
    c["row"] = pad((p[:64, None] // LS) == np.arange(NB)[None, :])
    c["first"] = np.broadcast_to(np.array([4, 3, 2, 1], f), (P, 4)).copy()
    valid = np.ones((P, NT), f)
    valid[64:, 4] = 0
    c["valid"] = valid
    c["slot0"] = np.broadcast_to(P * np.arange(NEXP, dtype=f), (P, NEXP)).copy()
    c["ovbase"] = np.broadcast_to(P * (NEXP - 1 - np.arange(NEXP, dtype=f)), (P, NEXP)).copy()
    c["token"] = (p[:, None] + P * np.arange(NT)[None, :]).astype(f)
    return c


def const_layout():
    at, off = {}, 0
    for k, v in constant_tables().items():
        at[k] = (off, v.shape[1])
        off += v.shape[1]
    return at, off


CHUNKS = ["qk", "v", "dq", "dk", "dv", "rg", "dz", "ga0", "ga1", "upr", "gb0", "gb1", "upd", "wo0", "wo1", "proj"]


def schedule():
    s = [("ss",)]
    for t in range(NT):
        s += [("tmq", t)]
        if t: s += [("rS", t - 1)]
        s += [("tmv", t)]
        if t: s += [("rO", t - 1)]
        s += [("rTq", t), ("rTk", t)]
        if t: s += [("rU", t - 1)]
    s += [("cv", 0), ("rS", 4), ("ab",), ("cv", 1), ("cvs", 0), ("abT",), ("rO", 4)]
    norm = lambda kind, m: [(kind, m), ("nf", kind, m)]
    between = {2: [("nq", "rN", 0)], 3: norm("rN", 0) + [("nq", "rN", 1)],
               4: norm("rN", 1) + [("nq", "rN", 2)], 5: norm("rN", 2) + [("nq", "rN", 3)],
               6: norm("rN", 3) + [("nq", "qn", 0)], 7: norm("qn", 0) + [("nq", "qn", 1)],
               8: norm("qn", 1) + [x for t in range(NT) for x in (("gG", t), ("gC", t))] + [("gE",), ("nq", "qn", 2)],
               9: norm("qn", 2) + [("nq", "qn", 3)], 10: norm("qn", 3) + [("nq", "qn", 4)],
               11: norm("qn", 4) + [("nq", "qn", 5)]}
    for m in range(2, NCONV):
        s += ([("rUs", m - 2)] if m < 6 else []) + [("cv", m), ("cvs", m - 1)] + between[m]
    s += [("rg", 0), ("cvs", NCONV - 1), ("rgs", 0)] + norm("qn", 5) + [("nq", "qn", 6)]
    s += [("nq", "qn", 7), ("rg", 1), ("rgs", 1)] + norm("qn", 6)
    s += [("qn", 7), ("rg", 2), ("nf", "qn", 7), ("rgs", 2)]
    for t in range(NT):
        s += [("gK", t), ("gQ", t)]
    for t in range(NT):
        s += [("gA", t)]
    s += [("rg", 3), ("rgs", 3)]
    s += [("l1", t) for t in range(NT)]
    for v in LEVELS:
        on = [t for t in range(NT) if v in levels(t)]
        s += [("lA", v, t) for t in on[:2]]
        for n, t in enumerate(on):
            s += [("lY", v, t)]
            if n + 2 < len(on): s += [("lA", v, on[n + 2])]
        for t in on:
            if v != levels(t)[-1]: s += [("lX", v, t)]
            s += [("lT", v, t)]
    s += [("gV", 0), ("gk", 0)]
    for t in range(NT):
        s += [("gV", t + 1), ("gk", t + 1)] if t + 1 < NT else []
        s += [("gW", t), ("gU", t), ("gq", t)]
    s += [("sO", 0), ("sU", 0), ("dz", 0), ("sD", 1), ("sDs",), ("sO", 1), ("sU", 1), ("sT",),
          ("sD", 2), ("sO", 4), ("sO", 2), ("sU", 2), ("dz", 1), ("sD", 3), ("sUs", 0), ("sO", 3), ("sU", 3), ("dz", 2),
          ("sUs", 1), ("dz", 3), ("sUs", 2), ("sUs", 3)]
    for m in range(H):
        s += [("nq", "oN", m), ("gt", m)] + norm("oN", m)
    s += [("gt", m) for m in range(H, 8)] + [("up", m) for m in range(8)]
    s += [("gt", m) for m in range(8, 16)] + [("up", m) for m in range(8, 16)]
    for n in range(2):
        s += [("wo", n, t) for t in range(NT)]
    pps = [("pp", t, n) for t in range(NT) for n in range(2)]
    s += [("u2", t) for t in range(NT)] + pps[:2]
    for t in range(NT):
        s += [("x2", t, n) for n in range(2)]
        if t in (1, 2): s += [pps[1 + t]]
    s += [("rt",), pps[4], ("rtT",)] + pps[5:8] + [("rank",)] + pps[8:] + [("ids",), ("rtE",)]
    return s


PAIR = {"ss", "ab", "rt", "tmq", "tmv", "rUs", "rN", "qn", "oN", "cv", "rg", "dz", "sUs", "gt", "up", "wo", "pp"}
SINGLE = {"abT", "rtT", "ids", "rTq", "rTk", "rS", "rO", "rU", "gG", "gC", "gK", "gQ", "gA", "lY", "lX", "lT", "gV", "gk", "gW", "gU",
          "sD", "sDs", "sO", "sU", "sT", "x2", "rank"}
CHUNK_OF = {"tmq": lambda s: 0, "tmv": lambda s: 1, "cv": lambda s: 2 + s[1] // 4, "rg": lambda s: 5, "dz": lambda s: 6,
            "gt": lambda s: (7, 8, 10, 11)[s[1] // 4], "up": lambda s: (9, 12)[s[1] // 8],
            "wo": lambda s: 13 + s[1], "pp": lambda s: 15}


class Plan:

    def __init__(self):
        self.steps = schedule()
        self.order, self.mm, self.buf, self.before, self.chunk_last, self.norm = {}, {}, {}, {}, {}, {}
        count, nmm, npair, nsingle, last = {}, 0, 0, 0, {}
        for s in self.steps:
            k = s[0]
            count[k] = count.get(k, 0) + 1
            self.order[s] = count[k]
            if k in PAIR or k in SINGLE:
                nmm += 1
                self.mm[s] = nmm
                key = ("pair", npair % 2) if k in PAIR else ("single", nsingle % 4)
                if k in PAIR: npair += 1
                else: nsingle += 1
                self.buf[s] = key[1]
                self.before[s] = last.get(key)
                last[key] = s
            if k in CHUNK_OF:
                self.chunk_last[CHUNK_OF[k](s)] = s
            if k in ("rN", "qn", "oN"):
                self.norm[s] = len(self.norm)
        self.last_use = last
        self.norm_step = {n: s for s, n in self.norm.items()}


def build(nc, a, o):
    plan = Plan()
    CAT, NCONST = const_layout()
    STEPS = plan.steps

    u_rows = nc.dram_tensor("u_rows", (TOK, D), F32, kind="Internal").ap()
    y_slots = nc.dram_tensor("y_slots", (SLOTS, D), F32, kind="Internal").ap()

    with ExitStack() as ctx:
        def sb(name, shape, dt=F32):
            return ctx.enter_context(nc.sbuf_tensor(name, shape, dt))

        sems = {}

        def sem(name):
            if name not in sems:
                sems[name] = ctx.enter_context(nc.semaphore(name))
            return sems[name]

        const = sb("const", [P, NCONST])
        HEAD = 2 * P + 1

        def C(name, n=P):
            off, w = CAT[name]
            return const[0:n, off:off + w]

        vec = sb("vec", [P, 8 * 3 + 48 + 4 + 4 + 1 + 20])
        g_mix, g_ffn, g_ple = (vec[:, 8 * i:8 * i + 8] for i in range(3))
        conv_w = vec[:, 24:72].rearrange("p (m j) -> p m j", m=NCONV)
        a_log, dt_b, dn_gain, rt_bias = vec[:, 72:76], vec[:, 76:80], vec[:, 80:81], vec[:, 81:101]
        w_ab = sb("w_ab", [P, KD, 8])
        w_rt = sb("w_rt", [P, KD, 20])
        ab = sb("ab", [P, NT, 8])
        gl = sb("gl", [P, NT, H])
        beta = sb("beta", [P, NT, H])
        gcum = sb("gcum", [P, NT, 8])
        gx = sb("gx", [P, NT, 8])
        sm = sb("sm", [P, 3, NT, H])
        glast = sb("glast", [P, 4, H])
        glast_s = sb("glast_s", [P, H, NB])

        RINGO, UT, OR, CS, SQ, RR, MISC = 0, 12288, 16896, 19200, 26112, 27264, 28416
        BLK = MISC + 612
        MEM = BLK + 36 * 512
        mem = sb("mem", [P, MEM])

        def view(off, *dims, n=P):
            size = int(np.prod(dims))
            v = mem[0:n, off:off + size]
            if len(dims) == 2:
                v = v.rearrange("p (a b) -> p a b", a=dims[0])
            if len(dims) == 3:
                v = v.rearrange("p (a b c) -> p a b c", a=dims[0], b=dims[1])
            return v

        def slot(i):
            return BLK + 512 * i

        ring = [view(RINGO + CHUNK_W * i, CHUNK_W) for i in range(RING)]
        uT = view(UT, KD, TOK)
        o_ret = view(OR, H, TOK)
        cs = view(CS, NCONV, TOK)
        sq = [view(SQ + TOK * i, TOK) for i in range(2)]
        rr = [view(RR + TOK * i, TOK) for i in range(2)]
        cst = view(MISC, NCONV, NB, CW - 1)
        cnew = view(MISC + 288, NCONV, 27)
        qk = [view(slot(0) + 512 * i, 512) for i in range(2)]
        rot = [view(slot(2) + 512 * i, 512) for i in range(2)]
        rtmp = view(slot(4), 512)
        vt = [view(slot(5) + 512 * i, 512) for i in range(2)]
        qT = [view(slot(7) + 512 * i, H, P) for i in range(2)]
        kT = [view(slot(9) + 512 * i, H, P) for i in range(2)]
        qdT = [view(slot(11) + 512 * i, H, P) for i in range(2)]
        kdec_r = [view(slot(13) + 256 * i, H, RDK) for i in range(2)]
        sT = [view(slot(14) + 512 * i, H, P) for i in range(2)]
        S_ret = view(slot(16), H, DV)
        vexp = view(slot(17), NB, DV)
        sr = view(slot(20), NB, H, DV)
        cbuf = [view(slot(28) + 603 * i, 603) for i in range(2)]
        acc = [view(slot(28) + 1206 + 576 * i, TOK) for i in range(2)]
        def hb(base, t, n=None):
            w = ntok(t)
            return view(base, H, w, n=w if n is None else n)
        Am_ = [(slot(0 + t) if t < 4 else slot(20)) for t in range(NT)]
        D2_ = [(slot(4 + t) if t < 4 else slot(20) + 256) for t in range(NT)]
        E_ = [(slot(8 + t) if t < 4 else slot(21)) for t in range(NT)]
        AT_ = [(slot(12 + t) if t < 4 else slot(21) + 256) for t in range(NT)]
        X_ = [(slot(16 + t) if t < 4 else slot(22)) for t in range(NT)]
        XT_ = [(slot(23 + t) if t < 4 else slot(31)) for t in range(NT)]
        Y_ = [(slot(27 + t) if t < 4 else slot(31) + 256) for t in range(NT)]
        MSK = [slot(32), slot(33)]
        A = [hb(Am_[t], t) for t in range(NT)]
        D2 = [hb(D2_[t], t) for t in range(NT)]
        E = [hb(E_[t], t, P) for t in range(NT)]
        AT = [hb(AT_[t], t) for t in range(NT)]
        X = [hb(X_[t], t) for t in range(NT)]
        Gr = [hb(X_[t], t, P) for t in range(NT)]
        XT = [hb(XT_[t], t) for t in range(NT)]
        Y = [hb(Y_[t], t) for t in range(NT)]
        U_ = [(slot(0 + t) if t < 4 else slot(34)) for t in range(NT)]
        U = [view(U_[t], H, DV, n=ntok(t)) for t in range(NT)]
        nwT = [hb(AT_[t], t, P) for t in range(NT)]
        KD_ = [(slot(16 + t) if t < 4 else slot(35)) for t in range(NT)]
        kdec = [view(KD_[t], H, DK, n=ntok(t)) for t in range(NT)]
        bek = [view(slot(27 + t) if t < 4 else slot(28), H, DK, n=ntok(t)) for t in range(NT)]
        bV = [view(MSK[t % 2], H, DV, n=ntok(t)) for t in range(NT)]
        S_dn = view(SQ, H, DV)
        dlt = [view(MSK[t % 2], H, DV, n=ntok(t)) for t in range(4)] + [view(slot(16), H, DV, n=64)]
        sdn = view(slot(23), NB, H, DV)
        dexp = view(slot(0), NB, DV, n=64)
        dTs = view(slot(22), H, 64)
        o_dn = view(CS + 8 * TOK, H, TOK)
        dzs = view(CS, H, TOK)
        sg = view(slot(0), KD, TOK)
        abT = rr[1][0:8]
        rtT = rr[1][0:20]
        pick = view(CS + 5120, 2, NT, P)
        pickb = view(CS + 6400, 2, NT, NEXP + NOV)
        iota = view(CS + 6640, P)
        mT = view(slot(27), KD, TOK)
        h2 = view(CS, NT, D)
        pp = view(RINGO + 7168, NT, D)
        u2n = [view(off, D) for off in (OR, OR + D, CS + 5120)]
        u2T = view(UT, KD, TOK)
        pT = view(SQ, 2, TOK)
        lg = sb("lg", [P, NT, 20])
        oneh = sb("oneh", [P, 3, NT, 4])
        rt = sb("rt", [P, 8, NT, 4])
        rs = sb("rs", [P, 8, NT])
        e12 = sb("e12", [P, 3, NT + 1, NEXP])
        ecum = view(CS + 6784, NT + 1, NEXP)
        rk = sb("rk", [P, 6, NEXP])
        rx = sb("rx", [P, NT, NEXP])
        ov = sb("ov", [P, 4, NEXP])
        ovm = sb("ovm", [P, NOV, NEXP])
        ovf = sb("ovf", [P, NOV + 1])
        ovi = sb("ovi", [P, NOV + 1], U32)
        posu = sb("posu", [P, 2, NT], U32)
        placeu = sb("placeu", [P, 4, NT], U32)
        placef = sb("placef", [P, 4, NT])
        ids = sb("ids", [P, NEXP + NOV], U32)
        idx1 = sb("idx1", [P, 1], U32)
        wcomb = sb("wcomb", [P, 2, NT])
        ms = sb("ms", [P, 3, NT])
        WB = [BLK + 6144, BLK, BLK + 12288, RINGO]
        w_gu_flat = [view(b, CHUNK_W) for b in WB]
        w_dn_flat = [view(b + 4096, 2 * D) for b in WB]
        w_gu = [view(b, KD, 2 * DE) for b in WB]
        w_dn = [view(b + 4096, 2, D) for b in WB]
        xg = [view(OR + D * i, D) for i in range(2)]
        xT = [view(SQ + D * i, KD, P) for i in range(2)]
        hid = [view(CS + 5120 + DE * i, DE) for i in range(2)]
        hT = [view(CS + 5632 + DE * i, 2, P) for i in range(2)]
        sgt = [view(CS + 6144 + DE * i, DE) for i in range(2)]
        yb = [view(UT + D * i, D) for i in range(2)]
        w_pg = [view(BLK + CHUNK_W * i, KD, 512) for i in range(2)]
        ga = [[view(BLK + 8192 + 2048 * i + D * j, D) for j in range(2)] for i in range(2)]
        yout = [view(BLK + 12288 + D * i, D) for i in range(2)]
        nfin = view(BLK + 14336, D)
        sgp = [view(SQ + D * i, D) for i in range(2)]
        u3n = [view(OR + D * i, D) for i in range(2)]
        u3T = view(UT, KD, TOK)
        junk = view(CS + 5120, D)

        pair = [ctx.enter_context(nc.psum_tensor(f"pair{i}", [P, 2, 512], F32)) for i in range(2)]
        single = [ctx.enter_context(nc.psum_tensor(f"single{i}", [P, 512], F32)) for i in range(4)]

        def split(ap):
            return ap.rearrange("p (a b) -> p a b", a=2)

        def pair576(s):
            return pair[plan.buf[s]][:, :, 0:HALF]

        def heads(s, n, w):
            return single[plan.buf[s]][0:n, 0:H * w].rearrange("p (h w) -> p h w", h=H)

        def tri(t):
            return C("tri") if t < 4 else C("tri_s", 64)

        def bc(ap, n, a_, w):
            return ap.unsqueeze(2).broadcast_to([n, a_, w])

        def bh(ap, n, w):
            return ap.unsqueeze(1).broadcast_to([n, H, w])

        s_mm = sem("mm_done")

        def ev(kind):
            return sem("ev_" + kind)

        def mm_wait(eng, s):
            eng.wait_ge(s_mm, plan.mm[s])

        def ev_wait(eng, s):
            eng.wait_ge(ev(s[0]), plan.order[s])

        block = ctx.enter_context(nc.Block())

        @block.sync
        def _(sp):
            sp.dma_start(const[:, 0:HEAD], a["const"][:, 0:HEAD]).then_inc(sem("ld_head"), 16)
            for k in range(0, KD, 4):
                sp.dma_start(uT[:, k:k + 4, :], a["xT"][:, k:k + 4, :]).then_inc(sem(f"ld_x{k // 4}"), 16)
            for n, name in enumerate(CHUNKS):
                if n == 1:
                    sp.dma_start(const[:, HEAD:], a["const"][:, HEAD:]).then_inc(sem("ld_const"), 16)
                if n == 2:
                    sp.dma_start(sr[0:RDK, :, :, :], a["state_ret"]).then_inc(sem("ld_sr"), 16)
                if n >= RING:
                    mm_wait(sp, plan.chunk_last[n - RING])
                dst = ring[n % RING][:, 0:2 * D] if name == "proj" else ring[n % RING]
                sp.dma_start(dst, a["w_" + name]).then_inc(sem(f"ring{n % RING}"), 16)
            free = {0: ("up", 0), 1: ("up", 15), 2: ("wo", 1, 4), 3: ("pp", 4, 1)}
            for e in range(4):
                mm_wait(sp, free[e])
                if e == 0:
                    sp.wait_ge(sem("sd_stored"), 16)
                if e == 1:
                    sp.wait_ge(sem("mT"), KD)
                sp.dma_start(w_gu_flat[e], a["w_gu"][e * P:(e + 1) * P, :]).then_inc(sem(f"wgu{e}"), 16)
                sp.dma_start(w_dn_flat[e], a["w_down"][e * P:(e + 1) * P, :]).then_inc(sem(f"wgu{e}"), 16)

            def after_expert(e, u, more):
                sp.wait_ge(sem("y_ready"), 2 * e + 2)
                sp.dma_start(y_slots[bass.ds(e * P, P), :], yb[u % 2]).then_inc(sem(f"y_stored{u % 2}"), 16)
                if more:
                    sp.dma_start(w_gu_flat[u], a["w_gu"][bass.ds((e + 4) * P, P), :]).then_inc(sem(f"wgu{u}"), 16)
                    sp.dma_start(w_dn_flat[u], a["w_down"][bass.ds((e + 4) * P, P), :]).then_inc(sem(f"wgu{u}"), 16)

            for e in range(4):
                after_expert(e, e, True)
            with sp.Fori(1, 3) as i:
                for u in range(4):
                    after_expert(4 * i + u, u, True)
            for e in range(12, 16):
                after_expert(e, e % 4, False)
                if e == 13:
                    for n in range(2):
                        sp.dma_start(view(BLK + CHUNK_W * n, CHUNK_W), a[f"w_pg{n}"]).then_inc(sem("w_pg"), 16)
                if e == 14:
                    sp.dma_start(nfin, a["norm_final"]).then_inc(sem("w_pg"), 16)
            sp.wait_ge(sem("ov_ready"), 1)
            n_ov = sp.value_load(ovi[0:1, NOV:NOV + 1], min_val=0, max_val=NOV)
            with sp.If(n_ov > 0):
                with sp.Fori(0, n_ov) as i:
                    sp.wait_ge(sem("ov_free"), i + 1)
                    e = sp.value_load(ovi[0:1, bass.ds(i, 1)], min_val=0, max_val=NEXP - 1)
                    sp.dma_start(w_gu_flat[3], a["w_gu"][bass.ds(e * P, P), :]).then_inc(sem("ov_w"), 16)
                    sp.dma_start(w_dn_flat[3], a["w_down"][bass.ds(e * P, P), :]).then_inc(sem("ov_w"), 16)
                    sp.wait_ge(sem("ov_y"), 2 * i + 2)
                    sp.dma_start(y_slots[bass.ds((i + NEXP) * P, P), :], yb[0]).then_inc(sem("ov_stored"), 16)
                    sp.wait_ge(sem("ov_stored"), 16 * i + 16)
                    sp.sem_inc(sem("ov_free"), 1)
            for b in range(2):
                sp.wait_ge(sem(f"y_stored{b}"), 16 * 8)
            sp.sem_inc(sem("y_all"), 1)
            for t in range(NT):
                sp.wait_ge(sem("y_out"), t + 1)
                sp.dma_start(o["y"][t * P:t * P + ntok(t), :], yout[t % 2][0:ntok(t), :]).then_inc(sem(f"out{t % 2}"), 16)
            sp.wait_ge(sem("out0"), 48)
            sp.wait_ge(sem("out1"), 32)

        @block.tensor
        def _(pe):
            def bank_free(s):
                prev = plan.before[s]
                if prev is not None:
                    ev_wait(pe, prev)

            def chunk(s):
                n = CHUNK_OF[s[0]](s)
                pe.wait_ge(sem(f"ring{n % RING}"), 16 * (n // RING + 1))
                return ring[n % RING]

            def gemm_channels(s, w, rhs, kk, fresh=True):
                pb = pair[plan.buf[s]]
                for k in range(kk):
                    for hf in range(2):
                        last = nc.tensor.matmul(pb[:, hf, 0:HALF], w(k), rhs[:, k, hf * HALF:(hf + 1) * HALF],
                                                start=(k == 0), stop=(k == kk - 1))
                last.then_inc(s_mm, 1)

            pe.wait_ge(sem("ld_head"), 16)
            for s in STEPS:
                k0 = s[0]
                if s not in plan.mm:
                    continue
                bank_free(s)
                if s == ("rS", 0):
                    pe.wait_ge(sem("ld_const"), 16)
                if s == ("tmq", 2):
                    pe.wait_ge(sem("uT"), 2 * KD)
                if k0 == "ss":
                    pb = pair[plan.buf[s]]
                    for k in range(KD):
                        pe.wait_ge(sem("xsq"), k + 1)
                        for hf in range(2):
                            last = nc.tensor.matmul(pb[:, hf, 0:HALF], C("ones"), sq[k % 2][:, hf * HALF:(hf + 1) * HALF],
                                                    start=(k == 0), stop=(k == KD - 1))
                        if k < KD - 1:
                            last.then_inc(sem("xsq_used"), 1)
                    last.then_inc(s_mm, 1)
                elif k0 in ("ab", "rt"):
                    w, rhs, m = (w_ab, uT, 8) if k0 == "ab" else (w_rt, u2T, 20)
                    pe.wait_ge(sem("ld_small"), 16 * 4)
                    if k0 == "rt":
                        ev_wait(pe, ("x2", 4, 1))
                    for k in range(KD):
                        for hf in range(2):
                            last = nc.tensor.matmul(pair[plan.buf[s]][0:m, hf, 0:HALF], w[:, k, :],
                                                    rhs[:, k, hf * HALF:(hf + 1) * HALF], start=(k == 0), stop=(k == KD - 1))
                    last.then_inc(s_mm, 1)
                elif k0 in ("abT", "rtT"):
                    src, m = (abT, 8) if k0 == "abT" else (rtT, 20)
                    ev_wait(pe, ("ab",) if k0 == "abT" else ("rt",))
                    for t in range(NT):
                        last = nc.tensor.transpose(single[plan.buf[s]][0:ntok(t), m * t:m * t + m], src[:, t * P:t * P + ntok(t)],
                                                   C("ident")[0:m, 0:m])
                    last.then_inc(s_mm, 1)
                elif k0 == "ids":
                    pe.wait_ge(sem("pick"), 1)
                    for j in range(2):
                        for t in range(NT):
                            last = nc.tensor.matmul(single[plan.buf[s]][:, 0:NEXP + NOV], pick[0:ntok(t), j, t, :],
                                                    pickb[0:ntok(t), j, t, :], start=(j + t == 0), stop=(j + t == NT))
                    last.then_inc(s_mm, 1)
                elif k0 in ("tmq", "tmv"):
                    t = s[1]
                    w = chunk(s).rearrange("p (k c) -> p k c", k=KD)
                    for k in range(KD):
                        if s == ("tmq", 0):
                            pe.wait_ge(sem("uT"), k + 1)
                        last = nc.tensor.matmul(pair[plan.buf[s]][0:ntok(t), 0, :], uT[:, k, t * P:t * P + ntok(t)],
                                                w[:, k, :], start=(k == 0), stop=(k == KD - 1))
                    last.then_inc(s_mm, 1)
                elif k0 in ("rTq", "rTk"):
                    t, n = s[1], ntok(s[1])
                    pe.wait_ge(sem("rot"), t + 1)
                    base = 0 if k0 == "rTq" else H * RDK
                    out = heads(s, RDK, n)
                    for h in range(H):
                        last = nc.tensor.transpose(out[:, h, :], rot[t % 2][0:n, base + h * RDK:base + (h + 1) * RDK],
                                                   C("ident")[0:n, 0:n])
                    last.then_inc(s_mm, 1)
                elif k0 == "rS":
                    t, n = s[1], ntok(s[1])
                    ev_wait(pe, ("rTq", t))
                    ev_wait(pe, ("rTk", t))
                    out = heads(s, n, n)
                    for h in range(H):
                        last = nc.tensor.matmul(out[:, h, :], kT[t % 2][0:RDK, h, 0:n], qT[t % 2][0:RDK, h, 0:n],
                                                start=True, stop=True)
                    last.then_inc(s_mm, 1)
                elif k0 == "rO":
                    t, n = s[1], ntok(s[1])
                    ev_wait(pe, ("rS", t))
                    ev_wait(pe, ("tmv", t))
                    if 0 < t < 4:
                        ev_wait(pe, ("rU", t - 1))
                    if t == 4:
                        pe.wait_ge(sem("ld_sr"), 16)
                    out = heads(s, P, n)
                    for h in range(H):
                        last = nc.tensor.matmul(out[:, h, :], vt[t % 2][0:n, h * DV:(h + 1) * DV], sT[t % 2][0:n, h, 0:n],
                                                start=True, stop=(t == 0), skip_group_check=(t == 4))
                        if 0 < t < 4:
                            last = nc.tensor.matmul(out[:, h, :], S_ret[0:RDK, h, :], qdT[t % 2][0:RDK, h, 0:n],
                                                    start=False, stop=True)
                        if t == 4:
                            for b in range(NB):
                                last = nc.tensor.matmul(out[:, h, LS * b:LS * b + LS], sr[0:RDK, b, h, :],
                                                        qdT[t % 2][0:RDK, h, LS * b:LS * b + LS],
                                                        start=False, stop=(b == NB - 1), skip_group_check=True)
                    last.then_inc(s_mm, 1)
                elif k0 == "rU":
                    t = s[1]
                    pe.wait_ge(sem("rkdec"), t + 1)
                    ev_wait(pe, ("tmv", t))
                    out = heads(s, RDK, DV)
                    for h in range(H):
                        last = nc.tensor.matmul(out[:, h, :], kdec_r[t % 2][:, h, :], vt[t % 2][:, h * DV:(h + 1) * DV],
                                                start=True, stop=True)
                    last.then_inc(s_mm, 1)
                elif k0 == "rUs":
                    h = s[1]
                    pe.wait_ge(sem("rkdec"), 5)
                    pe.wait_ge(sem("vexp"), h + 1)
                    pb = pair[plan.buf[s]]
                    for hf in range(2):
                        last = nc.tensor.matmul(pb[0:RDK, hf, :], kdec_r[0][0:64, h, :], vexp[0:64, 4 * hf:4 * hf + 4, :],
                                                start=True, stop=True)
                    last.then_inc(s_mm, 1)
                elif k0 in ("rN", "qn", "oN"):
                    q = plan.norm[s]
                    pe.wait_ge(sem("nsq"), q + 1)
                    pb = pair[plan.buf[s]]
                    for hf in range(2):
                        last = nc.tensor.matmul(pb[:, hf, 0:HALF], C("ones"), sq[q % 2][:, hf * HALF:(hf + 1) * HALF],
                                                start=True, stop=True)
                    last.then_inc(s_mm, 1)
                elif k0 in ("cv", "rg", "dz", "gt"):
                    w = chunk(s).rearrange("p (k c) -> p k c", k=KD)
                    m = s[1] % 4
                    gemm_channels(s, lambda k: w[:, k, m * P:(m + 1) * P], uT, KD)
                elif k0 == "up":
                    w = chunk(s).rearrange("p (k c) -> p k c", k=H)
                    m = s[1] % 8
                    if s[1] < 8:
                        pe.wait_ge(sem("o_ret"), H)
                        src = o_ret
                    else:
                        pe.wait_ge(sem("o_dn"), H)
                        src = o_dn
                    gemm_channels(s, lambda k: w[:, k, m * P:(m + 1) * P], src, H)
                elif k0 == "gG":
                    t, n = s[1], ntok(s[1])
                    pe.wait_ge(sem("g_beta"), 1)
                    out = heads(s, P, n)
                    for h in range(H):
                        last = nc.tensor.matmul(out[:, h, :], gl[0:n, t, h:h + 1].broadcast_to([n, P]), tri(t),
                                                start=True, stop=True)
                    last.then_inc(s_mm, 1)
                elif k0 == "gC":
                    t, n = s[1], ntok(s[1])
                    out = single[plan.buf[s]]
                    nc.tensor.matmul(out[0:n, 0:4], tri(t), gl[0:n, t, :], start=True, stop=True)
                    nc.tensor.matmul(out[0:n, 4:8], C("ones") if t < 4 else C("blk_s", 64), gl[0:n, t, :],
                                     start=True, stop=True).then_inc(s_mm, 1)
                elif k0 in ("gK", "gQ"):
                    t, n = s[1], ntok(s[1])
                    pe.wait_ge(sem("nfin"), 4 + 8)
                    out = heads(s, n, n)
                    for h in range(H):
                        kh = cs[:, 4 + h, t * P:t * P + n]
                        last = nc.tensor.matmul(out[:, h, :], kh, kh if k0 == "gK" else cs[:, h, t * P:t * P + n],
                                                start=True, stop=True)
                    last.then_inc(s_mm, 1)
                elif k0 == "gA":
                    t, n = s[1], ntok(s[1])
                    ev_wait(pe, ("gK", t))
                    out = heads(s, n, n)
                    for h in range(H):
                        last = nc.tensor.transpose(out[:, h, :], A[t][:, h, :], C("ident")[0:n, 0:n])
                    last.then_inc(s_mm, 1)
                elif k0 == "lY":
                    _, v, t = s
                    n = ntok(t)
                    pe.wait_ge(sem("lA"), plan.order[("lA", v, t)])
                    if v == 2:
                        pe.wait_ge(sem("l1X"), t + 1)
                    else:
                        ev_wait(pe, ("lX", v // 2, t))
                    out = heads(s, n, n)
                    am = hb(MSK[plan.order[("lA", v, t)] % 2], t)
                    for h in range(H):
                        last = nc.tensor.matmul(out[:, h, :], am[:, h, :], X[t][:, h, :], start=True, stop=True)
                    last.then_inc(s_mm, 1)
                elif k0 in ("lX", "lT"):
                    _, v, t = s
                    n = ntok(t)
                    ev_wait(pe, ("lY", v, t))
                    if v == 2:
                        pe.wait_ge(sem("l1T"), t + 1)
                    else:
                        ev_wait(pe, ("lT", v // 2, t))
                    out = heads(s, n, n)
                    for h in range(H):
                        if k0 == "lX":
                            last = nc.tensor.matmul(out[:, h, :], XT[t][:, h, :], Y[t][:, h, :], start=True, stop=True)
                        else:
                            last = nc.tensor.matmul(out[:, h, :], Y[t][:, h, :], XT[t][:, h, :], start=True, stop=True)
                    last.then_inc(s_mm, 1)
                elif k0 in ("gV", "gk"):
                    t, n = s[1], ntok(s[1])
                    if k0 == "gV":
                        pe.wait_ge(sem("conv"), NCONV)
                    out = single[plan.buf[s]][0:n, :].rearrange("p (h w) -> p h w", h=H)
                    for h in range(H):
                        last = nc.tensor.transpose(out[:, h, :], cs[:, (8 if k0 == "gV" else 4) + h, t * P:t * P + n],
                                                   C("ident"))
                    last.then_inc(s_mm, 1)
                elif k0 == "gW":
                    t, n = s[1], ntok(s[1])
                    ev_wait(pe, ("lT", levels(t)[-1], t))
                    pe.wait_ge(sem("bek"), t + 1)
                    out = heads(s, P, n)
                    for h in range(H):
                        last = nc.tensor.matmul(out[:, h, :], bek[t][:, h, :], XT[t][:, h, :], start=True, stop=True)
                    last.then_inc(s_mm, 1)
                elif k0 == "gU":
                    t, n = s[1], ntok(s[1])
                    ev_wait(pe, ("gV", t))
                    out = single[plan.buf[s]][0:n, :].rearrange("p (h w) -> p h w", h=H)
                    for h in range(H):
                        last = nc.tensor.matmul(out[:, h, :], XT[t][:, h, :], bV[t][:, h, :], start=True, stop=True)
                    last.then_inc(s_mm, 1)
                elif k0 in ("sD", "sDs"):
                    t = s[1] if k0 == "sD" else 4
                    n = ntok(t)
                    ev_wait(pe, ("gW", t))
                    if t < 4:
                        ev_wait(pe, ("sU", t - 1))
                        out = single[plan.buf[s]][0:n, :].rearrange("p (h w) -> p h w", h=H)
                        for h in range(H):
                            last = nc.tensor.matmul(out[:, h, :], nwT[t][:, h, :], S_dn[:, h, :], start=True, stop=True)
                    else:
                        pe.wait_ge(sem("ld_sd"), 16)
                        out = heads(s, P, n)
                        for h in range(H):
                            for b in range(NB):
                                last = nc.tensor.matmul(out[:, h, LS * b:LS * b + LS], sdn[:, b, h, :],
                                                        nwT[t][:, h, LS * b:LS * b + LS], start=True, stop=True)
                    last.then_inc(s_mm, 1)
                elif k0 == "sT":
                    ev_wait(pe, ("sDs",))
                    out = single[plan.buf[s]][0:64, :].rearrange("p (h w) -> p h w", h=H)
                    for h in range(H):
                        last = nc.tensor.transpose(out[:, h, :], dTs[:, h, :], C("ident"))
                    last.then_inc(s_mm, 1)
                elif k0 == "sO":
                    t, n = s[1], ntok(s[1])
                    ev_wait(pe, ("gQ", t))
                    pe.wait_ge(sem("qe"), t + 1)
                    if t == 0:
                        ev_wait(pe, ("gU", 0))
                    elif t < 4:
                        ev_wait(pe, ("sD", t))
                    else:
                        ev_wait(pe, ("sT",))
                    dl = U[0] if t == 0 else dlt[t]
                    out = heads(s, P, n)
                    for h in range(H):
                        last = nc.tensor.matmul(out[:, h, :], dl[:, h, :], D2[t][:, h, :], start=True, stop=(t == 0),
                                                skip_group_check=(t == 4))
                        if 0 < t < 4:
                            last = nc.tensor.matmul(out[:, h, :], S_dn[:, h, :], E[t][:, h, :], start=False, stop=True)
                        if t == 4:
                            for b in range(NB):
                                last = nc.tensor.matmul(out[:, h, LS * b:LS * b + LS], sdn[:, b, h, :],
                                                        E[t][:, h, LS * b:LS * b + LS],
                                                        start=False, stop=(b == NB - 1), skip_group_check=True)
                    last.then_inc(s_mm, 1)
                elif k0 == "sU":
                    t = s[1]
                    ev_wait(pe, ("gk", t))
                    dl = U[0] if t == 0 else dlt[t]
                    out = heads(s, P, P)
                    for h in range(H):
                        last = nc.tensor.matmul(out[:, h, :], kdec[t][:, h, :], dl[:, h, :], start=True, stop=True)
                    last.then_inc(s_mm, 1)
                elif k0 == "sUs":
                    h = s[1]
                    ev_wait(pe, ("gk", 4))
                    pe.wait_ge(sem("dexp"), h + 1)
                    pb = pair[plan.buf[s]]
                    for hf in range(2):
                        last = nc.tensor.matmul(pb[:, hf, :], kdec[4][:, h, :], dexp[:, 4 * hf:4 * hf + 4, :],
                                                start=True, stop=True)
                    last.then_inc(s_mm, 1)
                elif k0 == "wo":
                    _, n, t = s
                    w = chunk(s).rearrange("p (k c) -> p k c", k=KD)
                    ev_wait(pe, ("up", 15))
                    pe.wait_ge(sem("mT"), KD)
                    for k in range(KD):
                        last = nc.tensor.matmul(pair[plan.buf[s]][0:ntok(t), 0, :], mT[:, k, t * P:t * P + ntok(t)],
                                                w[:, k, :], start=(k == 0), stop=(k == KD - 1))
                    last.then_inc(s_mm, 1)
                elif k0 == "x2":
                    _, t, n = s
                    pe.wait_ge(sem("u2n"), t + 1)
                    out = single[plan.buf[s]][:, 0:4 * ntok(t)].rearrange("p (k w) -> p k w", k=4)
                    for k in range(4):
                        last = nc.tensor.transpose(out[:, k, :], u2n[t % 3][0:ntok(t), (4 * n + k) * P:(4 * n + k + 1) * P],
                                                   C("ident")[0:ntok(t), 0:ntok(t)])
                    last.then_inc(s_mm, 1)
                elif k0 == "rank":
                    pe.wait_ge(sem("picked"), 1)
                    out = single[plan.buf[s]][:, 0:(NT + 1) * NEXP]
                    nc.tensor.matmul(out, C("ones"), ecum[:, :, :].rearrange("p t e -> p (t e)"), start=True, stop=False)
                    nc.tensor.matmul(out, C("before"), e12[:, 2:2 + 1, :, :].rearrange("p o t e -> p (o t e)"),
                                     start=False, stop=True).then_inc(s_mm, 1)
                elif k0 == "pp":
                    _, t, n = s
                    w = chunk(s)[:, 0:2 * D].rearrange("p (k c) -> p k c", k=2)
                    pe.wait_ge(sem("ld_p"), 16)
                    for k in range(2):
                        last = nc.tensor.matmul(pair[plan.buf[s]][0:ntok(t), 0, :], pT[:, k, t * P:t * P + ntok(t)],
                                                w[:, k, n * 512:(n + 1) * 512], start=(k == 0), stop=(k == 1))
                    last.then_inc(s_mm, 1)
                else:
                    raise AssertionError(s)

            for key, s in plan.last_use.items():
                ev_wait(pe, s)

            def xpose(n_gather, n_prev, u):
                pe.wait_ge(sem(f"xg{u % 2}"), n_gather)
                if n_prev is not None:
                    pe.wait_ge(sem("xT"), n_prev)
                for k in range(KD):
                    out = single[k // 4][:, (k % 4) * P:(k % 4 + 1) * P]
                    last = nc.tensor.transpose(out, xg[u % 2][:, k * P:(k + 1) * P], C("ident"))
                last.then_inc(sem("xT_mm"), 1)

            def down(e, u, first):
                pe.wait_ge(sem("hT"), e + 1)
                if not first:
                    pe.wait_ge(sem("y_ready"), 2 * e - 2)
                for n in range(2):
                    for k in range(2):
                        last = nc.tensor.matmul(pair[u % 2][:, n, :], hT[u % 2][:, k, :], w_dn[u][:, k, n * 512:(n + 1) * 512],
                                                start=(k == 0), stop=(k == 1))
                last.then_inc(sem("dn_mm"), 1)

            def expert(e, u, nxt, first, xg_next):
                pe.wait_ge(sem("xT"), e + 1)
                pe.wait_ge(sem(f"wgu{u}"), xg_next[1])
                if not (first and u == 0):
                    pe.wait_ge(sem("hid"), e)
                for k in range(KD):
                    last = nc.tensor.matmul(single[3][:, :], xT[u % 2][:, k, :], w_gu[u][:, k, :],
                                            start=(k == 0), stop=(k == KD - 1))
                last.then_inc(sem("gu_mm"), 1)
                if nxt:
                    xpose(xg_next[0], e + 1, u + 1)
                if not (first and u == 0):
                    down(e - 1, (u - 1) % 4, first and u <= 2)
                pe.wait_ge(sem("hid"), e + 1)
                for k in range(2):
                    last = nc.tensor.transpose(single[2][:, k * P:(k + 1) * P], hid[u % 2][:, k * P:(k + 1) * P], C("ident"))
                last.then_inc(sem("hT_mm"), 1)

            xpose(16, None, 0)
            for e in range(4):
                expert(e, e, True, True, (16 * ((e + 1) // 2 + 1), 32))
            with pe.Fori(1, 3) as i:
                for u in range(4):
                    expert(4 * i + u, u, True, False, ((i * 2 + (u + 1) // 2 + 1) * 16, i * 32 + 32))
            for e in range(12, 16):
                expert(e, e % 4, e < 15, False, (16 * ((e + 1) // 2 + 1), 128))
            down(15, 3, False)
            pe.wait_ge(sem("ov_ready"), 1)
            pe.wait_ge(sem("y_ready"), 32)
            n_ov = pe.value_load(ovi[0:1, NOV:NOV + 1], min_val=0, max_val=NOV)
            pe.wait_ge(sem("dn_mm"), 16)
            pe.sem_inc(sem("ov_free"), 1)
            with pe.If(n_ov > 0):
                with pe.Fori(0, n_ov) as i:
                    pe.wait_ge(sem("ov_xg"), 16 * i + 16)
                    for k in range(KD):
                        out = single[k // 4][:, (k % 4) * P:(k % 4 + 1) * P]
                        last = nc.tensor.transpose(out, xg[0][:, k * P:(k + 1) * P], C("ident"))
                    last.then_inc(sem("ov_mm"), 1)
                    pe.wait_ge(sem("ov_xT"), i + 1)
                    pe.wait_ge(sem("ov_w"), 32 * i + 32)
                    for k in range(KD):
                        last = nc.tensor.matmul(single[3][:, :], xT[0][:, k, :], w_gu[3][:, k, :],
                                                start=(k == 0), stop=(k == KD - 1))
                    last.then_inc(sem("ov_gu"), 1)
                    pe.wait_ge(sem("ov_hid"), i + 1)
                    for k in range(2):
                        last = nc.tensor.transpose(single[2][:, k * P:(k + 1) * P], hid[0][:, k * P:(k + 1) * P], C("ident"))
                    last.then_inc(sem("ov_hTm"), 1)
                    pe.wait_ge(sem("ov_hT"), i + 1)
                    for n in range(2):
                        for k in range(2):
                            last = nc.tensor.matmul(pair[0][:, n, :], hT[0][:, k, :], w_dn[3][:, k, n * 512:(n + 1) * 512],
                                                    start=(k == 0), stop=(k == 1))
                    last.then_inc(sem("ov_dn"), 1)

            def u3_transpose(t):
                n = ntok(t)
                pe.wait_ge(sem("u3n"), t + 1)
                if t >= 2:
                    pe.wait_ge(sem("u3T"), 2 * t - 2)
                for k in range(KD):
                    out = single[2 * (t % 2) + k // 4][:, (k % 4) * n:(k % 4 + 1) * n]
                    last = nc.tensor.transpose(out, u3n[t % 2][0:n, k * P:(k + 1) * P], C("ident")[0:n, 0:n])
                last.then_inc(sem("u3_mm"), 1)

            u3_transpose(0)
            for t in range(NT):
                n = ntok(t)
                pe.wait_ge(sem("u3T"), 2 * t + 2)
                pe.wait_ge(sem("w_pg"), 48)
                if t >= 2:
                    pe.wait_ge(sem("sgp"), t - 1)
                for hf in range(2):
                    for k in range(KD):
                        last = nc.tensor.matmul(pair[t % 2][0:n, hf, :], u3T[:, k, t * P:t * P + n], w_pg[hf][:, k, :],
                                                start=(k == 0), stop=(k == KD - 1))
                    if hf == 0 and t + 1 < NT:
                        u3_transpose(t + 1)
                last.then_inc(sem("pg_mm"), 1)

        @block.scalar
        def _(act):
            act.dma_start(vec[:, :], a["vec"]).then_inc(sem("ld_small"), 16)
            act.dma_start(w_ab[:, :, :], a["w_ab"]).then_inc(sem("ld_small"), 16)
            act.dma_start(w_rt[:, :, :], a["w_rt"]).then_inc(sem("ld_small"), 16)
            act.dma_start(cst, a["state_conv"]).then_inc(sem("ld_small"), 16)
            link_n = [0]

            def link(ins):
                link_n[0] += 1
                ins.then_inc(sem("act_link"), 1)
                act.wait_ge(sem("act_link"), link_n[0])

            copy = lambda out, in_, scale=1.0: nc.scalar.activation(out, in_, ACT.Copy, scale=scale)
            act.wait_ge(sem("ld_head"), 16)
            for s in STEPS:
                k0 = s[0]
                if k0 == "ss":
                    mm_wait(act, s)
                    nc.scalar.activation(split(rr[0]), pair576(s), ACT.Sqrt, bias=C("eps"), scale=1.0 / D).then_inc(ev(k0), 1)
                elif k0 == "wo" and s[1] == 1:
                    t, n = s[2], ntok(s[2])
                    ev_wait(act, s)
                    if t:
                        act.wait_ge(sem("ms"), t)
                    nc.scalar.activation(yb[0][0:n, :], h2[0:n, t, :], ACT.Square, accum_out=ms[0:n, 0, t:t + 1]).then_inc(sem("ms"), 1)
                elif k0 == "tmq":
                    t, n = s[1], ntok(s[1])
                    mm_wait(act, s)
                    if t >= 2:
                        act.wait_ge(sem("rot"), t - 1)
                    copy(qk[t % 2][0:n, :], pair[plan.buf[s]][0:n, 0, :]).then_inc(ev(k0), 1)
                elif k0 == "tmv":
                    t, n = s[1], ntok(s[1])
                    mm_wait(act, s)
                    if t >= 2:
                        mm_wait(act, ("rU", t - 2))
                    copy(vt[t % 2][0:n, :], pair[plan.buf[s]][0:n, 0, :]).then_inc(ev(k0), 1)
                elif k0 == "rTk":
                    t, n = s[1], ntok(s[1])
                    mm_wait(act, s)
                    copy(kT[t % 2][0:RDK, :, 0:n], heads(s, RDK, n)).then_inc(ev(k0), 1)
                elif k0 in ("rO", "sO"):
                    t, n = s[1], ntok(s[1])
                    mm_wait(act, s)
                    dst = o_ret if k0 == "rO" else o_dn
                    copy(dst[:, :, t * P:t * P + n], heads(s, P, n)).then_inc(ev(k0), 1)
                elif k0 == "cv":
                    m = s[1]
                    mm_wait(act, s)
                    act.wait_ge(sem("cpad"), 1)
                    if m >= 2:
                        act.wait_ge(sem("cacc"), m - 1)
                        act.wait_ge(sem("cnew"), m - 1)
                    pb = pair[plan.buf[s]]
                    copy(cbuf[m % 2][:, 3:3 + HALF], pb[:, 0, 0:HALF])
                    copy(cbuf[m % 2][:, 3 + HALF:3 + LP], pb[:, 1, 0:LP - HALF])
                    copy(cbuf[m % 2][:, 515:603].rearrange("p (b l) -> p b l", b=NB)[:, :, 3:11],
                         pb[:, 1, LP - HALF:HALF].rearrange("p (b l) -> p b l", b=NB)).then_inc(ev(k0), 1)
                elif k0 == "cvs":
                    m = s[1]
                    act.wait_ge(sem("cacc"), m + 1)
                    nc.scalar.activation(cs[:, m, :], acc[m % 2], ACT.Silu).then_inc(sem("conv"), 1)
                elif k0 in ("rN", "qn", "oN"):
                    q = plan.norm[s]
                    mm_wait(act, s)
                    if q >= 2:
                        act.wait_ge(sem("nfin"), q - 1)
                    nc.scalar.activation(split(rr[q % 2]), pair576(s), ACT.Sqrt, bias=C("eps"),
                                         scale=1.0 if k0 == "qn" else 1.0 / DV).then_inc(ev(k0), 1)
                elif k0 == "rg":
                    m = s[1]
                    mm_wait(act, s)
                    if m:
                        act.wait_ge(sem("o_ret"), m)
                    else:
                        act.wait_ge(sem("conv"), NCONV - 1)
                    nc.scalar.activation(split(acc[0]), pair576(s), ACT.Silu).then_inc(ev(k0), 1)
                elif k0 == "gG":
                    t, n = s[1], ntok(s[1])
                    mm_wait(act, s)
                    act.wait_ge(sem("ret_free"), 1)
                    copy(Gr[t], heads(s, P, n)).then_inc(ev(k0), 1)
                elif k0 == "gE":
                    for t in range(NT):
                        n = ntok(t)
                        act.wait_ge(sem("gdiff"), t + 1)
                        nc.scalar.activation(A[t], A[t], ACT.Exp, scale=-1.0).then_inc(sem("gexp"), 1)
                        nc.scalar.activation(D2[t], D2[t], ACT.Exp).then_inc(sem("gexp"), 1)
                        nc.scalar.activation(E[t], Gr[t], ACT.Exp).then_inc(sem("gexp"), 1)
                        nc.scalar.activation(gx[0:n, t, 0:4], gcum[0:n, t, 0:4], ACT.Exp).then_inc(sem("gexp"), 1)
                        nc.scalar.activation(gx[0:n, t, 4:8], sm[0:n, 2, t, :], ACT.Exp).then_inc(sem("gexp"), 1)
                elif k0 in ("ab", "rt"):
                    mm_wait(act, s)
                    dst, m = (abT, 8) if k0 == "ab" else (rtT, 20)
                    copy(split(dst), pair576(s)[0:m]).then_inc(ev(k0), 1)
                elif k0 == "abT":
                    act.wait_ge(sem("ab_abs"), 1)
                    link(nc.scalar.activation(sm[:, 1, :, :], sm[:, 1, :, :], ACT.Exp, scale=-1.0))
                    nc.scalar.activation(sm[:, 1, :, :], sm[:, 1, :, :], ACT.Ln, bias=C("ones")[:, 0:1])
                    nc.scalar.activation(glast[:, 0, :], a_log, ACT.Exp)
                    nc.scalar.activation(beta[:, :, :], ab[:, :, 4:8], ACT.Sigmoid).then_inc(sem("ab_act"), 1)
                elif k0 == "gA":
                    t, n = s[1], ntok(s[1])
                    mm_wait(act, s)
                    copy(AT[t], heads(s, n, n)).then_inc(ev(k0), 1)
                elif k0 == "lY":
                    _, v, t = s
                    n = ntok(t)
                    mm_wait(act, s)
                    if v == 2 and t == 3:
                        act.wait_ge(sem("o_ret"), H)
                    copy(Y[t], heads(s, n, n)).then_inc(ev(k0), 1)
                elif k0 == "gW":
                    t, n = s[1], ntok(s[1])
                    mm_wait(act, s)
                    copy(nwT[t], heads(s, P, n), -1.0).then_inc(ev(k0), 1)
                elif k0 == "gU":
                    t, n = s[1], ntok(s[1])
                    mm_wait(act, s)
                    copy(U[t], single[plan.buf[s]][0:n, :].rearrange("p (h w) -> p h w", h=H)).then_inc(ev(k0), 1)
                    if t == 4:
                        mm_wait(act, ("gU", 4))
                        act.dma_start(sdn, a["state_dn"]).then_inc(sem("ld_sd"), 16)
                elif k0 == "sDs":
                    mm_wait(act, s)
                    copy(dTs, heads(s, P, 64)).then_inc(ev(k0), 1)
                elif k0 == "dz":
                    m = s[1]
                    mm_wait(act, s)
                    if m == 0:
                        act.wait_ge(sem("qe"), NT)
                    nc.scalar.activation(split(dzs[:, m, :]), pair576(s), ACT.Silu).then_inc(ev(k0), 1)
                elif k0 == "gt":
                    m = s[1]
                    mm_wait(act, s)
                    if m == 0:
                        mm_wait(act, ("sUs", 3))
                        ev_wait(act, ("sD", 3))
                        ev_wait(act, ("sT",))
                    if m >= 8:
                        ev_wait(act, ("up", m - 8))
                    nc.scalar.activation(split(sg[:, m % 8, :]), pair576(s), ACT.Sigmoid).then_inc(ev(k0), 1)
                elif k0 == "u2":
                    t, n = s[1], ntok(s[1])
                    if t == 0:
                        act.wait_ge(sem("ms"), NT)
                        nc.scalar.activation(ms[:, 1, :], ms[:, 0, :], ACT.Sqrt, bias=C("eps"), scale=1.0 / D)\
                            .then_inc(sem("ms_root"), 1)
                elif k0 == "rtE":
                    act.wait_ge(sem("rt_exp"), 1)
                    nc.scalar.activation(rt[:, 1, :, :], rt[:, 0, :, :], ACT.Exp)
                    nc.scalar.activation(rs[:, 1, :], rs[:, 0, :], ACT.Exp).then_inc(sem("rt_act"), 1)
                elif k0 == "pp":
                    _, t, n = s
                    mm_wait(act, s)
                    copy(pp[0:ntok(t), t, n * 512:(n + 1) * 512], pair[plan.buf[s]][0:ntok(t), 0, :]).then_inc(ev(k0), 1)

            def y_evac(b, e_done, stored):
                act.wait_ge(sem("dn_mm"), e_done)
                if stored is not None:
                    act.wait_ge(sem(f"y_stored{b}"), stored)
                copy(yb[b][:, 0:512], pair[b][:, 0, :]).then_inc(sem("y_ready"), 1)
                copy(yb[b][:, 512:D], pair[b][:, 1, :]).then_inc(sem("y_ready"), 1)

            def expert_act(e, u, before):
                act.wait_ge(sem("gu_mm"), e + 1)
                nc.scalar.activation(sgt[u % 2], single[3][:, 0:DE], ACT.Silu).then_inc(sem("silu"), 1)
                if before is not None:
                    y_evac((u - 1) % 2, e, before[0])
                act.wait_ge(sem("hT_mm"), e + 1)
                copy(hT[u % 2], single[2][:, 0:2 * P].rearrange("p (k w) -> p k w", k=2)).then_inc(sem("hT"), 1)

            for e in range(4):
                expert_act(e, e, None if e == 0 else (16 * ((e - 1) // 2) or None,))
            with act.Fori(1, 4) as i:
                for u in range(4):
                    expert_act(4 * i + u, u, (i * 32 + 16 * ((u - 1) // 2),))
            y_evac(1, 16, 16 * 7)
            link(nc.scalar.activation(hT[0][0:1, 0, 0:1], C("eps", 1), ACT.Sqrt))
            act.wait_ge(sem("ov_ready"), 1)
            act.wait_ge(sem("y_stored0"), 128)
            n_ov = act.value_load(ovi[0:1, NOV:NOV + 1], min_val=0, max_val=NOV)
            with act.If(n_ov > 0):
                with act.Fori(0, n_ov) as i:
                    act.wait_ge(sem("ov_gu"), i + 1)
                    nc.scalar.activation(sgt[0], single[3][:, 0:DE], ACT.Silu).then_inc(sem("ov_silu"), 1)
                    act.wait_ge(sem("ov_hTm"), i + 1)
                    copy(hT[0], single[2][:, 0:2 * P].rearrange("p (k w) -> p k w", k=2)).then_inc(sem("ov_hT"), 1)
                    act.wait_ge(sem("ov_dn"), i + 1)
                    copy(yb[0][:, 0:512], pair[0][:, 0, :]).then_inc(sem("ov_y"), 1)
                    copy(yb[0][:, 512:D], pair[0][:, 1, :]).then_inc(sem("ov_y"), 1)
            for t in range(NT):
                n = ntok(t)
                act.wait_ge(sem("h3"), t + 1)
                nc.scalar.activation(junk[0:n, :], h2[0:n, t, :], ACT.Square,
                                     accum_out=ms[0:n, 0, t:t + 1]).then_inc(sem("ms"), 1)
                act.wait_ge(sem("ms"), NT + t + 1)
                nc.scalar.activation(ms[0:n, 1, t:t + 1], ms[0:n, 0, t:t + 1], ACT.Sqrt, bias=C("eps", n),
                                     scale=1.0 / D).then_inc(sem("ms_root"), 1)
            for t in range(NT):
                n = ntok(t)
                act.wait_ge(sem("pg_mm"), t + 1)
                if t >= 2:
                    act.wait_ge(sem("h4"), t - 1)
                nc.scalar.activation(sgp[t % 2][0:n, :].rearrange("p (a b) -> p a b", a=2), pair[t % 2][0:n, :, :],
                                     ACT.Sigmoid).then_inc(sem("sgp"), 1)
                act.wait_ge(sem("h4"), t + 1)
                nc.scalar.activation(junk[0:n, :], h2[0:n, t, :], ACT.Square,
                                     accum_out=ms[0:n, 0, t:t + 1]).then_inc(sem("ms"), 1)
                act.wait_ge(sem("ms"), 2 * NT + t + 1)
                nc.scalar.activation(ms[0:n, 1, t:t + 1], ms[0:n, 0, t:t + 1], ACT.Sqrt, bias=C("eps", n),
                                     scale=1.0 / D).then_inc(sem("ms_root"), 1)

        @block.vector
        def _(dve):
            V = nc.vector
            link_n = [0]

            def link(ins):
                link_n[0] += 1
                ins.then_inc(sem("dve_link"), 1)
                dve.wait_ge(sem("dve_link"), link_n[0])

            V.memset(cbuf[0][:, 0:3], 0.0)
            V.memset(cbuf[1][:, 0:3], 0.0).then_inc(sem("cpad"), 1)
            V.memset(ab[:, :, :], 0.0)
            V.memset(lg[:, :, :], 0.0)
            V.memset(e12[:, 2, NT, :], 0.0)
            link(V.memset(ms[:, :, :], 1.0))
            for s in STEPS:
                k0 = s[0]
                if k0 == "ss":
                    for k in range(KD):
                        dve.wait_ge(sem(f"ld_x{k // 4}"), 16)
                        if k >= 2:
                            dve.wait_ge(sem("xsq_used"), k - 1)
                        V.tensor_tensor(sq[k % 2], uT[:, k, :], uT[:, k, :], ALU.mult).then_inc(sem("xsq"), 1)
                    ev_wait(dve, s)
                    dve.wait_ge(sem("ld_small"), 16 * 4)
                    for hf in range(2):
                        h = slice(hf * HALF, (hf + 1) * HALF)
                        link(V.reciprocal(rr[0][:, h], rr[0][:, h]))
                        for k in range(KD):
                            V.scalar_tensor_tensor(out=uT[:, k, h], in0=uT[:, k, h], scalar=g_mix[:, k:k + 1], in1=rr[0][:, h],
                                                   op0=ALU.mult, op1=ALU.mult).then_inc(sem("uT"), 1)
                    dve.wait_ge(sem("ld_const"), 16)
                elif k0 == "abT":
                    mm_wait(dve, s)
                    src = single[plan.buf[s]]
                    V.tensor_copy(ab[:, 0:4, :], src[:, 0:32].rearrange("p (t c) -> p t c", t=4))
                    V.tensor_copy(ab[0:64, 4, :], src[0:64, 32:40]).then_inc(ev(k0), 1)
                    ev_wait(dve, s)
                    link(V.tensor_tensor(sm[:, 0, :, :], ab[:, :, 0:4], dt_b.unsqueeze(1).broadcast_to([P, NT, H]), ALU.add))
                    link(V.tensor_scalar(sm[:, 1, :, :], sm[:, 0, :, :], -1.0, None, ALU.mult))
                    V.tensor_tensor(sm[:, 1, :, :], sm[:, 1, :, :], sm[:, 0, :, :], ALU.max).then_inc(sem("ab_abs"), 1)
                    dve.wait_ge(sem("ab_act"), 1)
                    link(V.scalar_tensor_tensor(out=sm[:, 0, :, :].rearrange("p t h -> p (t h)"),
                                                in0=sm[:, 0, :, :].rearrange("p t h -> p (t h)"), scalar=0.0,
                                                in1=sm[:, 1, :, :].rearrange("p t h -> p (t h)"), op0=ALU.max, op1=ALU.add))
                    link(V.tensor_tensor(gl[:, :, :], sm[:, 0, :, :], glast[:, 0, :].unsqueeze(1).broadcast_to([P, NT, H]), ALU.mult))
                    V.tensor_scalar(gl[:, :, :], gl[:, :, :], -1.0, None, ALU.mult).then_inc(sem("g_beta"), 1)
                elif k0 == "rTq":
                    t, n = s[1], ntok(s[1])
                    mm_wait(dve, s)
                    V.tensor_scalar(qT[t % 2][0:RDK, :, 0:n], heads(s, RDK, n), 0.125, None, ALU.mult)
                    dec = (C("rq") if t < 4 else C("rq_s")).rearrange("p (h w) -> p h w", h=H)
                    V.tensor_tensor(qdT[t % 2][0:RDK, :, 0:n], heads(s, RDK, n), dec[0:RDK], ALU.mult).then_inc(ev(k0), 1)
                elif k0 == "rS":
                    t, n = s[1], ntok(s[1])
                    mm_wait(dve, s)
                    dec = (C("rdec") if t < 4 else C("rdec_s", 64)).rearrange("p (h w) -> p h w", h=H)
                    V.tensor_tensor(sT[t % 2][0:n, :, 0:n], heads(s, n, n), dec, ALU.mult).then_inc(ev(k0), 1)
                elif k0 == "rU":
                    t = s[1]
                    mm_wait(dve, s)
                    if t == 0:
                        V.tensor_copy(S_ret[0:RDK], heads(s, RDK, DV)).then_inc(ev(k0), 1)
                    else:
                        ev_wait(dve, ("rU", t - 1))
                        mm_wait(dve, ("rO", t))
                        link(V.tensor_tensor(S_ret[0:RDK], S_ret[0:RDK], bc(C("rstep")[0:RDK], RDK, H, DV), ALU.mult))
                        V.tensor_tensor(S_ret[0:RDK], S_ret[0:RDK], heads(s, RDK, DV), ALU.add).then_inc(ev(k0), 1)
                elif k0 == "rUs":
                    h = s[1]
                    mm_wait(dve, s)
                    pb = pair[plan.buf[s]]
                    for hf in range(2):
                        last = V.scalar_tensor_tensor(out=sr[0:RDK, 4 * hf:4 * hf + 4, h, :], in0=sr[0:RDK, 4 * hf:4 * hf + 4, h, :],
                                                      scalar=float(np.float32(GAMMA[h] ** LS)),
                                                      in1=pb[0:RDK, hf, :].rearrange("p (b v) -> p b v", b=4),
                                                      op0=ALU.mult, op1=ALU.add)
                    last.then_inc(ev(k0), 1)
                elif k0 == "cv":
                    m = s[1]
                    if m >= 2:
                        dve.wait_ge(sem("conv"), m - 1)
                    smp = cbuf[m % 2][:, 515:603].rearrange("p (b l) -> p b l", b=NB)
                    V.tensor_copy(smp[:, :, 0:3], cst[:, m, :, :]).then_inc(sem("cpads"), 1)
                    ev_wait(dve, s)
                    dve.wait_ge(sem("cpads"), m + 1)
                    V.tensor_copy(cnew[:, m, 0:3], cbuf[m % 2][:, 512:515])
                    V.tensor_copy(cnew[:, m, 3:27].rearrange("p (b l) -> p b l", b=NB), smp[:, :, 8:11]).then_inc(sem("cnew"), 1)
                    accs = acc[m % 2][:, LP:TOK].rearrange("p (b l) -> p b l", b=NB)
                    V.tensor_scalar(acc[m % 2][:, 0:LP], cbuf[m % 2][:, 0:LP], conv_w[:, m, 0:1], None, ALU.mult)
                    link(V.tensor_scalar(accs, smp[:, :, 0:LS], conv_w[:, m, 0:1], None, ALU.mult))
                    for j in range(1, CW):
                        V.scalar_tensor_tensor(out=acc[m % 2][:, 0:LP], in0=cbuf[m % 2][:, j:j + LP], scalar=conv_w[:, m, j:j + 1],
                                               in1=acc[m % 2][:, 0:LP], op0=ALU.mult, op1=ALU.add)
                        last = V.scalar_tensor_tensor(out=accs, in0=smp[:, :, j:j + LS], scalar=conv_w[:, m, j:j + 1],
                                                      in1=accs, op0=ALU.mult, op1=ALU.add)
                        if j < CW - 1:
                            link(last)
                    last.then_inc(sem("cacc"), 1)
                elif k0 == "nf":
                    _, kind, m = s
                    q = plan.norm[(kind, m)]
                    ev_wait(dve, (kind, m))
                    link(V.reciprocal(rr[q % 2], rr[q % 2]))
                    if kind == "rN":
                        V.tensor_tensor(o_ret[:, m, :], o_ret[:, m, :], rr[q % 2], ALU.mult).then_inc(sem("nfin"), 1)
                    elif kind == "qn":
                        V.scalar_tensor_tensor(out=cs[:, m, :], in0=cs[:, m, :], scalar=DK ** -0.5 if m < H else 1.0,
                                               in1=rr[q % 2], op0=ALU.mult, op1=ALU.mult).then_inc(sem("nfin"), 1)
                    else:
                        V.scalar_tensor_tensor(out=o_dn[:, m, :], in0=o_dn[:, m, :], scalar=dn_gain, in1=rr[q % 2],
                                               op0=ALU.mult, op1=ALU.mult).then_inc(sem("nfin"), 1)
                        dve.wait_ge(sem("nfin"), q + 1)
                        ev_wait(dve, ("dz", m))
                        V.tensor_tensor(o_dn[:, m, :], o_dn[:, m, :], dzs[:, m, :], ALU.mult).then_inc(sem("o_dn"), 1)
                elif k0 == "rgs":
                    m = s[1]
                    ev_wait(dve, ("rg", m))
                    dve.wait_ge(sem("nfin"), m + 1)
                    V.tensor_tensor(o_ret[:, m, :], o_ret[:, m, :], acc[0], ALU.mult).then_inc(sem("o_ret"), 1)
                elif k0 == "gC":
                    t, n = s[1], ntok(s[1])
                    mm_wait(dve, s)
                    V.tensor_copy(gcum[0:n, t, :], single[plan.buf[s]][0:n, 0:8]).then_inc(ev(k0), 1)
                    ev_wait(dve, s)
                    V.tensor_tensor(sm[0:n, 2, t, :], gcum[0:n, t, 4:8], gcum[0:n, t, 0:4], ALU.subtract)
                    ev_wait(dve, ("gG", t))
                    for h in range(H):
                        V.tensor_scalar(A[t][:, h, :], Gr[t][0:n, h, :], gcum[0:n, t, h:h + 1], 0.0, ALU.subtract, ALU.max)
                        last = V.tensor_scalar(D2[t][:, h, :], Gr[t][0:n, h, :], gcum[0:n, t, h:h + 1], 0.0, ALU.subtract, ALU.min)
                    last.then_inc(sem("gdiff"), 1)
                elif k0 == "gE":
                    dve.wait_ge(sem("gexp"), 5 * NT)
                    for t in range(NT):
                        n = ntok(t)
                        if t < 4:
                            V.tensor_copy(glast[:, t, :], E[t][:, :, P - 1])
                        else:
                            V.tensor_copy(glast_s[:, :, :], E[t].rearrange("p h (b l) -> p h b l", b=NB)[:, :, :, LS - 1])
                        last = V.tensor_tensor(gx[0:n, t, 0:4], gx[0:n, t, 0:4], beta[0:n, t, :], ALU.mult)
                    last.then_inc(sem("gx"), 1)
                elif k0 == "gK":
                    t, n = s[1], ntok(s[1])
                    mm_wait(dve, s)
                    dve.wait_ge(sem("gmask"), 2 * t + 1)
                    for h in range(H):
                        last = V.scalar_tensor_tensor(out=A[t][:, h, :], in0=heads(s, n, n)[:, h, :], scalar=beta[0:n, t, h:h + 1],
                                                      in1=A[t][:, h, :], op0=ALU.mult, op1=ALU.mult)
                    last.then_inc(ev(k0), 1)
                elif k0 == "gQ":
                    t, n = s[1], ntok(s[1])
                    mm_wait(dve, s)
                    dve.wait_ge(sem("gmask"), 2 * t + 2)
                    V.tensor_tensor(D2[t], heads(s, n, n), D2[t], ALU.mult).then_inc(ev(k0), 1)
                elif k0 == "l1":
                    t, n = s[1], ntok(s[1])
                    ev_wait(dve, ("gA", t))
                    link(V.tensor_tensor(XT[t], AT[t], bh(C("lev1", n)[:, 0:n], n, n), ALU.mult))
                    V.tensor_tensor(XT[t], bh(C("ident", n)[:, 0:n], n, n), XT[t], ALU.subtract).then_inc(sem("l1T"), 1)
                elif k0 in ("lX", "lT"):
                    _, v, t = s
                    n = ntok(t)
                    mm_wait(dve, s)
                    if k0 == "lX":
                        if v == 2:
                            dve.wait_ge(sem("l1X"), t + 1)
                        dst = X[t]
                    else:
                        dst = XT[t]
                    V.tensor_tensor(dst, dst, heads(s, n, n), ALU.subtract).then_inc(ev(k0), 1)
                elif k0 == "gV":
                    t, n = s[1], ntok(s[1])
                    mm_wait(dve, s)
                    if t >= 2:
                        mm_wait(dve, ("gU", t - 2))
                    V.tensor_tensor(bV[t], single[plan.buf[s]][0:n, :].rearrange("p (h w) -> p h w", h=H),
                                    bc(beta[0:n, t, :], n, H, DV), ALU.mult).then_inc(ev(k0), 1)
                elif k0 == "gk":
                    t, n = s[1], ntok(s[1])
                    mm_wait(dve, s)
                    src = single[plan.buf[s]][0:n, :].rearrange("p (h w) -> p h w", h=H)
                    dve.wait_ge(sem("gx"), 1)
                    V.tensor_tensor(bek[t], src, bc(gx[0:n, t, 0:4], n, H, DK), ALU.mult).then_inc(sem("bek"), 1)
                    V.tensor_tensor(kdec[t], src, bc(gx[0:n, t, 4:8], n, H, DK), ALU.mult).then_inc(ev(k0), 1)
                elif k0 == "sD":
                    t, n = s[1], ntok(s[1])
                    mm_wait(dve, s)
                    ev_wait(dve, ("gU", t))
                    V.tensor_tensor(dlt[t], single[plan.buf[s]][0:n, :].rearrange("p (h w) -> p h w", h=H), U[t],
                                    ALU.add).then_inc(ev(k0), 1)
                elif k0 == "sT":
                    mm_wait(dve, s)
                    ev_wait(dve, ("gU", 4))
                    V.tensor_tensor(dlt[4], single[plan.buf[s]][0:64, :].rearrange("p (h w) -> p h w", h=H), U[4],
                                    ALU.add).then_inc(ev(k0), 1)
                elif k0 == "sU":
                    t = s[1]
                    mm_wait(dve, s)
                    if t == 0:
                        V.tensor_copy(S_dn, heads(s, P, P)).then_inc(ev(k0), 1)
                    else:
                        ev_wait(dve, ("sU", t - 1))
                        for h in range(H):
                            last = V.scalar_tensor_tensor(out=S_dn[:, h, :], in0=S_dn[:, h, :], scalar=glast[:, t, h:h + 1],
                                                          in1=heads(s, P, P)[:, h, :], op0=ALU.mult, op1=ALU.add)
                        last.then_inc(ev(k0), 1)
                elif k0 == "sUs":
                    h = s[1]
                    mm_wait(dve, s)
                    dve.wait_ge(sem("sdec"), h + 1)
                    pb = pair[plan.buf[s]]
                    for hf in range(2):
                        last = V.tensor_tensor(sdn[:, 4 * hf:4 * hf + 4, h, :], sdn[:, 4 * hf:4 * hf + 4, h, :],
                                               pb[:, hf, :].rearrange("p (b v) -> p b v", b=4), ALU.add)
                    last.then_inc(ev(k0), 1)
                elif k0 == "up":
                    m = s[1]
                    mm_wait(dve, s)
                    ev_wait(dve, ("gt", m))
                    if m == 0:
                        dve.wait_ge(sem("sd_stored"), 16)
                    if m < 8:
                        V.tensor_tensor(split(mT[:, m, :]), split(sg[:, m, :]), pair576(s), ALU.mult).then_inc(ev(k0), 1)
                    else:
                        V.tensor_tensor(split(sg[:, m - 8, :]), split(sg[:, m - 8, :]), pair576(s), ALU.mult).then_inc(ev(k0), 1)
                        ev_wait(dve, s)
                        V.tensor_tensor(mT[:, m - 8, :], mT[:, m - 8, :], sg[:, m - 8, :], ALU.add).then_inc(sem("mT"), 1)
                elif k0 == "wo":
                    _, n, t = s
                    mm_wait(dve, s)
                    dve.wait_ge(sem("ld_h"), 16 if t < 4 else 32)
                    V.tensor_tensor(h2[0:ntok(t), t, n * 512:(n + 1) * 512], h2[0:ntok(t), t, n * 512:(n + 1) * 512],
                                    pair[plan.buf[s]][0:ntok(t), 0, :], ALU.add).then_inc(ev(k0), 1)
                elif k0 == "u2":
                    t, n = s[1], ntok(s[1])
                    if t == 0:
                        dve.wait_ge(sem("ms_root"), 1)
                        link(V.reciprocal(ms[:, 2, :], ms[:, 1, :]))
                    if t >= 3:
                        mm_wait(dve, ("x2", t - 3, 1))
                        dve.wait_ge(sem(f"u_rows{t % 3}"), 16)
                    V.tensor_scalar(u2n[t % 3][0:n, :], h2[0:n, t, :], ms[0:n, 2, t:t + 1], None, ALU.mult).then_inc(sem("u2n"), 1)
                    for tt in ([t - 1] if t else []) + ([4] if t == 4 else []):
                        for hf in range(2):
                            st = ("x2", tt, hf)
                            mm_wait(dve, st)
                            V.tensor_tensor(u2T[:, 4 * hf:4 * hf + 4, tt * P:tt * P + ntok(tt)],
                                            single[plan.buf[st]][:, 0:4 * ntok(tt)].rearrange("p (k w) -> p k w", k=4),
                                            bc(g_ffn[:, 4 * hf:4 * hf + 4], P, 4, ntok(tt)), ALU.mult).then_inc(ev("x2"), 1)
                elif k0 == "rtT":
                    link(V.memset(ecum[:, 0, :], 0.0))
                    mm_wait(dve, s)
                    src = single[plan.buf[s]]
                    bias = rt_bias.unsqueeze(1)
                    V.tensor_tensor(lg[:, 0:4, :], src[:, 0:80].rearrange("p (t c) -> p t c", t=4), bias.broadcast_to([P, 4, 20]), ALU.add)
                    V.tensor_tensor(lg[0:64, 4, :], src[0:64, 80:100], rt_bias[0:64, :], ALU.add).then_inc(ev(k0), 1)
                    ev_wait(dve, s)
                    b4 = lambda x: x.unsqueeze(2).broadcast_to([P, NT, 4])

                    def first_max(values, best, diff, hot):
                        link(V.reduce_max(best, values, AX.X))
                        link(V.tensor_tensor(diff, values, b4(best), ALU.subtract))
                        link(V.tensor_scalar(hot, diff, 0.0, None, ALU.is_equal))
                        link(V.tensor_tensor(hot, hot, C("first").unsqueeze(1).broadcast_to([P, NT, 4]), ALU.mult))
                        link(V.reduce_max(rs[:, 6, :], hot, AX.X))
                        link(V.tensor_tensor(hot, hot, b4(rs[:, 6, :]), ALU.is_equal))

                    first_max(lg[:, :, 0:4], rs[:, 2, :], rt[:, 0, :, :], oneh[:, 0])
                    for g in range(NG):
                        dst = rt[:, 2, :, :] if g == 0 else rt[:, 3, :, :]
                        link(V.tensor_tensor(dst, lg[:, :, 4 + 4 * g:8 + 4 * g], b4(oneh[:, 0, :, g]), ALU.mult))
                        if g:
                            link(V.tensor_tensor(rt[:, 2, :, :], rt[:, 2, :, :], rt[:, 3, :, :], ALU.add))
                    first_max(rt[:, 2], rs[:, 3, :], rt[:, 3], oneh[:, 1])
                    link(V.tensor_scalar(rt[:, 4], oneh[:, 1], -BIG, None, ALU.mult))
                    link(V.tensor_tensor(rt[:, 4], rt[:, 4], rt[:, 2], ALU.add))
                    first_max(rt[:, 4], rs[:, 4, :], rt[:, 3], oneh[:, 2])
                    V.tensor_tensor(rs[:, 0, :], rs[:, 4, :], rs[:, 3, :], ALU.subtract).then_inc(sem("rt_exp"), 1)
                    link(V.tensor_tensor(oneh[:, 0], oneh[:, 0], b4(C("valid")), ALU.mult))
                    for j in range(2):
                        for g in range(NG):
                            last = V.tensor_tensor(e12[:, j, 0:NT, 4 * g:4 * g + 4], oneh[:, 1 + j], b4(oneh[:, 0, :, g]), ALU.mult)
                    link(last)
                    link(V.tensor_tensor(e12[:, 2, 0:NT], e12[:, 0, 0:NT], e12[:, 1, 0:NT], ALU.add))
                    for t in range(NT):
                        last = V.tensor_tensor(ecum[:, t + 1, :], ecum[:, t, :], e12[:, 2, t, :], ALU.add)
                        if t < NT - 1:
                            link(last)
                    last.then_inc(sem("picked"), 1)
                elif k0 == "rtE":
                    dve.wait_ge(sem("rt_act"), 1)
                    link(V.reduce_sum(rs[:, 2, :], rt[:, 1], AX.X))
                    link(V.tensor_scalar(rs[:, 3, :], rs[:, 1, :], 1.0, None, ALU.add))
                    link(V.tensor_tensor(rs[:, 2, :], rs[:, 2, :], rs[:, 3, :], ALU.mult))
                    link(V.reciprocal(wcomb[:, 0, :], rs[:, 2, :]))
                    link(V.tensor_tensor(wcomb[:, 1, :], wcomb[:, 0, :], rs[:, 1, :], ALU.mult))
                elif k0 == "rank":
                    mm_wait(dve, s)
                    V.tensor_copy(rk[:, :, :], single[plan.buf[s]][:, 0:96].rearrange("p (t e) -> p t e", t=6)).then_inc(ev(k0), 1)
                    ev_wait(dve, s)
                    cnt = rk[:, 5, :]
                    link(V.tensor_scalar(ov[:, 0, :], cnt, 128.0, None, ALU.is_gt))
                    for k in (256.0, 384.0, 512.0):
                        link(V.tensor_scalar(ov[:, 1, :], cnt, k, None, ALU.is_gt))
                        link(V.tensor_tensor(ov[:, 0, :], ov[:, 0, :], ov[:, 1, :], ALU.add))
                    link(V.tensor_tensor_scan(ov[:, 1, :], C("ones")[:, 0:NEXP], ov[:, 0, :], 0.0, ALU.mult, ALU.add))
                    link(V.tensor_tensor(ov[:, 2, :], ov[:, 1, :], ov[:, 0, :], ALU.subtract))
                    link(V.scalar_tensor_tensor(out=ov[:, 3, :], in0=ov[:, 2, :], scalar=float(P), in1=C("ovbase"), op0=ALU.mult, op1=ALU.add))
                    link(V.tensor_scalar(rx[:, :, :], rk[:, 0:5, :], 128.0, None, ALU.is_ge))
                    link(V.tensor_tensor(rx[:, :, :], rx[:, :, :], ov[:, 3, :].unsqueeze(1).broadcast_to([P, NT, NEXP]), ALU.mult))
                    link(V.tensor_tensor(rx[:, :, :], rx[:, :, :], rk[:, 0:5, :], ALU.add))
                    link(V.tensor_tensor(rx[:, :, :], rx[:, :, :], C("slot0").unsqueeze(1).broadcast_to([P, NT, NEXP]), ALU.add))
                    for j in range(2):
                        link(V.tensor_tensor(e12[:, j, 0:NT], e12[:, j, 0:NT], rx[:, :, :], ALU.mult))
                        link(V.reduce_sum(rs[:, 5, :], e12[:, j, 0:NT], AX.X))
                        link(V.tensor_copy(posu[:, j, :], rs[:, 5, :]))
                    link(V.tensor_scalar(placeu[:, 0:2], posu[:, :, :], P - 1, None, ALU.bitwise_and))
                    link(V.tensor_scalar(placeu[:, 2:4], posu[:, :, :], 7, None, ALU.logical_shift_right))
                    link(V.tensor_copy(placef[:, :, :], placeu[:, :, :]))
                    dve.wait_ge(sem("ld_iota"), 16)
                    dve.wait_ge(sem("u_rows2"), 16)
                    row = placef[:, 0:2, :].rearrange("p j t -> p (j t)").unsqueeze(2).broadcast_to([P, 2 * NT, P])
                    blk = placef[:, 2:4, :].rearrange("p j t -> p (j t)").unsqueeze(2).broadcast_to([P, 2 * NT, NEXP + NOV])
                    V.tensor_tensor(pick.rearrange("p j t r -> p (j t) r"), iota.unsqueeze(1).broadcast_to([P, 2 * NT, P]), row,
                                    ALU.is_equal)
                    link(V.tensor_tensor(pickb.rearrange("p j t r -> p (j t) r"),
                                         iota[:, 0:NEXP + NOV].unsqueeze(1).broadcast_to([P, 2 * NT, NEXP + NOV]), blk, ALU.is_equal))
                    for j in range(2):
                        last = V.tensor_tensor(pickb[:, j], pickb[:, j], C("token").unsqueeze(2).broadcast_to([P, NT, NEXP + NOV]),
                                               ALU.mult)
                    last.then_inc(sem("pick"), 1)
                    link(V.tensor_tensor(ovm[:, :, :], ov[:, 1, :].unsqueeze(1).broadcast_to([P, NOV, NEXP]),
                                         iota[:, 0:NOV].unsqueeze(2).broadcast_to([P, NOV, NEXP]), ALU.is_le))
                    link(V.reduce_sum(ovf[:, 0:NOV], ovm[:, :, :], AX.X))
                    link(V.tensor_scalar(ovf[:, 0:NOV], ovf[:, 0:NOV], float(NEXP - 1), None, ALU.min))
                    link(V.tensor_copy(ovf[:, NOV:NOV + 1], ov[:, 1, NEXP - 1:NEXP]))
                    V.tensor_copy(ovi[:, :], ovf[:, :]).then_inc(sem("ov_ready"), 1)
                elif k0 == "ids":
                    mm_wait(dve, s)
                    V.tensor_copy(ids[:, :], single[plan.buf[s]][:, 0:NEXP + NOV]).then_inc(ev(k0), 1)

            def expert_dve(e, u, first):
                dve.wait_ge(sem("gu_mm"), e + 1)
                dve.wait_ge(sem("silu"), e + 1)
                if not (first and u < 2):
                    dve.wait_ge(sem("hT_mm"), e - 1)
                V.tensor_tensor(hid[u % 2], sgt[u % 2], single[3][:, DE:2 * DE], ALU.mult).then_inc(sem("hid"), 1)

            def x_evac(u, count, into, done):
                dve.wait_ge(sem("xT_mm"), count)
                for hf in range(2):
                    last = V.tensor_tensor(into[u % 2][:, 4 * hf:4 * hf + 4, :], single[hf][:, :].rearrange("p (k w) -> p k w", k=4),
                                           bc(g_ffn[:, 4 * hf:4 * hf + 4], P, 4, P), ALU.mult)
                last.then_inc(done, 1)

            x_evac(0, 1, xT, sem("xT"))
            for e in range(4):
                expert_dve(e, e, True)
                x_evac(e + 1, e + 2, xT, sem("xT"))
            with dve.Fori(1, 3) as i:
                for u in range(4):
                    expert_dve(4 * i + u, u, False)
                    x_evac(u + 1, 4 * i + u + 2, xT, sem("xT"))
            for e in range(12, 16):
                expert_dve(e, e % 4, False)
                if e < 15:
                    x_evac(e + 1, e + 2, xT, sem("xT"))
            dve.wait_ge(sem("ov_ready"), 1)
            n_ov = dve.value_load(ovi[0:1, NOV:NOV + 1], min_val=0, max_val=NOV)
            dve.wait_ge(sem("dn_mm"), 16)
            with dve.If(n_ov > 0):
                with dve.Fori(0, n_ov) as i:
                    dve.wait_ge(sem("ov_mm"), i + 1)
                    for hf in range(2):
                        last = V.tensor_tensor(xT[0][:, 4 * hf:4 * hf + 4, :], single[hf][:, :].rearrange("p (k w) -> p k w", k=4),
                                               bc(g_ffn[:, 4 * hf:4 * hf + 4], P, 4, P), ALU.mult)
                    last.then_inc(sem("ov_xT"), 1)
                    dve.wait_ge(sem("ov_gu"), i + 1)
                    dve.wait_ge(sem("ov_silu"), i + 1)
                    V.tensor_tensor(hid[0], sgt[0], single[3][:, DE:2 * DE], ALU.mult).then_inc(sem("ov_hid"), 1)
            def combine(t):
                n = ntok(t)
                for j in range(2):
                    dve.wait_ge(sem(f"ga{j}{t % 2}"), 16 * (t // 2 + 1))
                    ins = V.scalar_tensor_tensor(out=h2[0:n, t, :], in0=ga[t % 2][j][0:n, :], scalar=wcomb[0:n, j, t:t + 1],
                                                 in1=h2[0:n, t, :], op0=ALU.mult, op1=ALU.add)
                    if j == 0:
                        link(ins)
                ins.then_inc(sem("h3"), 1)

            def u3_norm(t):
                n = ntok(t)
                dve.wait_ge(sem("ms_root"), 1 + t + 1)
                link(V.reciprocal(ms[0:n, 2, t:t + 1], ms[0:n, 1, t:t + 1]))
                if t >= 2:
                    dve.wait_ge(sem("u3_mm"), t - 1)
                dve.wait_ge(sem("h3"), t + 1)
                V.tensor_scalar(u3n[t % 2][0:n, :], h2[0:n, t, :], ms[0:n, 2, t:t + 1], None, ALU.mult).then_inc(sem("u3n"), 1)
                dve.wait_ge(sem("u3_mm"), t + 1)
                for hf in range(2):
                    V.tensor_tensor(u3T[:, 4 * hf:4 * hf + 4, t * P:t * P + n], single[2 * (t % 2) + hf][:, 0:4 * n].rearrange("p (k w) -> p k w", k=4),
                                    bc(g_ple[:, 4 * hf:4 * hf + 4], P, 4, n), ALU.mult).then_inc(sem("u3T"), 1)

            def finish(t):
                n = ntok(t)
                dve.wait_ge(sem("sgp"), t + 1)
                link(V.tensor_tensor(sgp[t % 2][0:n, :], sgp[t % 2][0:n, :], pp[0:n, t, :], ALU.mult))
                V.tensor_tensor(h2[0:n, t, :], h2[0:n, t, :], sgp[t % 2][0:n, :], ALU.add).then_inc(sem("h4"), 1)
                if t == 0:
                    dve.wait_ge(sem("w_pg"), 48)
                dve.wait_ge(sem("ms_root"), 1 + NT + t + 1)
                link(V.reciprocal(ms[0:n, 2, t:t + 1], ms[0:n, 1, t:t + 1]))
                if t >= 2:
                    dve.wait_ge(sem(f"out{t % 2}"), 16 * (t // 2))
                V.scalar_tensor_tensor(out=yout[t % 2][0:n, :], in0=h2[0:n, t, :], scalar=ms[0:n, 2, t:t + 1], in1=nfin[0:n, :],
                                       op0=ALU.mult, op1=ALU.mult).then_inc(sem("y_out"), 1)

            for t in range(2):
                combine(t)
                u3_norm(t)
            for t in range(2, NT):
                combine(t)
            for t in range(2, NT):
                u3_norm(t)
                finish(t - 2)
            finish(3)
            finish(4)

        @block.gpsimd
        def _(pool):
            G = nc.gpsimd
            pool.wait_ge(sem("ld_const"), 16)
            for s in STEPS:
                k0 = s[0]
                if k0 == "tmq":
                    t, n = s[1], ntok(s[1])
                    ev_wait(pool, s)
                    if t >= 2:
                        mm_wait(pool, ("rTk", t - 2))
                        pool.wait_ge(sem("rkdec"), t - 1)
                    x4 = qk[t % 2][0:n, :].rearrange("p (h a w) -> p h a w", h=2 * H, a=2)
                    r4 = rot[t % 2][0:n, :].rearrange("p (h a w) -> p h a w", h=2 * H, a=2)
                    m4 = rtmp[0:n, :].rearrange("p (h a w) -> p h a w", h=2 * H, a=2)
                    cos = C("cos", n).rearrange("p (t w) -> p t w", t=NT)[:, t, :]
                    sin = C("sin", n).rearrange("p (t a w) -> p t a w", t=NT, a=2)
                    cosb = cos.unsqueeze(1).broadcast_to([n, 2 * H, RDK // 2])
                    if t:
                        pool.wait_ge(sem("rot"), t)
                    for a_ in range(2):
                        G.tensor_tensor(r4[:, :, a_, :], x4[:, :, a_, :], cosb, ALU.mult).then_inc(sem("rot_part"), 1)
                        G.tensor_tensor(m4[:, :, a_, :], x4[:, :, 1 - a_, :],
                                        sin[:, t, a_, :].unsqueeze(1).broadcast_to([n, 2 * H, RDK // 2]), ALU.mult)\
                            .then_inc(sem("rot_part"), 1)
                    pool.wait_ge(sem("rot_part"), 4 * (t + 1))
                    G.tensor_tensor(rot[t % 2][0:n, :], rot[t % 2][0:n, :], rtmp[0:n, :], ALU.add).then_inc(sem("rot"), 1)
                    pool.wait_ge(sem("rot"), t + 1)
                    if t >= 2:
                        mm_wait(pool, ("rU", t - 2))
                    G.tensor_tensor(kdec_r[t % 2][0:n], rot[t % 2][0:n, H * RDK:].rearrange("p (h w) -> p h w", h=H),
                                    bc(C("rk", n) if t < 4 else C("rk_s", n), n, H, RDK), ALU.mult).then_inc(sem("rkdec"), 1)
                elif k0 == "nq":
                    _, kind, m = s
                    q = plan.norm[(kind, m)]
                    src = {"rN": o_ret, "qn": cs, "oN": o_dn}[kind][:, m, :]
                    if kind == "rN": ev_wait(pool, ("rO", 4))
                    if kind == "oN": ev_wait(pool, ("sO", 3))
                    if kind == "qn": pool.wait_ge(sem("conv"), m + 1)
                    if q >= 2:
                        mm_wait(pool, plan.norm_step[q - 2])
                    G.tensor_tensor(sq[q % 2], src, src, ALU.mult).then_inc(sem("nsq"), 1)
                elif k0 == "rU" and s[1] == 3:
                    ev_wait(pool, s)
                    pool.dma_start(o["ret_prompt"], S_ret[0:RDK]).then_inc(sem("ret_stored"), 16)
                elif k0 == "rUs":
                    h = s[1]
                    ev_wait(pool, ("tmv", 4))
                    if h:
                        mm_wait(pool, ("rUs", h - 1))
                    G.tensor_tensor(vexp[0:64], vt[0][0:64, h * DV:(h + 1) * DV].unsqueeze(1).broadcast_to([64, NB, DV]),
                                    bc(C("row", 64), 64, NB, DV), ALU.mult).then_inc(sem("vexp"), 1)
                    if h == 3:
                        ev_wait(pool, s)
                        pool.dma_start(o["ret_sample"], sr[0:RDK]).then_inc(sem("ret_stored"), 16)
                        pool.wait_ge(sem("ret_stored"), 32)
                        G.memset(idx1[:, :], 0).then_inc(sem("ret_free"), 1)
                elif k0 == "cv" and s[1] == 1:
                    for i in range(NOV):
                        pool.dma_start(y_slots[(NEXP + i) * P:(NEXP + i + 1) * P, :], a["zeros"]).then_inc(sem("y_zero"), 16)
                elif k0 == "cv" and s[1] == NCONV - 1:
                    pool.wait_ge(sem("cnew"), NCONV)
                    pool.dma_start(o["conv"], cnew).then_inc(sem("cv_stored"), 16)
                elif k0 == "gE":
                    for t in range(NT):
                        n = ntok(t)
                        pool.wait_ge(sem("gexp"), 5 * t + 1)
                        G.tensor_tensor(A[t], A[t], bh(C("low") if t < 4 else C("low_s", 64), n, n), ALU.mult).then_inc(sem("gmask"), 1)
                        pool.wait_ge(sem("gexp"), 5 * t + 2)
                        G.tensor_tensor(D2[t], D2[t], bh(tri(t), n, n), ALU.mult).then_inc(sem("gmask"), 1)
                elif k0 == "l1":
                    t, n = s[1], ntok(s[1])
                    ev_wait(pool, ("gK", t))
                    pool.wait_ge(sem("gx"), 1)
                    G.tensor_tensor(X[t], A[t], bh(C("lev1t", n)[:, 0:n], n, n), ALU.mult).then_inc(sem("l1m"), 1)
                    pool.wait_ge(sem("l1m"), t + 1)
                    G.tensor_tensor(X[t], bh(C("ident", n)[:, 0:n], n, n), X[t], ALU.subtract).then_inc(sem("l1X"), 1)
                elif k0 == "lA":
                    _, v, t = s
                    n = ntok(t)
                    q = plan.order[s]
                    if v == 2:
                        ev_wait(pool, ("gA", t))
                    if q > 2:
                        prev = [x for x in STEPS if x[0] == "lA"][q - 3]
                        mm_wait(pool, ("lY",) + prev[1:])
                    G.tensor_tensor(hb(MSK[q % 2], t), AT[t], bh(C(f"lev{v}", n)[:, 0:n], n, n), ALU.mult).then_inc(sem("lA"), 1)
                elif k0 == "gq":
                    t, n = s[1], ntok(s[1])
                    pool.wait_ge(sem("gx"), 1)
                    G.tensor_tensor(E[t], E[t], cs[:, 0:H, t * P:t * P + n], ALU.mult).then_inc(sem("qe"), 1)
                elif k0 == "sU" and s[1] == 3:
                    ev_wait(pool, s)
                    pool.dma_start(o["dn_prompt"], S_dn).then_inc(sem("dp_stored"), 16)
                elif k0 == "sUs":
                    h = s[1]
                    ev_wait(pool, ("sT",))
                    if h:
                        mm_wait(pool, ("sUs", h - 1))
                    else:
                        mm_wait(pool, ("sO", 1))
                    G.tensor_tensor(dexp, dlt[4][:, h, :].unsqueeze(1).broadcast_to([64, NB, DV]),
                                    bc(C("row", 64), 64, NB, DV), ALU.mult).then_inc(sem("dexp"), 1)
                    mm_wait(pool, ("sO", 4))
                    G.tensor_tensor(sdn[:, :, h, :], sdn[:, :, h, :], bc(glast_s[:, h, :], P, NB, DV), ALU.mult).then_inc(sem("sdec"), 1)
                    if h == 3:
                        ev_wait(pool, s)
                        pool.dma_start(o["dn_sample"], sdn).then_inc(sem("sd_stored"), 16)
                        pool.wait_ge(sem("dp_stored"), 16)
                elif k0 == "up" and s[1] == 0:
                    pool.wait_ge(sem("o_dn"), H)
                    pool.dma_start(h2[:, 0:4, :], a["x_main"]).then_inc(sem("ld_h"), 16)
                    pool.dma_start(pT, a["pT"]).then_inc(sem("ld_p"), 16)
                elif k0 == "up" and s[1] == 15:
                    mm_wait(pool, s)
                    pool.wait_ge(sem("ld_h"), 16)
                    pool.dma_start(h2[0:64, 4, :], a["x_tail"]).then_inc(sem("ld_h"), 16)
                    pool.dma_start(iota, a["iota"]).then_inc(sem("ld_iota"), 16)
                elif k0 == "u2":
                    t, n = s[1], ntok(s[1])
                    pool.wait_ge(sem("u2n"), t + 1)
                    pool.dma_start(u_rows[t * P:t * P + n, :], u2n[t % 3][0:n, :]).then_inc(sem(f"u_rows{t % 3}"), 16)
                elif k0 == "ids":
                    ev_wait(pool, s)
                    for b, count in enumerate((32, 32, 16)):
                        pool.wait_ge(sem(f"u_rows{b}"), count)
                    mm_wait(pool, ("x2", 4, 1))

            def gather(e, col):
                pool.indirect_dma_start(xg[e % 2], None, u_rows, bass.IndirectOffsetOnAxis(ap=col, axis=0)).then_inc(sem(f"xg{e % 2}"), 16)

            for e in range(NEXP):
                if e >= 2:
                    pool.wait_ge(sem("xT_mm"), e - 1)
                gather(e, ids[:, e:e + 1])
            pool.wait_ge(sem("ov_ready"), 1)
            n_ov = pool.value_load(ovi[0:1, NOV:NOV + 1], min_val=0, max_val=NOV)
            pool.wait_ge(sem("xT_mm"), 16)
            with pool.If(n_ov > 0):
                with pool.Fori(0, n_ov) as i:
                    pool.wait_ge(sem("ov_free"), i + 1)
                    pool.sem_inc(sem("ov_pool"), 1)
                    G.tensor_copy(idx1[:, :], ids[:, bass.ds(i + NEXP, 1)]).then_inc(sem("ov_idx"), 1)
                    pool.wait_ge(sem("ov_idx"), i + 1)
                    pool.sem_inc(sem("ov_pool"), 1)
                    pool.indirect_dma_start(xg[0], None, u_rows, bass.IndirectOffsetOnAxis(ap=idx1[:, :], axis=0)).then_inc(sem("ov_xg"), 16)
            pool.wait_ge(sem("y_all"), 1)
            pool.wait_ge(sem("y_zero"), 16 * NOV)
            for t in range(NT):
                n = ntok(t)
                if t >= 2:
                    pool.wait_ge(sem("h3"), t - 1)
                for j in range(2):
                    pool.indirect_dma_start(ga[t % 2][j][0:n, :], None, y_slots,
                                            bass.IndirectOffsetOnAxis(ap=posu[0:n, j, t:t + 1], axis=0)).then_inc(sem(f"ga{j}{t % 2}"), 16)
            pool.wait_ge(sem("cv_stored"), 16)


def tiles(w, cols):
    k, n = w.shape
    return [np.ascontiguousarray(w[:, c:c + cols].reshape(k // P, P, cols).transpose(1, 0, 2)).reshape(P, -1)
            for c in range(0, n, cols)]


def kernel(x_prompt, x_sample, p_prompt, p_sample, state_ret, state_dn, state_conv, norm_mix, w_in, conv_w, dn_a_log,
           dn_dt_bias, dn_norm, w_ret_up, w_dn_up, w_out, norm_ffn, w_router_group, b_router_group, w_router_expert,
           b_router_expert, w_gate_up, w_down, norm_ple, w_ple_gate, w_ple_proj, norm_final):
    import concourse.bacc as bacc
    from concourse.bass_utils import run_bass_kernel_spmd as run

    A_ = np.asarray
    ch = lambda v: A_(v).reshape(-1, P).T
    rep = lambda v: np.broadcast_to(A_(v)[None, :], (P, A_(v).shape[0]))
    x = np.concatenate([A_(x_prompt).reshape(LP, D), A_(x_sample).reshape(NB * LS, D)])
    pe_ = np.concatenate([A_(p_prompt).reshape(LP, 2 * P), A_(p_sample).reshape(NB * LS, 2 * P)])
    a = {"const": np.concatenate(list(constant_tables().values()), 1)}
    a["xT"] = x.T.reshape(KD, P, TOK).transpose(1, 0, 2)
    a["x_main"] = x[:LP].reshape(4, P, D).transpose(1, 0, 2)
    a["x_tail"] = x[LP:]
    a["pT"] = pe_.T.reshape(2, P, TOK).transpose(1, 0, 2)
    a["vec"] = np.concatenate([ch(norm_mix[0]), ch(norm_ffn[0]), ch(norm_ple[0]),
                               A_(conv_w[0]).reshape(CW, NCONV, P).transpose(2, 1, 0).reshape(P, -1),
                               rep(dn_a_log[0]), rep(dn_dt_bias[0]), A_(dn_norm[0])[:, None],
                               rep(b_router_group[0]), rep(b_router_expert[0])], 1)
    w = A_(w_in[0])
    qk, v, rg, dqkv, dz, ab, gates = (w[:, lo:hi] for lo, hi in ((0, 512), (512, 1024), (1024, 1536), (1536, 3072),
                                                                (3072, 3584), (3584, 3592), (3592, 5640)))
    for name, part in (("qk", qk), ("v", v), ("rg", rg), ("dq", dqkv[:, 0:512]), ("dk", dqkv[:, 512:1024]),
                       ("dv", dqkv[:, 1024:]), ("dz", dz), ("ga0", gates[:, 0:512]), ("ga1", gates[:, 512:1024]),
                       ("gb0", gates[:, 1024:1536]), ("gb1", gates[:, 1536:])):
        a["w_" + name] = tiles(part, 512)[0]
    a["w_upr"] = tiles(A_(w_ret_up[0]), D)[0]
    a["w_upd"] = tiles(A_(w_dn_up[0]), D)[0]
    a["w_wo0"], a["w_wo1"] = tiles(A_(w_out[0]), 512)
    a["w_proj"] = tiles(A_(w_ple_proj[0]), D)[0]
    a["w_pg0"], a["w_pg1"] = tiles(A_(w_ple_gate[0]), 512)
    a["w_ab"] = ab.reshape(KD, P, 8).transpose(1, 0, 2)
    a["w_rt"] = np.concatenate([A_(w_router_group[0]), A_(w_router_expert[0])], 1).reshape(KD, P, 20).transpose(1, 0, 2)
    a["w_gu"] = A_(w_gate_up[0]).reshape(NEXP, KD, P, 2 * DE).transpose(0, 2, 1, 3).reshape(NEXP * P, CHUNK_W)
    a["w_down"] = A_(w_down[0]).reshape(NEXP, 2, P, D).transpose(0, 2, 1, 3).reshape(NEXP * P, 2 * D)
    a["state_ret"] = A_(state_ret[0]).transpose(2, 0, 1, 3)
    a["state_dn"] = A_(state_dn[0]).transpose(2, 0, 1, 3)
    a["state_conv"] = A_(state_conv[0]).reshape(NB, CW - 1, NCONV, P).transpose(3, 2, 0, 1)
    a["norm_final"] = rep(norm_final)
    a["iota"] = np.broadcast_to(np.arange(P, dtype=np.float32), (P, P))
    a["zeros"] = np.zeros((P, D), np.float32)
    a = {k: np.ascontiguousarray(v_) for k, v_ in a.items()}

    nc = bacc.Bacc("TRN2", target_bir_lowering=False, num_devices=1)
    ins = {k: nc.dram_tensor("in_" + k, v_.shape, mybir.dt.from_np(v_.dtype), kind="ExternalInput").ap() for k, v_ in a.items()}
    shapes = {"y": (TOK, D), "ret_prompt": (RDK, H, DV), "ret_sample": (RDK, NB, H, DV), "dn_prompt": (DK, H, DV),
              "dn_sample": (DK, NB, H, DV), "conv": (P, NCONV, 27)}
    outs = {k: nc.dram_tensor("out_" + k, sh, F32, kind="ExternalOutput").ap() for k, sh in shapes.items()}
    build(nc, ins, outs)
    r = run(nc, [{"in_" + k: v_ for k, v_ in a.items()}], core_ids=[0]).results[0]
    y = r["out_y"]
    conv = r["out_conv"].reshape(P, NCONV, 1 + NB, CW - 1).transpose(2, 3, 1, 0).reshape(1 + NB, CW - 1, NCONV * P)
    return (y[:LP].reshape(1, LP, D), y[LP:].reshape(NB, LS, D),
            r["out_ret_prompt"].transpose(1, 0, 2)[None, None], r["out_dn_prompt"].transpose(1, 0, 2)[None, None],
            conv[None, :1], r["out_ret_sample"].transpose(1, 2, 0, 3)[None], r["out_dn_sample"].transpose(1, 2, 0, 3)[None],
            conv[None, 1:])
```
